# Optimizing a Trainium2 kernel written in Bass

```python
import jax, jax.numpy as jnp
from jax import lax
import numpy as np

D_MODEL = 1024
BATCH = 1
SEQ = 128
DEPTH = 2
DEC_BATCH = 1
DEC_SEQ = 128
PAST_LEN = 128

GRID_W = 64
N_BRANCH = 4
BR_W = D_MODEL // N_BRANCH
MLA_HEADS = 4
MLA_NOPE = 64
MLA_ROPE = 32
MLA_QK = MLA_NOPE + MLA_ROPE
MLA_V = BR_W // MLA_HEADS
MLA_Q_LORA = 256
MLA_KV_LORA = 128
SC_W = BR_W
SC_K = 3
NA_HEADS = 4
NA_HD = BR_W // NA_HEADS
NA_W = NA_HEADS * NA_HD
NA_WIN_R = 8
NA_WIN_C = 16
CF_W = BR_W
CF_K = 31
D_FF = 3584
N_EXPERTS = 8
TOP_K = 2
D_FF_E = 3584
N_DENSE = (DEPTH + 1) // 2
N_MOE = DEPTH // 2
ROPE_THETA = 10000.0
EPS = 1e-6
Q_BLOCK = 128
DENSE_SWEEP_KEYS = 2048
_S1 = MLA_Q_LORA
_S2 = _S1 + MLA_KV_LORA + MLA_ROPE
_S3 = _S2 + 3 * SC_W
_S4 = _S3 + 3 * NA_W
_S5 = _S4 + 2 * CF_W
IN_COLS = _S5 + N_BRANCH * D_MODEL
IN_SPLITS = (_S1, _S2, _S3, _S4, _S5)

kernel_name = 'hybrid_diffusion_mla_natten_conv_step'

def rmsnorm(x, g):
    xf = x.astype(jnp.float32)
    y = xf * lax.rsqrt(jnp.mean(xf * xf, axis=-1, keepdims=True) + EPS)
    return (y * g.astype(jnp.float32)).astype(x.dtype)

def layernorm(x, g, b):
    xf = x.astype(jnp.float32)
    mu = jnp.mean(xf, axis=-1, keepdims=True)
    var = jnp.mean(jnp.square(xf - mu), axis=-1, keepdims=True)
    y = (xf - mu) * lax.rsqrt(var + EPS)
    return (y * g.astype(jnp.float32) + b.astype(jnp.float32)).astype(x.dtype)

def dwconv(x, w):
    K = w.shape[0]
    return lax.conv_general_dilated(x, w[:, None, :].astype(x.dtype), window_strides=(1,),
                                    padding=[(K // 2, K // 2)], dimension_numbers=('NWC', 'WIO', 'NWC'),
                                    feature_group_count=x.shape[-1])

def axial_rope(x):
    S = x.shape[1]
    half = MLA_ROPE // 2
    nf = half // 2
    t = jnp.arange(S)
    inv = ROPE_THETA ** (-jnp.arange(nf, dtype=jnp.float32) / nf)

    def rot(xa, pos):
        ang = pos.astype(jnp.float32)[:, None] * inv[None, :]
        cos = jnp.cos(ang)[None, :, None, :].astype(x.dtype)
        sin = jnp.sin(ang)[None, :, None, :].astype(x.dtype)
        x1, x2 = xa[..., :nf], xa[..., nf:]
        return jnp.concatenate([x1 * cos - x2 * sin, x1 * sin + x2 * cos], axis=-1)

    return jnp.concatenate([rot(x[..., :half], t // GRID_W), rot(x[..., half:], t % GRID_W)], axis=-1)

def rope_tail(x):
    return jnp.concatenate([x[..., :MLA_NOPE], axial_rope(x[..., MLA_NOPE:])], axis=-1)

def _attn(q, k, v, scale):
    s = jnp.einsum('bqhd,bkhd->bhqk', q, k, preferred_element_type=jnp.float32) * scale
    p = jax.nn.softmax(s, axis=-1).astype(v.dtype)
    return jnp.einsum('bhqk,bkhd->bqhd', p, v)

def dense_attention(q, k, v, scale):
    Bn, Sq, H, dq = q.shape
    if k.shape[1] < DENSE_SWEEP_KEYS or Sq % Q_BLOCK:
        return _attn(q, k, v, scale)
    qb = jnp.moveaxis(q.reshape(Bn, Sq // Q_BLOCK, Q_BLOCK, H, dq), 1, 0)
    ob = lax.map(lambda qi: _attn(qi, k, v, scale), qb)
    return jnp.moveaxis(ob, 0, 1).reshape(Bn, Sq, H, v.shape[-1])

def mla_keys_values(ckv, kpe, w_ukv, g_k):
    Bn, L, _ = ckv.shape
    kv = (ckv @ w_ukv).reshape(Bn, L, MLA_HEADS, MLA_NOPE + MLA_V)
    k_pe = jnp.broadcast_to(kpe[:, :, None, :], (Bn, L, MLA_HEADS, MLA_ROPE))
    k = rmsnorm(jnp.concatenate([kv[..., :MLA_NOPE], k_pe], axis=-1), g_k)
    return k, kv[..., MLA_NOPE:]

def neighbourhood_attention(q, k, v, k_ctx, v_ctx, rpb):
    Bn, S, H, dh = q.shape
    R = S // GRID_W
    wr = min(NA_WIN_R, R)
    scale = dh ** -0.5
    qg = q.reshape(Bn, R, GRID_W, H, dh)
    kg = k.reshape(Bn, R, GRID_W, H, dh)
    vg = v.reshape(Bn, R, GRID_W, H, dh)
    rows = jnp.arange(R)
    row_idx = jnp.clip(rows - wr // 2, 0, R - wr)[:, None] + jnp.arange(wr)[None, :]
    k_rows = kg[:, row_idx]
    v_rows = vg[:, row_idx]
    cols = jnp.arange(GRID_W)
    col_start = jnp.clip(cols - NA_WIN_C // 2, 0, GRID_W - NA_WIN_C)
    col_ok = (cols[None, :] >= col_start[:, None]) & (cols[None, :] < col_start[:, None] + NA_WIN_C)
    dr = row_idx - rows[:, None]
    dc = jnp.clip(cols[None, :] - cols[:, None], -(NA_WIN_C - 1), NA_WIN_C - 1)
    bias = rpb[:, dr[:, None, :, None] + (NA_WIN_R - 1), dc[None, :, None, :] + (NA_WIN_C - 1)]
    s_loc = jnp.einsum('brchd,brikhd->bhrcik', qg, k_rows, preferred_element_type=jnp.float32) * scale
    s_loc = jnp.where(col_ok[:, None, :], s_loc + bias[None].astype(jnp.float32), -jnp.inf)
    s_ctx = jnp.einsum('brchd,blhd->bhrcl', qg, k_ctx, preferred_element_type=jnp.float32) * scale
    n_loc = wr * GRID_W
    s = jnp.concatenate([s_loc.reshape(Bn, H, R, GRID_W, n_loc), s_ctx], axis=-1)
    p = jax.nn.softmax(s, axis=-1).astype(v.dtype)
    p_loc = p[..., :n_loc].reshape(Bn, H, R, GRID_W, wr, GRID_W)
    o = (jnp.einsum('bhrcik,brikhd->brchd', p_loc, v_rows)
         + jnp.einsum('bhrcl,blhd->brchd', p[..., n_loc:], v_ctx))
    return o.reshape(Bn, S, H * dh)

def swiglu(h, w_g, w_u, w_d):
    return (jax.nn.silu(h @ w_g) * (h @ w_u)) @ w_d

def moe_swiglu(h, w_router, w_g, w_u, w_d):
    shp = h.shape
    t = h.reshape(-1, D_MODEL)
    logits = (t @ w_router).astype(jnp.float32)
    top_v, top_i = lax.top_k(logits, TOP_K)
    top_w = jax.nn.softmax(top_v, axis=-1)
    gate = jnp.sum(jax.nn.one_hot(top_i, N_EXPERTS, dtype=jnp.float32) * top_w[..., None], axis=1).astype(h.dtype)
    out = jnp.zeros_like(t)
    for e in range(N_EXPERTS):
        out = out + gate[:, e:e + 1] * swiglu(t, w_g[e], w_u[e], w_d[e])
    return out.reshape(shp)

def trunk_layer(x, cvec, l, P, ctx):
    latent = ctx is not None
    Bn, S, _ = x.shape
    mod = (jax.nn.silu(cvec) @ P['w_ada'][l] + P['b_ada'][l]).reshape(cvec.shape[0], 1, 6, D_MODEL)
    shift1, scale1, gate1, shift2, scale2, gate2 = (mod[:, :, i] for i in range(6))
    h = rmsnorm(x, P['g_norm1'][l]) * (1 + scale1) + shift1
    p_qa, p_kva, p_sc, p_na, p_cf, p_gate = jnp.split(h @ P['w_in'][l], IN_SPLITS, axis=-1)

    q = rmsnorm(p_qa, P['g_qa'][l]) @ P['w_uq'][l]
    q = rmsnorm(q.reshape(Bn, S, MLA_HEADS, MLA_QK), P['g_mla_q'][l])
    ckv = rmsnorm(p_kva[..., :MLA_KV_LORA], P['g_kva'][l])
    kpe = p_kva[..., MLA_KV_LORA:]
    k, v = mla_keys_values(ckv, kpe, P['w_ukv'][l], P['g_mla_k'][l])
    if latent:
        q = rope_tail(q)
        k = rope_tail(k)
        k_c, v_c = mla_keys_values(ctx[0], ctx[1], P['w_ukv'][l], P['g_mla_k'][l])
        k = jnp.concatenate([k_c, k], axis=1)
        v = jnp.concatenate([v_c, v], axis=1)
    o_a = dense_attention(q, k, v, MLA_QK ** -0.5).reshape(Bn, S, MLA_HEADS * MLA_V)

    b_g, c_g, xv = jnp.split(p_sc, 3, axis=-1)
    o_b = b_g * dwconv(c_g * xv, P['sc_w'][l])

    q_na, k_na, v_na = (z.reshape(Bn, S, NA_HEADS, NA_HD) for z in jnp.split(p_na, 3, axis=-1))
    q_na = rmsnorm(q_na, P['g_na_q'][l])
    k_na = rmsnorm(k_na, P['g_na_k'][l])
    if latent:
        o_c = neighbourhood_attention(q_na, k_na, v_na, ctx[2], ctx[3], P['na_rpb'][l])
    else:
        o_c = dense_attention(q_na, k_na, v_na, NA_HD ** -0.5).reshape(Bn, S, NA_W)

    a_cf, b_cf = jnp.split(p_cf, 2, axis=-1)
    u = dwconv(a_cf * jax.nn.sigmoid(b_cf), P['cf_w'][l]) + P['cf_b'][l]
    o_d = jax.nn.silu(layernorm(u, P['cf_ln_g'][l], P['cf_ln_b'][l]))

    branches = jnp.stack([o_a, o_b, o_c, o_d], axis=2)
    proj = jnp.einsum('bsnc,ncd->bsnd', branches, P['w_br'][l])
    gates = jax.nn.sigmoid(p_gate.reshape(Bn, S, N_BRANCH, D_MODEL))
    x = x + gate1 * (jnp.sum(gates * proj, axis=2) @ P['w_o'][l])

    h2 = rmsnorm(x, P['g_norm2'][l]) * (1 + scale2) + shift2
    if l % 2 == 0:
        j = l // 2
        f = swiglu(h2, P['w_ff_gate'][j], P['w_ff_up'][j], P['w_ff_down'][j])
    else:
        j = l // 2
        f = moe_swiglu(h2, P['w_router'][j], P['w_e_gate'][j], P['w_e_up'][j], P['w_e_down'][j])
    x = x + gate2 * f
    if latent:
        return x, None
    return x, (ckv, kpe, k_na, v_na)

def setup_inputs(seed: int = 0) -> dict:
    key = jax.random.key(seed)
    ks = iter(jax.random.split(key, 48))

    def nrm(shape, scale=1.0):
        return jax.random.normal(next(ks), shape, jnp.float32) * scale

    def gain(shape):
        return 1.0 + nrm(shape, 0.02)

    D = D_MODEL
    return {
        'x_prompt': nrm((BATCH, SEQ, D)),
        'x_sample': nrm((DEC_BATCH, DEC_SEQ, D)),
        'cache_mla_ckv': nrm((DEC_BATCH, DEPTH, PAST_LEN, MLA_KV_LORA)),
        'cache_mla_kpe': nrm((DEC_BATCH, DEPTH, PAST_LEN, MLA_ROPE)),
        'cache_na_k': nrm((DEC_BATCH, DEPTH, PAST_LEN, NA_HEADS, NA_HD)),
        'cache_na_v': nrm((DEC_BATCH, DEPTH, PAST_LEN, NA_HEADS, NA_HD)),
        'c': nrm((DEC_BATCH, D)),
        'c_ctx': nrm((D,)),
        'w_ada': nrm((DEPTH, D, 6 * D), D ** -0.5),
        'b_ada': nrm((DEPTH, 6 * D), 0.01),
        'g_norm1': gain((DEPTH, D)),
        'w_in': nrm((DEPTH, D, IN_COLS), D ** -0.5),
        'g_qa': gain((DEPTH, MLA_Q_LORA)),
        'w_uq': nrm((DEPTH, MLA_Q_LORA, MLA_HEADS * MLA_QK), MLA_Q_LORA ** -0.5),
        'g_kva': gain((DEPTH, MLA_KV_LORA)),
        'w_ukv': nrm((DEPTH, MLA_KV_LORA, MLA_HEADS * (MLA_NOPE + MLA_V)), MLA_KV_LORA ** -0.5),
        'g_mla_q': gain((DEPTH, MLA_QK)),
        'g_mla_k': gain((DEPTH, MLA_QK)),
        'sc_w': nrm((DEPTH, SC_K, SC_W), SC_K ** -0.5),
        'g_na_q': gain((DEPTH, NA_HD)),
        'g_na_k': gain((DEPTH, NA_HD)),
        'na_rpb': nrm((DEPTH, NA_HEADS, 2 * NA_WIN_R - 1, 2 * NA_WIN_C - 1), 0.1),
        'cf_w': nrm((DEPTH, CF_K, CF_W), CF_K ** -0.5),
        'cf_b': nrm((DEPTH, CF_W), 0.01),
        'cf_ln_g': gain((DEPTH, CF_W)),
        'cf_ln_b': nrm((DEPTH, CF_W), 0.01),
        'w_br': nrm((DEPTH, N_BRANCH, BR_W, D), BR_W ** -0.5),
        'w_o': nrm((DEPTH, D, D), D ** -0.5),
        'g_norm2': gain((DEPTH, D)),
        'w_ff_gate': nrm((N_DENSE, D, D_FF), D ** -0.5),
        'w_ff_up': nrm((N_DENSE, D, D_FF), D ** -0.5),
        'w_ff_down': nrm((N_DENSE, D_FF, D), D_FF ** -0.5),
        'w_router': nrm((N_MOE, D, N_EXPERTS), D ** -0.5),
        'w_e_gate': nrm((N_MOE, N_EXPERTS, D, D_FF_E), D ** -0.5),
        'w_e_up': nrm((N_MOE, N_EXPERTS, D, D_FF_E), D ** -0.5),
        'w_e_down': nrm((N_MOE, N_EXPERTS, D_FF_E, D), D_FF_E ** -0.5),
    }

def reference(x_prompt, x_sample, cache_mla_ckv, cache_mla_kpe, cache_na_k, cache_na_v, c, c_ctx,
              w_ada, b_ada, g_norm1, w_in, g_qa, w_uq, g_kva, w_ukv, g_mla_q, g_mla_k, sc_w,
              g_na_q, g_na_k, na_rpb, cf_w, cf_b, cf_ln_g, cf_ln_b, w_br, w_o, g_norm2,
              w_ff_gate, w_ff_up, w_ff_down, w_router, w_e_gate, w_e_up, w_e_down):
    P = dict(w_ada=w_ada, b_ada=b_ada, g_norm1=g_norm1, w_in=w_in, g_qa=g_qa, w_uq=w_uq, g_kva=g_kva,
             w_ukv=w_ukv, g_mla_q=g_mla_q, g_mla_k=g_mla_k, sc_w=sc_w, g_na_q=g_na_q, g_na_k=g_na_k,
             na_rpb=na_rpb, cf_w=cf_w, cf_b=cf_b, cf_ln_g=cf_ln_g, cf_ln_b=cf_ln_b, w_br=w_br, w_o=w_o,
             g_norm2=g_norm2, w_ff_gate=w_ff_gate, w_ff_up=w_ff_up, w_ff_down=w_ff_down,
             w_router=w_router, w_e_gate=w_e_gate, w_e_up=w_e_up, w_e_down=w_e_down)

    y_prompt = x_prompt
    cvec_ctx = c_ctx[None, :]
    ckv_l, kpe_l, nak_l, nav_l = [], [], [], []
    for l in range(DEPTH):
        y_prompt, st = trunk_layer(y_prompt, cvec_ctx, l, P, None)
        ckv_l.append(st[0])
        kpe_l.append(st[1])
        nak_l.append(st[2])
        nav_l.append(st[3])
    new_mla_ckv = jnp.stack(ckv_l, axis=1)
    new_mla_kpe = jnp.stack(kpe_l, axis=1)
    new_na_k = jnp.stack(nak_l, axis=1)
    new_na_v = jnp.stack(nav_l, axis=1)

    y_sample = x_sample
    for l in range(DEPTH):
        y_sample, _ = trunk_layer(y_sample, c, l, P,
                                  (cache_mla_ckv[:, l], cache_mla_kpe[:, l], cache_na_k[:, l], cache_na_v[:, l]))

    return (y_prompt, y_sample, new_mla_ckv, new_mla_kpe, new_na_k, new_na_v)


_drawn_inputs = setup_inputs


def setup_inputs(seed=0):
    import zlib

    import numpy as np

    out = dict(_drawn_inputs(seed))
    spreads = {}
    factors = {'g_qa': 8.0,
     'g_kva': 2.867,
     'g_mla_q': 4.3,
     'g_mla_k': 8.0,
     'g_na_q': 8.0,
     'g_na_k': 2.995,
     'na_rpb': 4.227,
     'cf_b': 5.4,
     'cf_ln_g': 2.781,
     'cf_ln_b': 5.595}
    for name, (base, spread) in spreads.items():
        noise = np.random.default_rng([zlib.crc32(name.encode()), seed]).standard_normal(out[name].shape)
        drawn = base * np.exp(spread * noise) if base else spread * noise
        out[name] = __import__('jax').numpy.asarray(drawn.astype(out[name].dtype))
    for name, factor in factors.items():
        out[name] = (out[name] * factor).astype(out[name].dtype)
    return out
```

```python
import concourse.bass as bass
from concourse import mybir
from contextlib import ExitStack

F32 = mybir.dt.float32
F32R = mybir.dt.float32r
I32 = mybir.dt.int32
ALU = mybir.AluOpType
ACT = mybir.ActivationFunctionType
AX = mybir.AxisListType

P = 128
D = 1024
KT = D // P
TOK = 128
NT = 2 * TOK
DEPTH = 2
GRID_W = 64
HEADS = 4
QL, KVL, ROPE, NOPE = 256, 128, 32, 64
QK = NOPE + ROPE
HD = 64
BW = 256
CFK, SCK = 31, 3
DFF = 3584
CHUNKS = DFF // 512
NEXP = 8
CAP = 128
OVER = 512 // (CAP + 1)
ITEMS = NEXP + OVER
EPS = 1e-6
RAW = 3
HALF = 2048

C_QA, C_SC, C_NA, C_CF, C_GATE = 0, 416, 1184, 1952, 2464

V_N1, V_N2, V_QA, V_CFB, V_LNG, V_LNB, V_SC, V_CF = 0, 8, 16, 18, 20, 22, 24, 30
V_ROWS = V_CF + 2 * CFK

K_ID, K_UP, K_IOTA, K_MASK, K_FLIP = 0, 128, 256, 384, 512
K_COS, K_SIN, K_FOLD, K_BEFORE, K_EXP, K_LEFT = 640, 656, 672, 674, 738, 746
K_COLS = 754

M_TOK, M_SC, M_CF, M_GATE, M_BR, M_O, M_HALVES = 0, 5, 8, 10, 26, 30, 34


def ffn_order():
    order = []
    for c in range(CHUNKS):
        order += [("gate", c), ("up", c)]
        if c:
            order.append(("down", c - 1))
    order.append(("down", CHUNKS - 1))
    return order


FFN = ffn_order()
FFN_HALVES = 2 * len(FFN)


def plan_slots():
    slots = []
    for l in range(DEPTH):
        slots += [("ada", l, c, 2) for c in range(12)]
        slots += [("tok", l, 0, 2), ("na_qk", l, 0, 2), ("na_v", l, 0, 1),
                  ("sc", l, 0, 2), ("sc", l, 1, 1), ("cf", l, 0, 2)]
        slots += [("gates", l, c, 2) for c in range(8)]
        slots += [("branch", l, c, 2) for c in range(2)] + [("out", l, c, 2) for c in range(2)]
        if l == 0:
            slots += [(kind, 0, c, 2) for kind, c in FFN]
    return slots


SLOTS = plan_slots()
SLOT_OF = []
FIRST_HALF = []
for _s, _slot in enumerate(SLOTS):
    FIRST_HALF.append(len(SLOT_OF))
    SLOT_OF += [(_s, _h) for _h in range(_slot[3])]
HALVES = len(SLOT_OF)
PHASE = {(k, l): min(s for s, x in enumerate(SLOTS) if x[0] == k and x[1] == l) for k, l, _, _ in SLOTS}


def first_half(kind, layer):
    return FIRST_HALF[PHASE[(kind, layer)]]


def build(nc, x_prompt, x_sample, cache_mla_ckv, cache_mla_kpe, cache_na_k, cache_na_v, c, c_ctx,
          w_ada, b_ada, g_norm1, w_in, g_qa, w_uq, g_kva, w_ukv, g_mla_q, g_mla_k, sc_w,
          g_na_q, g_na_k, na_rpb, cf_w, cf_b, cf_ln_g, cf_ln_b, w_br, w_o, g_norm2,
          w_ff_gate, w_ff_up, w_ff_down, w_router, w_e_gate, w_e_up, w_e_down, shape_consts,
          y_prompt, y_sample, new_ckv, new_kpe, new_na_k, new_na_v):
    with ExitStack() as ctx:
        def sb(name, shape, dt=F32):
            return ctx.enter_context(nc.sbuf_tensor(name, shape, dt))

        def sem(name):
            return ctx.enter_context(nc.semaphore(name))

        raw = sb("raw", [P, RAW, 2 * HALF])
        whi = sb("whi", [P, 2, HALF], F32R)
        wlo = sb("wlo", [P, 2, HALF], F32R)
        hT_hi = sb("hT_hi", [P, KT, NT], F32R)
        hT_lo = sb("hT_lo", [P, KT, NT], F32R)
        br_hi = sb("br_hi", [P, 8, NT], F32R)
        br_lo = sb("br_lo", [P, 8, NT], F32R)
        xT = sb("xT", [P, KT, NT])
        big = sb("big", [P, 8192])
        tokA = sb("tokA", [P, 2, 416])
        tokN = sb("tokN", [P, 2, 768])
        qk = sb("qk", [P, 1920])
        KV = sb("KV", [P, 3, 512])
        QT = sb("QT", [P, 2, HEADS, TOK])
        KTt = sb("KTt", [P, 3, HEADS, TOK])
        bias = sb("bias", [P, HEADS, TOK])
        consts = sb("consts", [P, K_COLS])
        ones = sb("ones", [P, P])
        wuq = sb("wuq", [P, 2, 384])
        wukv = sb("wukv", [P, 512])
        vrow = sb("vrow", [P, P])
        vecT = sb("vecT", [P, DEPTH, V_ROWS])
        badaT = sb("badaT", [P, DEPTH, 48])
        modT = sb("modT", [P, 48, 2])
        scaleT = sb("scaleT", [P, 2, KT, 2])
        gkv_b = sb("gkv_b", [P, KVL])
        gq_b = sb("gq_b", [P, QK])
        gk_b = sb("gk_b", [P, QK])
        gnq_b = sb("gnq_b", [P, HD])
        gnk_b = sb("gnk_b", [P, HD])
        scpad = sb("scpad", [P, 2, 2, TOK + 2])
        cfpad = sb("cfpad", [P, 2, 2, TOK + 30])
        conv = sb("conv", [P, 2, NT])
        small = sb("small", [P, 192])
        cond_hl = sb("cond_hl", [P, KT, 4], F32R)
        itab = sb("itab", [1, 16], I32)
        minus_half = sb("minus_half", [P, 1])
        ps = ctx.enter_context(nc.psum_tensor("ps", [P, 8, 512], F32))

        ident = consts[:, K_ID:K_ID + P]

        sq = big[:, 0:2048].rearrange("p (k t) -> p k t", k=KT)
        hF = big[:, 2048:4096].rearrange("p (k t) -> p k t", k=KT)
        xtok = big[:, 0:2048].rearrange("p (g d) -> p g d", g=2)
        rstd = big[:, 4096:4352]
        gates = big[:, :].rearrange("p (n j t) -> p n j t", n=4, j=8)
        bc = big[:, 6144:7168].rearrange("p (b t) -> p b t", b=4)
        cf = big[:, 7168:8192].rearrange("p (b t) -> p b t", b=4)
        ff_act = big[:, 0:1024].rearrange("p (b n) -> p b n", b=2)
        ff_hid = big[:, 1024:2048].rearrange("p (b n) -> p b n", b=2)
        h2tok = big[:, 4096:6144].rearrange("p (g d) -> p g d", g=2)
        fT = big[:, 6144:8192].rearrange("p (k t) -> p k t", k=KT)
        y_tok = big[:, 2048:3072]
        sel = big[:, 3072:3328].rearrange("p (t s) -> p t s", t=2)
        selg = big[:, 3328:3584].rearrange("p (t s) -> p t s", t=2)
        selT = big[:, 3584:3840]
        arow = tokN[0:4, :, :].rearrange("p g n -> p (g n)")[:, 0:1024].rearrange("p (a n) -> p a n", a=2)
        Q = qk[:, 0:768].rearrange("p (g h d) -> p g h d", g=2, h=HEADS)
        Kn = qk[:, 768:1920].rearrange("p (s h d) -> p s h d", s=3, h=HEADS)
        heads_sq = qk[:, 768:1536]
        Pr = qk[:, 0:1536].rearrange("p (s h d) -> p s h d", s=3, h=HEADS)
        QTf = QT[:, :, :, :].rearrange("p g h t -> p (g h t)")
        KTf = KTt[:, :, :, :].rearrange("p s h t -> p (s h t)")
        qaT = QTf[:, 0:512].rearrange("p (a t) -> p a t", a=2)
        ckvT = KTf[:, 0:384]
        sbias = KV[:, 0, :]
        O = tokA[:, :, 0:256]
        ckc = qk[:, 1536:1664]
        kpc = small[:, 128:160]
        nakc = KV[:, 1, 0:256]
        navc = KV[:, 1, 256:512]
        ropet = big[:, 1024:1536].rearrange("p (a n) -> p a n", a=8)
        hank = KV[:, 2, :].rearrange("p (h k) -> p h k", h=HEADS)
        na_sq = big[:, 0:1024].rearrange("p (g d) -> p g d", g=2)
        ln_sq = QTf[:, 0:512]
        ln_sd = QTf[:, 512:768]
        wr = qk[:, 0:64].rearrange("p (k e) -> p k e", k=KT)
        lg = qk[:, 64:80].rearrange("p (g e) -> p g e", g=2)
        lg2 = qk[:, 80:96].rearrange("p (g e) -> p g e", g=2)
        oh1 = qk[:, 96:112].rearrange("p (g e) -> p g e", g=2)
        oh2 = qk[:, 112:128].rearrange("p (g e) -> p g e", g=2)
        tmp = qk[:, 128:144].rearrange("p (g e) -> p g e", g=2)
        tq = qk[:, 144:160]
        ov = qk[:, 168:176]
        rank = qk[:, 176:184]
        mask = qk[:, 1010:1026].rearrange("p (g e) -> p g e", g=2)
        ohk = qk[:, 184:184 + 8 * OVER].rearrange("p (k e) -> p k e", k=OVER)
        w64 = qk[:, 300:364].rearrange("p (a e) -> p a e", a=8)
        tab = qk[:, 400:400 + 6 * ITEMS].rearrange("p (q t i) -> p q t i", q=3, t=2)
        wide = qk[:, 600:600 + 16 * OVER].rearrange("p (t k e) -> p t k e", t=2, k=OVER)
        eidx = qk[:, 900:900 + OVER + 2]
        stage = qk[:, 1000:1006].rearrange("p (q t) -> p q t", q=3)

        raw_landed = [sem(f"raw_landed{i}") for i in range(RAW)]
        (hi_done, lo_done, half_used, consts_in, x_in, cond_in, vrow_in, small_in,          nacache_in, cache_in, router_in, setup, pool_pow, dve_link, cond_turned, cond_th, cond_ready, cond_hi,
         cond_lo, v_turned, v_kept, x_turned, x_kept, ada_kept, ada_folded, mod_done,
         sq_done, stat_done, ms_done, sd_done, hF_done, h_hi, h_lo, drained, xv_read, proj_fill,
         proj_read, merged_f, merged_hi, merged_lo, wo_read) = map(sem, (
             "hi_done lo_done half_used consts_in x_in cond_in vrow_in small_in "
             "nacache_in cache_in router_in setup pool_pow dve_link cond_turned cond_th cond_ready cond_hi "
             "cond_lo v_turned v_kept x_turned x_kept ada_kept ada_folded mod_done "
             "sq_done stat_done ms_done sd_done hF_done h_hi h_lo drained xv_read proj_fill "
             "proj_read merged_f merged_hi merged_lo wo_read").split())
        (stats_in, qa_normed, na_ready, hank_in, bias_turned, bias_kept, latent_turned, latent_kept,
         qkv_done, qkv_kept, qk_ready, heads_turned, heads_kept, scores_done, max_done, exp_done,
         probs_turned, probs_kept, o_done, o_scaled, o_turned, o_hi, o_lo, b_ready, b_hi, b_lo, cf_used,
         conv_v, conv_ready, ln_sum, ln_sq_done, ln_sqsum, ln_ms, ln_sdone, ln_z, ln_th, ln_o, d_hi, d_lo,
         stored) = map(sem, (
             "stats_in qa_normed na_ready hank_in bias_turned bias_kept latent_turned latent_kept "
             "qkv_done qkv_kept qk_ready heads_turned heads_kept scores_done max_done exp_done "
             "probs_turned probs_kept o_done o_scaled o_turned o_hi o_lo b_ready b_hi b_lo cf_used "
             "conv_v conv_ready ln_sum ln_sq_done ln_sqsum ln_ms ln_sdone ln_z ln_th ln_o d_hi d_lo "
             "stored").split())
        (ff_act_done, ff_hid_done, ff_hi, ff_lo, ff_read, lg_done, h2_turned, h2_kept,
         mask_done, pos_done, tab_done, staged, sel_done, selT_t, selT_kept, xe_t, xe_hi, xe_lo,          e_act, e_hid, e_turn, e_hi, e_lo, y_kept, sc_fill, moe_done, fin_t, fin_kept, pair_exp, item_added, y_stored) = map(sem, (
             "ff_act_done ff_hid_done ff_hi ff_lo ff_read lg_done h2_turned h2_kept "
             "mask_done pos_done tab_done staged sel_done selT_t selT_kept xe_t xe_hi xe_lo "
             "e_act e_hid e_turn e_hi e_lo y_kept sc_fill moe_done fin_t fin_kept pair_exp item_added y_stored").split())

        def cols(w, l, a, n):
            return w[l, :, a:a + n].rearrange("(k p) n -> p k n", p=P)

        def slot_parts(kind, l, i):
            if kind == "ada":
                return (8, 512), cols(w_ada, l, 512 * i, 512)
            if kind == "tok":
                return (8, 416), cols(w_in, l, C_QA, 416)
            if kind == "na_qk":
                return (8, 512), cols(w_in, l, C_NA, 512)
            if kind == "na_v":
                return (8, 256), cols(w_in, l, C_NA + 512, 256)
            if kind == "sc":
                return (8, 256 if i else 512), cols(w_in, l, C_SC + 512 * i, 256 if i else 512)
            if kind == "cf":
                return (8, 512), cols(w_in, l, C_CF, 512)
            if kind == "gates":
                return (8, 512), cols(w_in, l, C_GATE + 512 * i, 512)
            if kind == "branch":
                return (8, 512), w_br[l].rearrange("n (k p) d -> p (n k) d", p=P)[:, :, 512 * i:512 * i + 512]
            if kind == "out":
                return (8, 512), cols(w_o, l, 512 * i, 512)
            if kind == "gate":
                return (8, 512), cols(w_ff_gate, 0, 512 * i, 512)
            if kind == "up":
                return (8, 512), cols(w_ff_up, 0, 512 * i, 512)
            return (4, 1024), w_ff_down[0, 512 * i:512 * i + 512, :].rearrange("(k p) n -> p k n", p=P)

        BY_K = ("ada", "tok", "na_qk", "na_v")

        def half_shape(kind, i):
            if kind in ("ada", "na_qk"):
                return 4, 512
            if kind == "tok":
                return 4, 416
            if kind == "down":
                return 2, 1024
            return 8, 256

        def half_views(kind, i, h, raw_slot, buf, by_k=None):
            k, n = half_shape(kind, i)
            if kind in ("gate", "up") and by_k:
                k, n = 4, 512
            width = {"tok": 416, "na_v": 256, "down": 1024}.get(kind, 256 if kind == "sc" and i else 512)
            depth = 4 if kind == "down" else 8
            whole = raw[:, raw_slot, 0:depth * width].rearrange("p (k n) -> p k n", k=depth)
            part = whole[:, k * h:k * h + k, :] if n == width else whole[:, :, n * h:n * h + n]
            return (part,) + tuple(w[:, buf, 0:k * n].rearrange("p (k n) -> p k n", k=k) for w in (whi, wlo))

        def half(H):
            s, h = SLOT_OF[H]
            kind, _, i, _ = SLOTS[s]
            return half_views(kind, i, h, s % RAW, H % 2)

        def item_half(hh):
            kind, _ = FFN[hh // 2]
            return half_views(kind, 0, hh % 2, (len(SLOTS) + hh // 2) % RAW, (HALVES + hh) % 2, by_k=True)

        ada0 = {l: first_half("ada", l) for l in range(DEPTH)}
        mix0 = {l: first_half("tok", l) for l in range(DEPTH)}
        ff0 = first_half("gate", 0)

        def filled(l, f):
            return mix0[l] + (2 if f < 2 else 4 if f < 4 else f + 1)

        def ff_used(kind, ch):
            return ff0 + 2 * FFN.index((kind, ch)) + 2

        block = ctx.enter_context(nc.Block())

        @block.sync
        def _(sp):
            for s, (kind, l, i, n) in enumerate(SLOTS):
                (k, w), src = slot_parts(kind, l, i)
                if s >= RAW:
                    sp.wait_ge(lo_done, FIRST_HALF[s - RAW] + SLOTS[s - RAW][3])
                dst = raw[:, s % RAW, 0:k * w].rearrange("p (k n) -> p k n", k=k)
                sp.dma_start(dst, src).then_inc(raw_landed[s % RAW], 16)

            def item_loads(e, done):
                for j, (kind, ch) in enumerate(FFN):
                    if kind == "down":
                        src = w_e_down[0, bass.ds(e, 1), 512 * ch:512 * ch + 512, :].rearrange(
                            "a (k p) n -> p (a k) n", p=P)
                        k = 4
                    else:
                        w = w_e_gate if kind == "gate" else w_e_up
                        src = w[0, bass.ds(e, 1), :, 512 * ch:512 * ch + 512].rearrange(
                            "a (k p) n -> p (a k) n", p=P)
                        k = 8
                    slot = (len(SLOTS) + j) % RAW
                    sp.wait_ge(lo_done, done + (HALVES + 2 * (j - RAW + 1)))
                    sp.dma_start(raw[:, slot, :].rearrange("p (k n) -> p k n", k=k), src)\
                        .then_inc(raw_landed[slot], 16)

            with sp.Fori(0, NEXP) as i:
                item_loads(i, i * FFN_HALVES)
            sp.wait_ge(tab_done, 1)
            n_over = sp.value_load(itab[0:1, 1:2], min_val=0, max_val=OVER)
            with sp.If(n_over > 0):
                with sp.Fori(0, n_over) as j:
                    e = sp.value_load(itab[0:1, bass.ds(j + 2, 1)], min_val=0, max_val=NEXP - 1)
                    item_loads(e, (j + NEXP) * FFN_HALVES)
            sp.wait_ge(fin_kept, 4)
            sp.dma_start(y_prompt[0], xtok[:, 0, :]).then_inc(y_stored, 16)
            sp.dma_start(y_sample[0], xtok[:, 1, :]).then_inc(y_stored, 16)
            sp.wait_ge(y_stored, 32)
            sp.wait_ge(stored, 64 * DEPTH)

        @block.gpsimd
        def _(pool):
            pool.dma_start(consts[:, :], shape_consts).then_inc(consts_in, 16)
            pool.dma_start(vrow[0:8, :], c_ctx.rearrange("(k p) -> k p", p=P)).then_inc(cond_in, 16)
            pool.dma_start(vrow[8:16, :], c[0].rearrange("(k p) -> k p", p=P)).then_inc(cond_in, 16)
            pool.dma_start(xtok[:, 0, :], x_prompt[0]).then_inc(x_in, 16)
            pool.dma_start(xtok[:, 1, :], x_sample[0]).then_inc(x_in, 16)
            pool.memset(ones[:, :], 1.0).then_inc(setup, 1)
            pool.memset(minus_half[:, :], -0.5).then_inc(setup, 1)
            pool.memset(scpad[:, :, :, :], 0.0).then_inc(setup, 1)
            pool.memset(cfpad[:, :, :, :], 0.0).then_inc(setup, 1)

            for l in range(DEPTH):
                if l:
                    pool.wait_ge(v_turned, 2)
                else:
                    pool.wait_ge(cond_turned, 1)
                for src, at, n in ((g_norm1[l], V_N1, 8), (g_norm2[l], V_N2, 8), (g_qa[l], V_QA, 2),
                                   (cf_b[l], V_CFB, 2), (cf_ln_g[l], V_LNG, 2), (cf_ln_b[l], V_LNB, 2)):
                    pool.dma_start(vrow[at:at + n, :], src.rearrange("(k p) -> k p", p=P)).then_inc(vrow_in, 16)
                pool.dma_start(vrow[V_SC:V_SC + 2 * SCK, :], sc_w[l].rearrange("a (k p) -> (a k) p", p=P))\
                    .then_inc(vrow_in, 16)
                pool.dma_start(vrow[V_CF:V_ROWS, :], cf_w[l].rearrange("a (k p) -> (a k) p", p=P))\
                    .then_inc(vrow_in, 16)
                pool.wait_ge(v_turned, 2 * l + 1)
                pool.dma_start(vrow[0:48, :], b_ada[l].rearrange("(k p) -> k p", p=P)).then_inc(vrow_in, 16)

            for l in range(DEPTH):
                if l:
                    pool.wait_ge(half_used, mix0[l - 1] + M_HALVES)
                for dst, src in ((wuq[:, :, :], w_uq[l].rearrange("(k p) n -> p k n", p=P)),
                                 (wukv[:, :], w_ukv[l]),
                                 (gkv_b[:, :], g_kva[l].partition_broadcast(P)),
                                 (gq_b[:, :], g_mla_q[l].partition_broadcast(P)),
                                 (gk_b[:, :], g_mla_k[l].partition_broadcast(P)),
                                 (gnq_b[:, :], g_na_q[l].partition_broadcast(P)),
                                 (gnk_b[:, :], g_na_k[l].partition_broadcast(P))):
                    pool.dma_start(dst, src).then_inc(small_in, 16)
                pool.dma_start(ckc, cache_mla_ckv[0, l]).then_inc(cache_in, 16)
                pool.dma_start(kpc, cache_mla_kpe[0, l]).then_inc(cache_in, 16)
                for rq in range(2):
                    for rk in range(2):
                        src = bass.AP(na_rpb.tensor, l * 1860 + (rk - rq + 7) * 31 + 15 - (GRID_W - 1),
                                      [[1, GRID_W], [465, HEADS], [1, GRID_W]])
                        pool.dma_start(hank[rq * 64:rq * 64 + 64, :, rk * 64:rk * 64 + 64], src)\
                            .then_inc(hank_in, 16)
                if l == 0:
                    pool.wait_ge(setup, 2)
                pool.wait_ge(stats_in, 3 * l + 1)
                pool.tensor_tensor(small[:, 0:4], small[:, 0:4], minus_half[:, :].to_broadcast([P, 4]),
                                   ALU.pow).then_inc(pool_pow, 1)
                pool.wait_ge(qa_normed, l + 1)
                pool.dma_start(new_ckv[0, l], tokA[:, 0, 256:384]).then_inc(stored, 16)
                pool.dma_start(new_kpe[0, l], tokA[:, 0, 384:416]).then_inc(stored, 16)
                pool.wait_ge(stats_in, 3 * l + 2)
                pool.tensor_tensor(small[:, 8:28], small[:, 8:28], minus_half[:, :].to_broadcast([P, 20]),
                                   ALU.pow).then_inc(pool_pow, 1)
                pool.wait_ge(stats_in, 3 * l + 3)
                pool.tensor_tensor(small[:, 32:48], small[:, 32:48], minus_half[:, :].to_broadcast([P, 16]),
                                   ALU.pow).then_inc(pool_pow, 1)
                pool.wait_ge(na_ready, l + 1)
                pool.dma_start(new_na_k[0, l].rearrange("s h d -> s (h d)"), tokN[:, 0, 256:512])\
                    .then_inc(stored, 16)
                pool.dma_start(new_na_v[0, l].rearrange("s h d -> s (h d)"), tokN[:, 0, 512:768])\
                    .then_inc(stored, 16)
                pool.wait_ge(o_done, 2 * l + 1)
                pool.dma_start(nakc, cache_na_k[0, l].rearrange("s h d -> s (h d)")).then_inc(nacache_in, 16)
                pool.dma_start(navc, cache_na_v[0, l].rearrange("s h d -> s (h d)")).then_inc(nacache_in, 16)
            pool.wait_ge(half_used, mix0[DEPTH - 1] + M_HALVES)
            pool.dma_start(wr, w_router[0].rearrange("(k p) e -> p k e", p=P)).then_inc(router_in, 16)

        @block.scalar
        def _(act):
            def flat2(a):
                return a.rearrange("p a b -> p (a b)")

            def flat3(a):
                return a.rearrange("p a b c -> p (a b c)")

            def hi(H):
                s, _ = SLOT_OF[H]
                part, h, _ = half(H)
                act.wait_ge(raw_landed[s % RAW], 16 * (s // RAW + 1))
                if H >= 2:
                    act.wait_ge(half_used, H - 1)
                act.activation(h, part, ACT.Copy).then_inc(hi_done, 1)

            act.wait_ge(cond_turned, 1)
            act.activation(small[:, 64:80], ps[:, 7, 0:16], ACT.Tanh, scale=0.5).then_inc(cond_th, 1)
            act.wait_ge(cond_ready, 1)
            act.activation(cond_hl[:, :, 0:2], small[:, 80:96].rearrange("p (g k) -> p k g", g=2), ACT.Copy)\
                .then_inc(cond_hi, 1)
            for b in range(4):
                act.wait_ge(x_turned, b + 1)
                act.activation(flat2(xT[:, 2 * b:2 * b + 2, :]), ps[:, b, :], ACT.Copy).then_inc(x_kept, 1)

            def norm(n):
                if n == 0:
                    act.wait_ge(x_kept, 4)
                elif n == 2:
                    act.wait_ge(ff_read, 1)
                else:
                    act.wait_ge(wo_read, 4 * (n // 2 + 1))
                act.activation(sq, xT[:, :, :], ACT.Square).then_inc(sq_done, 1)
                act.wait_ge(ms_done, n + 1)
                act.activation(rstd, rstd, ACT.Sqrt).then_inc(sd_done, 1)
                for k in range(2):
                    act.wait_ge(hF_done, 2 * n + k + 1)
                    act.activation(hT_hi[:, 4 * k:4 * k + 4, :], hF[:, 4 * k:4 * k + 4, :], ACT.Copy)\
                        .then_inc(h_hi, 1)

            def evac(l, f, dst, func=ACT.Copy, n=512, scale=1.0):
                act.wait_ge(half_used, filled(l, f))
                act.activation(dst, ps[:, f % 4, 0:n], func, scale=scale).then_inc(drained, 1)

            def keep_heads(u, d, first):
                act.wait_ge(heads_turned, 2 * u + (1 if first else 2))
                if first:
                    for g in range(2):
                        act.activation(QTf[0:d, 512 * g:512 * g + 512], ps[0:d, 4 + g, :], ACT.Copy)\
                            .then_inc(heads_kept, 1)
                    for s in range(2):
                        act.activation(KTf[0:d, 512 * s:512 * s + 512], ps[0:d, 6 + s, :], ACT.Copy)\
                            .then_inc(heads_kept, 1)
                else:
                    act.activation(KTf[0:d, 1024:1536], ps[0:d, 4, :], ACT.Copy).then_inc(heads_kept, 1)

            def exps(u, scale):
                act.wait_ge(max_done, u + 1)
                for s in range(3):
                    for h in range(HEADS):
                        b = HEADS * s + h
                        src = sbias[:, TOK * h:TOK * h + TOK] if u % 2 and s == 1 else \
                            ps[:, 5 + s, TOK * h:TOK * h + TOK]
                        act.activation(Pr[:, s, h, :], src, ACT.Exp, bias=small[:, 60 + b:61 + b], scale=scale,
                                       accum_out=small[:, 76 + b:77 + b]).then_inc(exp_done, 1)

            def keep_probs(u):
                act.wait_ge(probs_turned, u + 1)
                for s in range(3):
                    act.activation(KTf[:, 512 * s:512 * s + 512], ps[:, 5 + s, :], ACT.Copy)\
                        .then_inc(probs_kept, 1)

            def out_hi(u):
                act.wait_ge(o_turned, u + 1)
                act.activation(flat2(br_hi[:, 4 * (u % 2):4 * (u % 2) + 2, :]), ps[:, 4, :], ACT.Copy)\
                    .then_inc(o_hi, 1)

            def mixer_task(l, h):
                if h == 1:
                    for g in range(2):
                        evac(l, g, tokA[:, g, :], n=416)
                if h == 3:
                    for g in range(2):
                        evac(l, 2 + g, tokN[:, g, 0:512])
                    act.wait_ge(latent_turned, l + 1)
                    for k in range(2):
                        act.activation(qaT[:, k, :], ps[:, 4, 256 * k:256 * k + 256], ACT.Copy,
                                       scale=vecT[:, l, V_QA + k:V_QA + k + 1]).then_inc(latent_kept, 1)
                    act.activation(ckvT, ps[:, 5, 0:384], ACT.Copy).then_inc(latent_kept, 1)
                if h == 4:
                    evac(l, 4, tokN[:, :, 512:768])
                    act.wait_ge(qkv_done, 2 * l + 1)
                    for g in range(2):
                        act.activation(qk[:, 384 * g:384 * g + 384], ps[:, 6 + g, 0:384], ACT.Copy)\
                            .then_inc(qkv_kept, 1)
                    for s in range(2):
                        act.activation(KV[:, s, :], ps[:, 4 + s, :], ACT.Copy).then_inc(qkv_kept, 1)
                if h == 5:
                    act.wait_ge(qkv_done, 2 * l + 2)
                    act.activation(KV[:, 2, :], ps[:, 4, :], ACT.Copy).then_inc(qkv_kept, 1)
                if h in (5, 6):
                    evac(l, h, flat2(bc[:, 2 * (h - 5):2 * (h - 5) + 2, :]))
                if h == 8:
                    evac(l, 8, flat2(cf[:, 0:2, :]))
                    keep_heads(2 * l, QK, True)
                if h == 9:
                    evac(l, 9, flat2(cf[:, 2:4, :]), ACT.Tanh, scale=0.5)
                    keep_heads(2 * l, QK, False)
                if M_GATE <= h < M_BR:
                    n, j = divmod(2 * (h - M_GATE), 8)
                    if h == M_GATE:
                        act.wait_ge(stats_in, 3 * l + 3)
                    if h == M_GATE + 12:
                        act.wait_ge(b_lo, l + 1)
                        act.wait_ge(cf_used, l + 1)
                    evac(l, h, flat2(gates[:, n, j:j + 2, :]), ACT.Tanh, scale=0.5)
                if h == 11:
                    exps(2 * l, QK ** -0.5)
                if h == 12:
                    keep_probs(2 * l)
                    act.wait_ge(b_ready, l + 1)
                    act.activation(br_hi[:, 2:4, :], bc[:, 0:2, :], ACT.Copy).then_inc(b_hi, 1)
                if h == 14:
                    out_hi(2 * l)
                if h == 15:
                    keep_heads(2 * l + 1, HD, True)
                if h == 16:
                    keep_heads(2 * l + 1, HD, False)
                if h == 18:
                    exps(2 * l + 1, 1.0)
                if h == 19:
                    keep_probs(2 * l + 1)
                if h == 21:
                    out_hi(2 * l + 1)
                if h == 23:
                    act.wait_ge(ln_ms, l + 1)
                    act.activation(ln_sd, ln_sd, ACT.Sqrt).then_inc(ln_sdone, 1)
                if h == 24:
                    act.wait_ge(ln_z, l + 1)
                    act.activation(ln_sq, flat2(conv[:, :, :]), ACT.Tanh, scale=0.5).then_inc(ln_th, 1)
                    act.wait_ge(ln_o, l + 1)
                    act.activation(flat2(br_hi[:, 6:8, :]), ln_sq, ACT.Copy, scale=0.5).then_inc(d_hi, 1)
                if M_BR <= h < M_O:
                    for j in (2 * (h - M_BR), 2 * (h - M_BR) + 1):
                        act.wait_ge(merged_f, 8 * l + j + 1)
                        act.activation(hT_hi[:, j, :], gates[:, 0, j, :], ACT.Copy, scale=0.5)\
                            .then_inc(merged_hi, 1)

            for l in range(DEPTH):
                if l:
                    act.wait_ge(stored, 64 * l)
                for h in range(24):
                    hi(ada0[l] + h)
                    if l == 0 and h in (7, 9, 11, 13):
                        m = (h - 7) // 2
                        dst, n = (badaT[:, m // 2, :], 48) if m % 2 else (vecT[:, m // 2, :], V_ROWS)
                        act.wait_ge(v_turned, m + 1)
                        act.activation(dst, ps[:, 6 - m % 2, 0:n], ACT.Copy).then_inc(v_kept, 1)
                    if h >= 2 and h % 2 == 0:
                        c_ = h // 2 - 1
                        act.wait_ge(half_used, ada0[l] + 2 * c_ + 2)
                        if c_ >= 2:
                            act.wait_ge(ada_folded, 12 * l + c_ - 1)
                        act.activation(arow[:, c_ % 2, :], ps[0:4, c_ % 2, :], ACT.Copy).then_inc(ada_kept, 1)
                act.wait_ge(half_used, ada0[l] + 24)
                act.wait_ge(ada_folded, 12 * l + 10)
                act.activation(arow[:, 1, :], ps[0:4, 1, :], ACT.Copy).then_inc(ada_kept, 1)
                norm(2 * l)
                act.wait_ge(bias_turned, l + 1)
                act.activation(bias[:, :, :].rearrange("p h k -> p (h k)"), ps[:, 6, :], ACT.Copy)\
                    .then_inc(bias_kept, 1)
                for h in range(M_HALVES):
                    hi(mix0[l] + h)
                    if h:
                        mixer_task(l, h - 1)
                norm(2 * l + 1)
                if l == 0:
                    def ff_task(hh):
                        kind, ch = FFN[hh // 2]
                        q = hh % 2
                        if kind == "gate":
                            act.wait_ge(half_used, ff0 + hh + 1)
                            if ch:
                                act.wait_ge(ff_hid_done, 2 * ch - 1 + q)
                            act.activation(ff_act[:, q, :], ps[:, q, :], ACT.Silu).then_inc(ff_act_done, 1)
                        if kind == "up":
                            act.wait_ge(ff_hid_done, 2 * ch + q + 1)
                            if ch >= 2:
                                act.wait_ge(half_used, ff_used("down", ch - 2))
                            a = 4 * (ch % 2) + 2 * q
                            act.activation(flat2(br_hi[:, a:a + 2, :]), ff_hid[:, q, :], ACT.Copy)\
                                .then_inc(ff_hi, 1)

                    for hh in range(FFN_HALVES):
                        hi(ff0 + hh)
                        if hh:
                            ff_task(hh - 1)
            for b in range(4):
                act.wait_ge(h2_turned, b + 1)
                act.activation(h2tok[:, b // 2, 512 * (b % 2):512 * (b % 2) + 512], ps[:, 4 + b, :], ACT.Copy)\
                    .then_inc(h2_kept, 1)

            act.wait_ge(mask_done, 1)
            act.activation(tq[:, 4:6], tq[:, 4:6], ACT.Exp).then_inc(pair_exp, 1)

            act.wait_ge(tab_done, 1)
            n_items = act.value_load(itab[0:1, 0:1], min_val=NEXP, max_val=ITEMS)
            with act.Fori(0, n_items) as i:
                def item_hi(hh):
                    part, h, _ = item_half(hh)
                    slot = len(SLOTS) + hh // 2
                    act.wait_ge(raw_landed[slot % RAW], i * (16 * len(FFN) // RAW) + 16 * (slot // RAW + 1))
                    act.wait_ge(half_used, i * FFN_HALVES + (HALVES + hh - 1))
                    act.activation(h, part, ACT.Copy).then_inc(hi_done, 1)

                def item_task(hh):
                    kind, ch = FFN[hh // 2]
                    if kind == "gate" and hh % 2:
                        act.wait_ge(half_used, i * FFN_HALVES + (HALVES + hh + 1))
                        act.activation(ff_act[:, 0, :], ps[:, 0, :], ACT.Silu).then_inc(e_act, 1)
                    if (kind == "down" and hh % 2 and ch < CHUNKS - 1) or (kind == "up" and hh % 2 and ch == 0):
                        t = 0 if kind == "up" else ch + 1
                        act.wait_ge(e_turn, i * CHUNKS + (t + 1))
                        act.activation(flat2(br_hi[:, 0:2, :]), ps[:, 2, :], ACT.Copy).then_inc(e_hi, 1)

                item_hi(0)
                act.wait_ge(selT_t, i + 1)
                act.activation(selT, ps[:, 7, 0:256], ACT.Copy).then_inc(selT_kept, 1)
                act.wait_ge(xe_t, i + 1)
                act.activation(flat2(hT_hi[:, 0:4, :]), flat2(ps[:, 5:7, :]), ACT.Copy).then_inc(xe_hi, 1)
                for hh in range(1, FFN_HALVES):
                    item_hi(hh)
                    item_task(hh - 1)
                act.wait_ge(half_used, i * FFN_HALVES + (HALVES + FFN_HALVES))
                act.activation(y_tok, flat2(ps[:, 3:5, :]), ACT.Copy).then_inc(y_kept, 1)

            for b in range(4):
                act.wait_ge(fin_t, b + 1)
                act.activation(xtok[:, b // 2, 512 * (b % 2):512 * (b % 2) + 512], ps[:, b, :], ACT.Copy)\
                    .then_inc(fin_kept, 1)

        @block.vector
        def _(dve):
            links = [0]

            def link(ins):
                links[0] += 1
                ins.then_inc(dve_link, 1)
                dve.wait_ge(dve_link, links[0])

            tt, ts, stt = dve.tensor_tensor, dve.tensor_scalar, dve.scalar_tensor_tensor

            def lo(H):
                part, h, w = half(H)
                dve.wait_ge(hi_done, H + 1)
                tt(w, part, h.bitcast(F32), ALU.subtract).then_inc(lo_done, 1)

            dve.wait_ge(cond_th, 1)
            link(ts(small[:, 64:80], small[:, 64:80], 0.5, 0.5, ALU.mult, ALU.add))
            tt(small[:, 80:96], small[:, 64:80], ps[:, 7, 0:16], ALU.mult).then_inc(cond_ready, 1)
            dve.wait_ge(cond_hi, 1)
            tt(cond_hl[:, :, 2:4], small[:, 80:96].rearrange("p (g k) -> p k g", g=2),
               cond_hl[:, :, 0:2].bitcast(F32), ALU.subtract).then_inc(cond_lo, 1)

            def modulation(l):
                dve.wait_ge(ada_folded, 12 * (l + 1))
                if l == 0:
                    dve.wait_ge(v_kept, 2 * DEPTH)
                link(tt(modT[:, :, :], ps[:, 2, 0:96].rearrange("p (m g) -> p m g", g=2),
                        badaT[:, l, :].unsqueeze(2).to_broadcast([P, 48, 2]), ALU.add))
                for s, v in ((0, V_N1), (1, V_N2)):
                    ins = stt(scaleT[:, s, :, :], modT[:, 24 * s + 8:24 * s + 16, :], 1.0,
                              vecT[:, l, v:v + 8].unsqueeze(2).to_broadcast([P, 8, 2]), ALU.add, ALU.mult)
                ins.then_inc(mod_done, 1)

            def norm(n):
                s = n % 2
                dve.wait_ge(stat_done, n + 1)
                ts(rstd, ps[:, 4, 0:256], 1.0 / D, EPS, ALU.mult, ALU.add).then_inc(ms_done, 1)
                dve.wait_ge(sd_done, n + 1)
                link(dve.reciprocal(rstd, rstd))
                if s == 0:
                    dve.wait_ge(mod_done, n // 2 + 1)
                for k in range(0, KT, 4):
                    link(tt(hF[:, k:k + 4, :], xT[:, k:k + 4, :], rstd.unsqueeze(1).to_broadcast([P, 4, NT]),
                            ALU.mult))
                    for kk in range(k, k + 4):
                        for g in range(2):
                            part = hF[:, kk, TOK * g:TOK * g + TOK]
                            ins = ts(part, part, scaleT[:, s, kk, g:g + 1], modT[:, 24 * s + kk, g:g + 1],
                                     ALU.mult, ALU.add)
                    ins.then_inc(hF_done, 1)
                for k in range(2):
                    dve.wait_ge(h_hi, 2 * n + k + 1)
                    tt(hT_lo[:, 4 * k:4 * k + 4, :], hF[:, 4 * k:4 * k + 4, :],
                       hT_hi[:, 4 * k:4 * k + 4, :].bitcast(F32), ALU.subtract).then_inc(h_lo, 1)

            def wide_col(a, n):
                return a.unsqueeze(2).to_broadcast([P, a.shape[1], n])

            def latents(l):
                dve.wait_ge(drained, 25 * l + 2)
                s = qk[:, 0:768].rearrange("p (g d) -> p g d", g=2)
                link(tt(s, tokA[:, :, 0:384], tokA[:, :, 0:384], ALU.mult))
                dve.tensor_reduce(small[:, 0:2], s[:, :, 0:256], AX.X, ALU.add)
                link(dve.tensor_reduce(small[:, 2:4], s[:, :, 256:384], AX.X, ALU.add))
                ts(small[:, 0:2], small[:, 0:2], 1.0 / QL, EPS, ALU.mult, ALU.add)
                ts(small[:, 2:4], small[:, 2:4], 1.0 / KVL, EPS, ALU.mult, ALU.add).then_inc(stats_in, 1)
                dve.wait_ge(pool_pow, 3 * l + 1)
                tt(tokA[:, :, 0:256], tokA[:, :, 0:256], wide_col(small[:, 0:2], 256), ALU.mult)
                link(tt(tokA[:, :, 256:384], tokA[:, :, 256:384], wide_col(small[:, 2:4], 128), ALU.mult))
                dve.wait_ge(small_in, 112 * (l + 1))
                tt(tokA[:, :, 256:384], tokA[:, :, 256:384], gkv_b[:, :].unsqueeze(1).to_broadcast([P, 2, KVL]),
                   ALU.mult).then_inc(qa_normed, 1)

            def head_stats(l):
                dve.wait_ge(qkv_kept, 5 * l + 5)
                dve.wait_ge(cache_in, 32 * (l + 1))
                link(tt(heads_sq, qk[:, 0:768], qk[:, 0:768], ALU.mult))
                link(dve.tensor_reduce(small[:, 8:16], heads_sq.rearrange("p (a d) -> p a d", d=QK), AX.X, ALU.add))
                knope = KV[:, :, :].rearrange("p s (h d) -> p s h d", h=HEADS)[:, :, :, 0:NOPE]
                link(tt(heads_sq.rearrange("p (s h d) -> p s h d", s=3, h=HEADS), knope, knope, ALU.mult))
                link(dve.tensor_reduce(small[:, 16:28], heads_sq.rearrange("p (a d) -> p a d", d=NOPE), AX.X,
                                       ALU.add))
                kpe = tokA[:, :, 384:416]
                tt(heads_sq[:, 0:64].rearrange("p (g d) -> p g d", g=2), kpe, kpe, ALU.mult)
                link(tt(heads_sq[:, 64:96], kpc, kpc, ALU.mult))
                link(dve.tensor_reduce(small[:, 112:115], heads_sq[:, 0:96].rearrange("p (s d) -> p s d", s=3),
                                       AX.X, ALU.add))
                kss = small[:, 16:28].rearrange("p (s h) -> p s h", s=3)
                link(tt(kss, kss, wide_col(small[:, 112:115], HEADS), ALU.add))
                ts(small[:, 8:28], small[:, 8:28], 1.0 / QK, EPS, ALU.mult, ALU.add).then_inc(stats_in, 1)

            def head_norm(l):
                dve.wait_ge(pool_pow, 3 * l + 2)
                q = qk[:, 0:768].rearrange("p (a d) -> p a d", d=QK)
                kn = qk[:, 768:1920].rearrange("p (a d) -> p a d", d=QK)
                tt(q, q, wide_col(small[:, 8:16], QK), ALU.mult)
                rs = small[:, 16:28].rearrange("p (s h) -> p s h", s=3)
                tt(Kn[:, :, :, 0:NOPE], KV[:, :, :].rearrange("p s (h d) -> p s h d", h=HEADS)[:, :, :, 0:NOPE],
                   rs.unsqueeze(3).to_broadcast([P, 3, HEADS, NOPE]), ALU.mult)
                tt(Kn[:, 0:2, :, NOPE:QK], tokA[:, :, 384:416].unsqueeze(2).to_broadcast([P, 2, HEADS, ROPE]),
                   rs[:, 0:2, :].unsqueeze(3).to_broadcast([P, 2, HEADS, ROPE]), ALU.mult)
                link(tt(Kn[:, 2, :, NOPE:QK], kpc.unsqueeze(1).to_broadcast([P, HEADS, ROPE]),
                        wide_col(small[:, 24:28], ROPE), ALU.mult))
                tt(q, q, gq_b[:, :].unsqueeze(1).to_broadcast([P, 8, QK]), ALU.mult)
                link(tt(kn, kn, gk_b[:, :].unsqueeze(1).to_broadcast([P, 12, QK]), ALU.mult))

            def rope(l):
                def trig(at):
                    return consts[:, at:at + 16].rearrange("p (a f) -> p a f", a=2).unsqueeze(1)\
                        .to_broadcast([P, HEADS, 2, 8])
                cos, sin = trig(K_COS), trig(K_SIN)
                parts = []
                for n, x in enumerate((Q[:, 1, :, NOPE:QK], Kn[:, 1, :, NOPE:QK])):
                    v = x.rearrange("p h (a b f) -> p h a b f", a=2, b=2)
                    x1, x2 = v[:, :, :, 0, :], v[:, :, :, 1, :]
                    t = [ropet[:, 4 * n + m, :].rearrange("p (h a f) -> p h a f", h=HEADS, a=2) for m in range(4)]
                    tt(t[0], x1, cos, ALU.mult)
                    tt(t[1], x2, sin, ALU.mult)
                    tt(t[2], x1, sin, ALU.mult)
                    ins = tt(t[3], x2, cos, ALU.mult)
                    parts.append((x1, x2, t))
                link(ins)
                for x1, x2, t in parts:
                    tt(x1, t[0], t[1], ALU.subtract)
                    ins = tt(x2, t[2], t[3], ALU.add)
                ins.then_inc(qk_ready, 1)

            def na_stats(l):
                dve.wait_ge(drained, 25 * l + 5)
                link(tt(na_sq, tokN[:, :, 0:512], tokN[:, :, 0:512], ALU.mult))
                link(dve.tensor_reduce(small[:, 32:48], big[:, 0:1024].rearrange("p (a d) -> p a d", d=HD), AX.X,
                                       ALU.add))
                ts(small[:, 32:48], small[:, 32:48], 1.0 / HD, EPS, ALU.mult, ALU.add).then_inc(stats_in, 1)

            def na_norm(l):
                dve.wait_ge(pool_pow, 3 * l + 3)
                x = tokN[:, :, 0:512].rearrange("p g (a d) -> p g a d", d=HD)
                rs = small[:, 32:48].rearrange("p (g a) -> p g a", g=2).unsqueeze(3).to_broadcast([P, 2, 8, HD])
                link(tt(x, x, rs, ALU.mult))
                link(ts(gnq_b[:, :], gnq_b[:, :], HD ** -0.5, None, ALU.mult))
                for a, gain in ((0, gnq_b), (4, gnk_b)):
                    y = x[:, :, a:a + 4, :]
                    ins = tt(y, y, gain[:, :].unsqueeze(1).unsqueeze(1).to_broadcast([P, 2, 4, HD]), ALU.mult)
                ins.then_inc(na_ready, 1)

            def softmax_max(u, scale):
                dve.wait_ge(scores_done, u + 1)
                if u % 2:
                    dve.wait_ge(bias_kept, u // 2 + 1)
                    if u // 2 == 0:
                        dve.wait_ge(consts_in, 16)
                    link(tt(sbias, ps[:, 6, :], bias[:, :, :].rearrange("p h k -> p (h k)"), ALU.add))
                    m = sbias.rearrange("p (h k) -> p h k", h=HEADS)
                    link(tt(m, m, consts[:, K_MASK:K_MASK + TOK].unsqueeze(1).to_broadcast([P, HEADS, TOK]),
                            ALU.add))
                for s in range(3):
                    src = sbias if u % 2 and s == 1 else ps[:, 5 + s, :]
                    ins = dve.tensor_reduce(small[:, 92 + 4 * s:96 + 4 * s],
                                            src.rearrange("p (h k) -> p h k", h=HEADS), AX.X, ALU.max)
                link(ins)
                link(tt(small[:, 96:100], small[:, 96:100], small[:, 100:104], ALU.max))
                ts(small[:, 60:68], small[:, 92:100], -scale, None, ALU.mult)
                ts(small[:, 68:72], small[:, 96:100], -scale, None, ALU.mult).then_inc(max_done, 1)

            def scale_out(u):
                dve.wait_ge(exp_done, 12 * (u + 1))
                link(tt(small[:, 80:84], small[:, 80:84], small[:, 84:88], ALU.add))
                link(dve.reciprocal(small[:, 104:112], small[:, 76:84]))
                dve.wait_ge(o_done, u + 1)
                tt(O.rearrange("p g (h d) -> p g h d", h=HEADS),
                   ps[:, 4, :].rearrange("p (g h d) -> p g h d", g=2, h=HEADS),
                   small[:, 104:112].rearrange("p (g h) -> p g h", g=2).unsqueeze(3)
                   .to_broadcast([P, 2, HEADS, HD]), ALU.mult).then_inc(o_scaled, 1)

            def out_lo(u):
                a = 4 * (u % 2)
                dve.wait_ge(o_hi, u + 1)
                tt(br_lo[:, a:a + 2, :].rearrange("p a b -> p (a b)"), ps[:, 4, :],
                   br_hi[:, a:a + 2, :].bitcast(F32).rearrange("p a b -> p (a b)"), ALU.subtract)\
                    .then_inc(o_lo, 1)

            def two(a):
                return a.rearrange("p (g t) -> p g t", g=2)

            conv_ops = [0]

            def tap(l, pad, taps, row, k, tile):
                src = pad[:, tile, :, k:k + TOK]
                dst = two(conv[:, tile, :])
                w = vecT[:, l, row + 2 * k + tile:row + 2 * k + tile + 1]
                if k:
                    dve.wait_ge(conv_v, conv_ops[0] - 1)
                    ins = stt(dst, src, w, dst, ALU.mult, ALU.add)
                else:
                    ins = ts(dst, src, w, None, ALU.mult)
                ins.then_inc(conv_v, 1)
                conv_ops[0] += 1

            def branch_b(l):
                for k in range(SCK):
                    for tile in range(2):
                        tap(l, scpad, SCK, V_SC, k, tile)
                dve.wait_ge(conv_v, conv_ops[0])
                tt(bc[:, 0:2, :], bc[:, 0:2, :], conv[:, :, :], ALU.mult).then_inc(b_ready, 1)

            def branch_d(l, first, last):
                for n in range(first, last):
                    tap(l, cfpad, CFK, V_CF, n // 2, n % 2)

            def mixer_task(l, h):
                if h == 1:
                    latents(l)
                if h == 5:
                    head_stats(l)
                if h == 6:
                    na_stats(l)
                    head_norm(l)
                if h == 7:
                    rope(l)
                    dve.wait_ge(drained, 25 * l + 7)
                    dve.wait_ge(half_used, filled(l, 7))
                    if l == 0:
                        dve.wait_ge(setup, 4)
                    tt(scpad[:, :, :, 1:1 + TOK], ps[:, 3, :].rearrange("p (a g t) -> p a g t", a=2, g=2),
                       bc[:, 2:4, :].rearrange("p a (g t) -> p a g t", g=2), ALU.mult).then_inc(xv_read, 1)
                if h == 8:
                    dve.wait_ge(xv_read, l + 1)
                    na_norm(l)
                    branch_b(l)
                if h == 10:
                    softmax_max(2 * l, QK ** -0.5)
                if h == 11:
                    dve.wait_ge(drained, 25 * l + 9)
                    for tile in range(2):
                        ins = stt(cfpad[:, tile, :, 15:15 + TOK], two(cf[:, 2 + tile, :]), 1.0,
                                  two(cf[:, tile, :]), ALU.add, ALU.mult)
                    ins.then_inc(cf_used, 1)
                    dve.wait_ge(cf_used, l + 1)
                    dve.wait_ge(b_ready, l + 1)
                    branch_d(l, 0, 6)
                if h == 12:
                    dve.wait_ge(b_hi, l + 1)
                    tt(br_lo[:, 2:4, :], bc[:, 0:2, :], br_hi[:, 2:4, :].bitcast(F32), ALU.subtract)\
                        .then_inc(b_lo, 1)
                    branch_d(l, 6, 12)
                if h == 13:
                    scale_out(2 * l)
                    branch_d(l, 12, 18)
                if h == 14:
                    out_lo(2 * l)
                    branch_d(l, 18, 24)
                if h == 15:
                    branch_d(l, 24, 32)
                if h == 16:
                    branch_d(l, 32, 40)
                if h == 17:
                    softmax_max(2 * l + 1, 1.0)
                if h == 18:
                    branch_d(l, 40, 48)
                if h == 19:
                    branch_d(l, 48, 56)
                if h == 20:
                    scale_out(2 * l + 1)
                    branch_d(l, 56, 62)
                if h == 21:
                    out_lo(2 * l + 1)
                    dve.wait_ge(conv_v, conv_ops[0])
                    for tile in range(2):
                        ins = ts(conv[:, tile, :], conv[:, tile, :], 0.5, vecT[:, l, V_CFB + tile:V_CFB + tile + 1],
                                 ALU.mult, ALU.add)
                    ins.then_inc(conv_ready, 1)
                if h == 22:
                    dve.wait_ge(ln_sum, l + 1)
                    dve.wait_ge(conv_ready, l + 1)
                    for tile in range(2):
                        ins = stt(conv[:, tile, :], ps[:, 5, 0:256], -1.0 / BW, conv[:, tile, :], ALU.mult, ALU.add)
                    link(ins)
                    tt(ln_sq, conv[:, :, :].rearrange("p a t -> p (a t)"),
                       conv[:, :, :].rearrange("p a t -> p (a t)"), ALU.mult).then_inc(ln_sq_done, 1)
                if h == 23:
                    dve.wait_ge(ln_sqsum, l + 1)
                    ts(ln_sd, ps[:, 6, 0:256], 1.0 / BW, EPS, ALU.mult, ALU.add).then_inc(ln_ms, 1)
                if h == 24:
                    dve.wait_ge(ln_sdone, l + 1)
                    link(dve.reciprocal(ln_sd, ln_sd))
                    link(tt(conv[:, :, :], conv[:, :, :], ln_sd.unsqueeze(1).to_broadcast([P, 2, NT]), ALU.mult))
                    for tile in range(2):
                        ins = ts(conv[:, tile, :], conv[:, tile, :], vecT[:, l, V_LNG + tile:V_LNG + tile + 1],
                                 vecT[:, l, V_LNB + tile:V_LNB + tile + 1], ALU.mult, ALU.add)
                    ins.then_inc(ln_z, 1)
                    dve.wait_ge(ln_th, l + 1)
                    stt(ln_sq, ln_sq, 1.0, conv[:, :, :].rearrange("p a t -> p (a t)"), ALU.add, ALU.mult)\
                        .then_inc(ln_o, 1)
                    dve.wait_ge(d_hi, l + 1)
                    stt(br_lo[:, 6:8, :].rearrange("p a t -> p (a t)"), ln_sq, 0.5,
                        br_hi[:, 6:8, :].bitcast(F32).rearrange("p a t -> p (a t)"), ALU.mult, ALU.subtract)\
                        .then_inc(d_lo, 1)
                if M_BR <= h < M_O:
                    for j in (2 * (h - M_BR), 2 * (h - M_BR) + 1):
                        if j % 2:
                            dve.wait_ge(half_used, mix0[l] + h + 1)
                        else:
                            dve.wait_ge(proj_fill, 4 * l + j // 2 + 1)
                        dve.wait_ge(drained, 25 * (l + 1))
                        for b in range(2):
                            g2 = gates[:, 2 * b:2 * b + 2, j, :]
                            ins = stt(g2, g2, 1.0, ps[:, 2 * (j % 2) + b, :].rearrange("p (n t) -> p n t", n=2),
                                      ALU.add, ALU.mult)
                        ins.then_inc(proj_read, 1)
                        dve.wait_ge(proj_read, 8 * l + j + 1)
                        link(tt(gates[:, 0:2, j, :], gates[:, 0:2, j, :], gates[:, 2:4, j, :], ALU.add))
                        tt(gates[:, 0, j, :], gates[:, 0, j, :], gates[:, 1, j, :], ALU.add).then_inc(merged_f, 1)
                        dve.wait_ge(merged_hi, 8 * l + j + 1)
                        stt(hT_lo[:, j, :], gates[:, 0, j, :], 0.5, hT_hi[:, j, :].bitcast(F32), ALU.mult,
                            ALU.subtract).then_inc(merged_lo, 1)
                if M_O <= h:
                    dve.wait_ge(half_used, mix0[l] + h + 1)
                    for jj in range(2):
                        j = 2 * (h - M_O) + jj
                        for g in range(2):
                            r = xT[:, j, TOK * g:TOK * g + TOK]
                            a = 256 * jj + TOK * g
                            ins = stt(r, ps[:, h - M_O, a:a + TOK], modT[:, 16 + j, g:g + 1], r, ALU.mult, ALU.add)
                    ins.then_inc(wo_read, 1)

            def ff_task(hh):
                kind, ch = FFN[hh // 2]
                q = hh % 2
                if kind == "up":
                    n = 2 * ch + q + 1
                    dve.wait_ge(ff_act_done, n)
                    dve.wait_ge(half_used, ff0 + hh + 1)
                    if ch:
                        dve.wait_ge(ff_hi, n - 2)
                    tt(ff_hid[:, q, :], ff_act[:, q, :], ps[:, 2 + q, :], ALU.mult).then_inc(ff_hid_done, 1)
                    dve.wait_ge(ff_hi, n)
                    a = 4 * (ch % 2) + 2 * q
                    tt(br_lo[:, a:a + 2, :].rearrange("p a b -> p (a b)"), ff_hid[:, q, :],
                       br_hi[:, a:a + 2, :].bitcast(F32).rearrange("p a b -> p (a b)"), ALU.subtract)\
                        .then_inc(ff_lo, 1)

            for l in range(DEPTH):
                for h in range(24):
                    lo(ada0[l] + h)
                modulation(l)
                norm(2 * l)
                for h in range(M_HALVES):
                    lo(mix0[l] + h)
                    if h:
                        mixer_task(l, h - 1)
                mixer_task(l, M_HALVES - 1)
                dve.wait_ge(wo_read, 4 * (l + 1))
                norm(2 * l + 1)
                if l == 0:
                    for hh in range(FFN_HALVES):
                        lo(ff0 + hh)
                        if hh:
                            ff_task(hh - 1)
                    dve.wait_ge(half_used, ff_used("down", CHUNKS - 1))
                    for j in range(KT):
                        for g in range(2):
                            r = xT[:, j, TOK * g:TOK * g + TOK]
                            a = 256 * (j % 2) + TOK * g
                            ins = stt(r, ps[:, 4 + j // 2, a:a + TOK], modT[:, 40 + j, g:g + 1], r,
                                      ALU.mult, ALU.add)
                    ins.then_inc(ff_read, 1)

            def col(a):
                return a.unsqueeze(2)

            left = consts[:, K_LEFT:K_LEFT + 8].unsqueeze(1).to_broadcast([P, 2, 8])
            dve.wait_ge(lg_done, 1)
            link(dve.tensor_copy(lg, ps[:, 0, 0:16].rearrange("p (g e) -> p g e", g=2)))

            def first_largest(logits, top, onehot):
                link(dve.tensor_reduce(top, logits, AX.X, ALU.max))
                link(tt(tmp, logits, col(top).to_broadcast([P, 2, 8]), ALU.is_ge))
                link(tt(tmp, tmp, left, ALU.mult))
                link(dve.tensor_reduce(tq[:, 8:10], tmp, AX.X, ALU.max))
                link(tt(onehot, left, col(tq[:, 8:10]).to_broadcast([P, 2, 8]), ALU.is_equal))

            first_largest(lg, tq[:, 0:2], oh1)
            link(stt(lg2, oh1, -1e30, lg, ALU.mult, ALU.add))
            first_largest(lg2, tq[:, 2:4], oh2)
            link(tt(tq[:, 4:6], tq[:, 2:4], tq[:, 0:2], ALU.subtract))
            tt(mask, oh1, oh2, ALU.add).then_inc(mask_done, 1)
            dve.wait_ge(pair_exp, 1)
            link(ts(tq[:, 6:8], tq[:, 4:6], 1.0, None, ALU.add))
            link(dve.reciprocal(tq[:, 6:8], tq[:, 6:8]))
            link(tt(tq[:, 4:6], tq[:, 4:6], tq[:, 6:8], ALU.mult))
            tt(oh1, oh1, col(tq[:, 6:8]).to_broadcast([P, 2, 8]), ALU.mult)
            link(tt(oh2, oh2, col(tq[:, 4:6]).to_broadcast([P, 2, 8]), ALU.mult))
            tt(tab[:, 2, :, 0:8], oh1, oh2, ALU.add)
            dve.tensor_copy(tab[:, 1, :, 0:8], mask)
            dve.wait_ge(pos_done, 1)
            dve.tensor_copy(tab[:, 0, :, 0:8], ps[:, 1, 0:16].rearrange("p (g e) -> p g e", g=2))
            link(ts(ov, ps[:, 1, 16:24], float(CAP), None, ALU.is_gt))
            link(tt(w64, consts[:, K_BEFORE:K_BEFORE + 64].rearrange("p (a e) -> p a e", a=8),
                    ov.unsqueeze(1).to_broadcast([P, 8, 8]), ALU.mult))
            link(dve.tensor_reduce(rank, w64, AX.X, ALU.add))
            for k in range(OVER):
                ins = stt(ohk[:, k, :], rank, float(k), ov, ALU.is_equal, ALU.mult)
            link(ins)
            for q in range(3):
                a = tab[:, q, :, 0:8]
                if q == 0:
                    link(ts(tmp, a, float(-CAP), None, ALU.add))
                    a = tmp
                for t in range(2):
                    link(tt(wide[:, t, :, :], ohk, a[:, t, :].unsqueeze(1).to_broadcast([P, OVER, 8]), ALU.mult))
                link(dve.tensor_reduce(tab[:, q, :, NEXP:ITEMS], wide, AX.X, ALU.add))
            link(tt(wide[:, 0, :, :], ohk, consts[:, K_EXP:K_EXP + 8].unsqueeze(1).to_broadcast([P, OVER, 8]),
                    ALU.mult))
            dve.tensor_reduce(eidx[:, 2:2 + OVER], wide[:, 0, :, :], AX.X, ALU.add)
            link(dve.tensor_reduce(eidx[:, 1:2], ov, AX.X, ALU.add))
            link(ts(eidx[:, 0:1], eidx[:, 1:2], float(NEXP), None, ALU.add))
            dve.memset(fT, 0.0)
            dve.tensor_copy(itab[0:1, 0:OVER + 2], eidx[0:1, :]).then_inc(tab_done, 1)

            dve.wait_ge(tab_done, 1)
            n_items = dve.value_load(itab[0:1, 0:1], min_val=NEXP, max_val=ITEMS)
            iota = consts[:, K_IOTA:K_IOTA + P]
            with dve.Fori(0, n_items) as i:
                def item_lo(hh):
                    part, h, w = item_half(hh)
                    dve.wait_ge(hi_done, i * FFN_HALVES + (HALVES + hh + 1))
                    tt(w, part, h.bitcast(F32), ALU.subtract).then_inc(lo_done, 1)

                def item_task(hh):
                    kind, ch = FFN[hh // 2]
                    if kind == "up" and hh % 2:
                        dve.wait_ge(e_act, i * CHUNKS + (ch + 1))
                        dve.wait_ge(half_used, i * FFN_HALVES + (HALVES + hh + 1))
                        tt(ff_hid[:, 0, :], ff_act[:, 0, :], ps[:, 1, :], ALU.mult).then_inc(e_hid, 1)
                    if (kind == "down" and hh % 2 and ch < CHUNKS - 1) or (kind == "up" and hh % 2 and ch == 0):
                        t = 0 if kind == "up" else ch + 1
                        dve.wait_ge(e_hi, i * CHUNKS + (t + 1))
                        tt(br_lo[:, 0:2, :].rearrange("p a b -> p (a b)"), ps[:, 2, :],
                           br_hi[:, 0:2, :].bitcast(F32).rearrange("p a b -> p (a b)"), ALU.subtract)\
                            .then_inc(e_lo, 1)

                dve.tensor_copy(stage, tab[:, :, :, bass.ds(i, 1)].rearrange("p q t i -> p q (t i)"))\
                    .then_inc(staged, 1)
                dve.wait_ge(staged, i + 1)
                for t in range(2):
                    ts(sel[:, t, :], iota, stage[:, 0, t:t + 1], stage[:, 1, t:t + 1], ALU.is_equal, ALU.mult)
                    ins = ts(selg[:, t, :], iota, stage[:, 0, t:t + 1], stage[:, 2, t:t + 1], ALU.is_equal,
                             ALU.mult)
                ins.then_inc(sel_done, 1)
                item_lo(0)
                dve.wait_ge(xe_hi, i + 1)
                tt(hT_lo[:, 0:4, :].rearrange("p a b -> p (a b)"), ps[:, 5:7, :].rearrange("p a b -> p (a b)"),
                   hT_hi[:, 0:4, :].bitcast(F32).rearrange("p a b -> p (a b)"), ALU.subtract).then_inc(xe_lo, 1)
                for hh in range(1, FFN_HALVES):
                    item_lo(hh)
                    item_task(hh - 1)
                for r, bank in enumerate((5, 6, 7, 2)):
                    dve.wait_ge(sc_fill, i * 4 + (r + 1))
                    f = fT[:, 2 * r:2 * r + 2, :].rearrange("p a b -> p (a b)")
                    ins = tt(f, ps[:, bank, :], f, ALU.add)
                ins.then_inc(item_added, 1)
            dve.wait_ge(item_added, n_items)
            for j in range(KT):
                for g in range(2):
                    r = xT[:, j, TOK * g:TOK * g + TOK]
                    ins = stt(r, fT[:, j, TOK * g:TOK * g + TOK], modT[:, 40 + j, g:g + 1], r, ALU.mult, ALU.add)
            ins.then_inc(moe_done, 1)

        @block.tensor
        def _(pe):
            mm = pe.matmul

            def mm3(out, a_hi, a_lo, b_hi, b_lo, start, stop, shared=False):
                mm(out, a_hi, b_hi, start=start, stop=False, skip_group_check=shared)
                mm(out, a_hi, b_lo, start=False, stop=False, skip_group_check=shared)
                return mm(out, a_lo, b_hi, start=False, stop=stop, skip_group_check=shared)

            def turn(out, x):
                return pe.transpose(out, x, ident[0:x.shape[0], 0:x.shape[0]])

            def tok(g):
                return slice(TOK * g, TOK * g + TOK)

            pe.wait_ge(consts_in, 16)
            pe.wait_ge(cond_in, 32)
            turn(ps[:, 7, 0:16], vrow[0:16, :]).then_inc(cond_turned, 1)
            pe.wait_ge(x_in, 32)
            for b in range(4):
                for k in (2 * b, 2 * b + 1):
                    for g in range(2):
                        a = 256 * (k % 2) + TOK * g
                        ins = turn(ps[:, b, a:a + TOK], xtok[:, g, P * k:P * k + P])
                ins.then_inc(x_turned, 1)

            def ada_fold(l, c_):
                pe.wait_ge(ada_kept, 12 * l + c_ + 1)
                for q in range(4):
                    a = 2 * (4 * c_ + q)
                    ins = mm(ps[:, 2, a:a + 2], arow[0:4, c_ % 2, P * q:P * q + P],
                             consts[0:4, K_FOLD:K_FOLD + 2], start=True, stop=True)
                ins.then_inc(ada_folded, 1)

            def ada(l):
                if l == 0:
                    pe.wait_ge(cond_lo, 1)
                    pe.wait_ge(x_kept, 4)
                for h in range(24):
                    c_, q = divmod(h, 2)
                    if q == 0 and c_ >= 2:
                        pe.wait_ge(ada_kept, 12 * l + c_ - 1)
                    pe.wait_ge(lo_done, ada0[l] + h + 1)
                    _, wh, wl = half(ada0[l] + h)
                    for k in range(4):
                        x = cond_hl[:, 4 * q + k, :]
                        mm(ps[0:4, c_ % 2, :], x, wh[:, k, :], start=(q == 0 and k == 0), stop=False)
                        ins = mm(ps[0:4, c_ % 2, :], x, wl[:, k, :], start=False, stop=(q == 1 and k == 3))
                    ins.then_inc(half_used, 1)
                    if q:
                        if c_:
                            ada_fold(l, c_ - 1)
                    if l == 0 and h in (5, 7, 9, 11):
                        m = (h - 5) // 2
                        n = V_ROWS if m % 2 == 0 else 48
                        pe.wait_ge(vrow_in, 16 * (9 * (m // 2) + (9 if m % 2 else 8)))
                        if m >= 2:
                            pe.wait_ge(v_kept, m - 1)
                        turn(ps[:, 6 - m % 2, 0:n], vrow[0:n, :]).then_inc(v_turned, 1)
                ada_fold(l, 11)

            def stat(n):
                pe.wait_ge(sq_done, n + 1)
                if n == 0:
                    pe.wait_ge(setup, 4)
                for k in range(KT):
                    ins = mm(ps[:, 4, 0:NT], ones[:, :], sq[:, k, :], start=(k == 0), stop=(k == KT - 1))
                ins.then_inc(stat_done, 1)

            def free_bank(l, f):
                if f - 4 == 7:
                    pe.wait_ge(xv_read, l + 1)
                elif f >= 4:
                    pe.wait_ge(drained, 25 * l + (f - 3 if f - 4 < 7 else f - 4))

            def heads(u, d, q, k, first):
                if first:
                    for g in range(2):
                        for h in range(HEADS):
                            turn(ps[0:d, 4 + g, TOK * h:TOK * h + TOK], q(g, h))
                    for s in range(2):
                        for h in range(HEADS):
                            ins = turn(ps[0:d, 6 + s, TOK * h:TOK * h + TOK], k(s, h))
                else:
                    pe.wait_ge(heads_kept, 5 * u + 1)
                    for h in range(HEADS):
                        ins = turn(ps[0:d, 4, TOK * h:TOK * h + TOK], k(2, h))
                ins.then_inc(heads_turned, 1)

            def scores(u, d):
                pe.wait_ge(heads_kept, 5 * (u + 1))
                for s in range(3):
                    for h in range(HEADS):
                        ins = mm(ps[:, 5 + s, TOK * h:TOK * h + TOK], QT[0:d, min(s, 1), h, :], KTt[0:d, s, h, :],
                                 start=True, stop=True)
                ins.then_inc(scores_done, 1)

            def turn_probs(u):
                pe.wait_ge(exp_done, 12 * (u + 1))
                for s in range(3):
                    for h in range(HEADS):
                        ins = turn(ps[:, 5 + s, TOK * h:TOK * h + TOK], Pr[:, s, h, :])
                ins.then_inc(probs_turned, 1)

            def weigh(u, v):
                pe.wait_ge(probs_kept, 3 * (u + 1))
                for g in range(2):
                    for h in range(HEADS):
                        o = ps[:, 4, 256 * g + HD * h:256 * g + HD * h + HD]
                        for s in ((0,), (1, 2))[g]:
                            ins = mm(o, KTt[:, s, h, :], v(s, h), start=(s < 2), stop=(s != 1))
                ins.then_inc(o_done, 1)

            def turn_out(u):
                pe.wait_ge(o_scaled, u + 1)
                for k in range(2):
                    for g in range(2):
                        a = NT * k + TOK * g
                        ins = turn(ps[:, 4, a:a + TOK], tokA[:, g, P * k:P * k + P])
                ins.then_inc(o_turned, 1)

            def mla_q(g, h):
                return Q[:, g, h, :]

            def mla_k(s, h):
                return Kn[:, s, h, :]

            def mla_v(s, h):
                return KV[:, s, 128 * h + NOPE:128 * h + 128]

            def na_q(g, h):
                return tokN[:, g, HD * h:HD * h + HD]

            def na_k(s, h):
                return tokN[:, s, 256 + HD * h:256 + HD * h + HD] if s < 2 else nakc[:, HD * h:HD * h + HD]

            def na_v(s, h):
                return tokN[:, s, 512 + HD * h:512 + HD * h + HD] if s < 2 else navc[:, HD * h:HD * h + HD]

            def attention_step(l, h):
                if h == 3:
                    pe.wait_ge(qa_normed, l + 1)
                    pe.wait_ge(cache_in, 32 * (l + 1))
                    for k in range(2):
                        for g in range(2):
                            a = NT * k + TOK * g
                            turn(ps[:, 4, a:a + TOK], tokA[:, g, P * k:P * k + P])
                    for s in range(3):
                        ins = turn(ps[:, 5, TOK * s:TOK * s + TOK], tokA[:, s, 256:384] if s < 2 else ckc)
                    ins.then_inc(latent_turned, 1)
                if h == 4:
                    pe.wait_ge(latent_kept, 3 * (l + 1))
                    pe.wait_ge(small_in, 112 * (l + 1))
                    pe.wait_ge(bias_kept, l + 1)
                    for g in range(2):
                        for k in range(2):
                            mm(ps[:, 6 + g, 0:384], qaT[:, k, tok(g)], wuq[:, k, :], start=(k == 0), stop=(k == 1))
                    for s in range(2):
                        ins = mm(ps[:, 4 + s, :], ckvT[:, tok(s)], wukv[:, :], start=True, stop=True)
                    ins.then_inc(qkv_done, 1)
                if h == 5:
                    pe.wait_ge(qkv_kept, 5 * l + 4)
                    mm(ps[:, 4, :], ckvT[:, 256:384], wukv[:, :], start=True, stop=True).then_inc(qkv_done, 1)
                if h == 8:
                    pe.wait_ge(qk_ready, l + 1)
                    heads(2 * l, QK, mla_q, mla_k, True)
                if h == 9:
                    heads(2 * l, QK, mla_q, mla_k, False)
                if h == 10:
                    scores(2 * l, QK)
                if h == 12:
                    turn_probs(2 * l)
                if h == 13:
                    weigh(2 * l, mla_v)
                if h == 14:
                    turn_out(2 * l)
                if h == 15:
                    pe.wait_ge(na_ready, l + 1)
                    pe.wait_ge(o_lo, 2 * l + 1)
                    heads(2 * l + 1, HD, na_q, na_k, True)
                if h == 16:
                    pe.wait_ge(nacache_in, 32 * (l + 1))
                    heads(2 * l + 1, HD, na_q, na_k, False)
                if h == 17:
                    scores(2 * l + 1, HD)
                if h == 19:
                    turn_probs(2 * l + 1)
                if h == 20:
                    weigh(2 * l + 1, na_v)
                if h == 21:
                    turn_out(2 * l + 1)
                if h == 22:
                    pe.wait_ge(conv_ready, l + 1)
                    for tile in range(2):
                        ins = mm(ps[:, 5, 0:NT], ones[:, :], conv[:, tile, :], start=(tile == 0), stop=(tile == 1))
                    ins.then_inc(ln_sum, 1)
                if h == 23:
                    pe.wait_ge(ln_sq_done, l + 1)
                    for tile in range(2):
                        ins = mm(ps[:, 6, 0:NT], ones[:, :], ln_sq[:, NT * tile:NT * tile + NT],
                                 start=(tile == 0), stop=(tile == 1))
                    ins.then_inc(ln_sqsum, 1)

            def mixer_half(l, h):
                H = mix0[l] + h
                kind, _, i, _ = SLOTS[SLOT_OF[H][0]]
                q = SLOT_OF[H][1]
                pe.wait_ge(lo_done, H + 1)
                _, wh, wl = half(H)
                if kind in ("tok", "na_qk"):
                    n = 416 if kind == "tok" else 512
                    for g in range(2):
                        for k in range(4):
                            ins = mm3(ps[:, (2 if kind == "na_qk" else 0) + g, 0:n],
                                      hT_hi[:, 4 * q + k, tok(g)], hT_lo[:, 4 * q + k, tok(g)],
                                      wh[:, k, :], wl[:, k, :], q == 0 and k == 0, q == 1 and k == 3)
                elif kind == "na_v":
                    free_bank(l, 4)
                    for g in range(2):
                        for k in range(KT):
                            ins = mm3(ps[:, 0, 256 * g:256 * g + 256], hT_hi[:, k, tok(g)], hT_lo[:, k, tok(g)],
                                      wh[:, k, :], wl[:, k, :], k == 0, k == KT - 1)
                elif kind in ("sc", "cf", "gates"):
                    free_bank(l, h)
                    for c_ in range(2):
                        for k in range(KT):
                            a = slice(P * c_, P * c_ + P)
                            ins = mm3(ps[:, h % 4, NT * c_:NT * c_ + NT], wh[:, k, a], wl[:, k, a],
                                      hT_hi[:, k, :], hT_lo[:, k, :], k == 0, k == KT - 1)
                elif kind == "branch":
                    if h == M_BR:
                        pe.wait_ge(drained, 25 * (l + 1))
                        pe.wait_ge(b_lo, l + 1)
                        pe.wait_ge(d_lo, l + 1)
                        pe.wait_ge(o_lo, 2 * l + 2)
                    for c_ in range(2):
                        j = 2 * (h - M_BR) + c_
                        if j >= 2:
                            pe.wait_ge(proj_read, 8 * l + j - 1)
                        for n in range(4):
                            for k in range(2):
                                a = slice(P * c_, P * c_ + P)
                                ins = mm3(ps[:, 2 * c_ + n // 2, NT * (n % 2):NT * (n % 2) + NT],
                                          wh[:, 2 * n + k, a], wl[:, 2 * n + k, a],
                                          br_hi[:, 2 * n + k, :], br_lo[:, 2 * n + k, :], k == 0, k == 1)
                        if c_ == 0:
                            ins.then_inc(proj_fill, 1)
                else:
                    pe.wait_ge(merged_lo, 8 * (l + 1))
                    pe.wait_ge(proj_read, 8 * (l + 1))
                    for c_ in range(2):
                        for k in range(KT):
                            a = slice(P * c_, P * c_ + P)
                            ins = mm3(ps[:, h - M_O, NT * c_:NT * c_ + NT], wh[:, k, a], wl[:, k, a],
                                      hT_hi[:, k, :], hT_lo[:, k, :], k == 0, k == KT - 1)
                ins.then_inc(half_used, 1)

            def ff(hh):
                kind, ch = FFN[hh // 2]
                q = hh % 2
                _, wh, wl = half(ff0 + hh)
                pe.wait_ge(lo_done, ff0 + hh + 1)
                if kind == "down":
                    pe.wait_ge(ff_lo, 2 * ch + q + 1)
                    for k in range(2):
                        x = 4 * (ch % 2) + 2 * q + k
                        first, last = (ch, q, k) == (0, 0, 0), (ch, q, k) == (CHUNKS - 1, 1, 1)
                        for j in range(KT):
                            ins = mm3(ps[:, 4 + j // 2, NT * (j % 2):NT * (j % 2) + NT],
                                      wh[:, k, P * j:P * j + P], wl[:, k, P * j:P * j + P],
                                      br_hi[:, x, :], br_lo[:, x, :], first and j % 2 == 0, last, shared=True)
                else:
                    up = kind == "up"
                    if ch:
                        pe.wait_ge(ff_hid_done if up else ff_act_done, 2 * ch - 1 + q)
                    for c_ in range(2):
                        for k in range(KT):
                            a = slice(P * c_, P * c_ + P)
                            ins = mm3(ps[:, 2 * up + q, NT * c_:NT * c_ + NT], wh[:, k, a], wl[:, k, a],
                                      hT_hi[:, k, :], hT_lo[:, k, :], k == 0, k == KT - 1)
                ins.then_inc(half_used, 1)

            for l in range(DEPTH):
                ada(l)
                stat(2 * l)
                pe.wait_ge(hank_in, 64 * (l + 1))
                mm(ps[:, 6, :], consts[:, K_FLIP:K_FLIP + P], KV[:, 2, :], start=True, stop=True)\
                    .then_inc(bias_turned, 1)
                pe.wait_ge(h_lo, 4 * l + 2)
                for h in range(M_HALVES):
                    mixer_half(l, h)
                    attention_step(l, h)
                stat(2 * l + 1)
                pe.wait_ge(h_lo, 4 * l + 4)
                if l == 0:
                    for hh in range(FFN_HALVES):
                        ff(hh)

            pe.wait_ge(router_in, 16)
            for g in range(2):
                for k in range(KT):
                    ins = mm(ps[:, 0, 8 * g:8 * g + 8], hF[:, k, tok(g)], wr[:, k, :], start=(k == 0),
                             stop=(k == KT - 1))
            ins.then_inc(lg_done, 1)
            for b in range(4):
                for k in range(4 * (b % 2), 4 * (b % 2) + 4):
                    ins = turn(ps[:, 4 + b, P * (k % 4):P * (k % 4) + P], hF[:, k, tok(b // 2)])
                ins.then_inc(h2_turned, 1)
            pe.wait_ge(mask_done, 1)
            upper = consts[:, K_UP:K_UP + P]
            mm(ps[:, 1, 0:8], upper, mask[:, 0, :], start=True, stop=True)
            mm(ps[:, 1, 8:16], ones[:, :], mask[:, 0, :], start=True, stop=False)
            mm(ps[:, 1, 8:16], upper, mask[:, 1, :], start=False, stop=True)
            mm(ps[:, 1, 16:24], ones[:, :], mask[:, 0, :], start=True, stop=False)
            mm(ps[:, 1, 16:24], ones[:, :], mask[:, 1, :], start=False, stop=True).then_inc(pos_done, 1)

            pe.wait_ge(h2_kept, 4)
            pe.wait_ge(tab_done, 1)
            n_items = pe.value_load(itab[0:1, 0:1], min_val=NEXP, max_val=ITEMS)
            xe_h = hT_hi[:, 0:4, :].rearrange("p a (b s) -> p (a b) s", b=2)
            xe_l = hT_lo[:, 0:4, :].rearrange("p a (b s) -> p (a b) s", b=2)
            hd_h = br_hi[:, 0:2, :].rearrange("p a (b s) -> p (a b) s", b=2)
            hd_l = br_lo[:, 0:2, :].rearrange("p a (b s) -> p (a b) s", b=2)
            with pe.Fori(0, n_items) as i:
                pe.wait_ge(sel_done, i + 1)
                for t in range(2):
                    ins = turn(ps[:, 7, TOK * t:TOK * t + TOK], selg[:, t, :])
                ins.then_inc(selT_t, 1)
                for k in range(KT):
                    for t in range(2):
                        ins = mm(ps[:, 5 + k // 4, P * (k % 4):P * (k % 4) + P], h2tok[:, t, P * k:P * k + P],
                                 sel[:, t, :], start=(t == 0), stop=(t == 1))
                ins.then_inc(xe_t, 1)
                pe.wait_ge(xe_lo, i + 1)
                for hh in range(FFN_HALVES):
                    kind, ch = FFN[hh // 2]
                    q = hh % 2
                    _, wh, wl = item_half(hh)
                    if kind == "down":
                        pe.wait_ge(e_lo, i * CHUNKS + (ch + 1))
                    pe.wait_ge(lo_done, i * FFN_HALVES + (HALVES + hh + 1))
                    if kind == "down":
                        for k in range(2):
                            for n in range(2):
                                c_ = slice(512 * n, 512 * n + 512)
                                ins = mm3(ps[:, 3 + n, :], hd_h[:, 2 * q + k, :], hd_l[:, 2 * q + k, :],
                                          wh[:, k, c_], wl[:, k, c_], (ch, q, k) == (0, 0, 0),
                                          (ch, q, k) == (CHUNKS - 1, 1, 1))
                    else:
                        for k in range(4):
                            ins = mm3(ps[:, 1 if kind == "up" else 0, :], xe_h[:, 4 * q + k, :],
                                      xe_l[:, 4 * q + k, :], wh[:, k, :], wl[:, k, :], (q, k) == (0, 0),
                                      (q, k) == (1, 3))
                    ins.then_inc(half_used, 1)
                    if (kind == "down" and q and ch < CHUNKS - 1) or (kind == "up" and q and ch == 0):
                        t = 0 if kind == "up" else ch + 1
                        pe.wait_ge(e_hid, i * CHUNKS + (t + 1))
                        for k in range(4):
                            ins = turn(ps[:, 2, P * k:P * k + P], ff_hid[:, 0, P * k:P * k + P])
                        ins.then_inc(e_turn, 1)
                pe.wait_ge(y_kept, i + 1)
                pe.wait_ge(selT_kept, i + 1)
                for r, bank in enumerate((5, 6, 7, 2)):
                    for jj in range(2):
                        j = 2 * r + jj
                        ins = mm(ps[:, bank, NT * jj:NT * jj + NT], y_tok[:, P * j:P * j + P], selT, start=True,
                                 stop=True)
                    ins.then_inc(sc_fill, 1)

            pe.wait_ge(moe_done, 1)
            for b in range(4):
                for k in range(4 * (b % 2), 4 * (b % 2) + 4):
                    ins = turn(ps[:, b, P * (k % 4):P * (k % 4) + P], xT[:, k, tok(b // 2)])
                ins.then_inc(fin_t, 1)


_INS = ['x_prompt', 'x_sample', 'cache_mla_ckv', 'cache_mla_kpe', 'cache_na_k', 'cache_na_v', 'c', 'c_ctx',
        'w_ada', 'b_ada', 'g_norm1', 'w_in', 'g_qa', 'w_uq', 'g_kva', 'w_ukv', 'g_mla_q', 'g_mla_k', 'sc_w',
        'g_na_q', 'g_na_k', 'na_rpb', 'cf_w', 'cf_b', 'cf_ln_g', 'cf_ln_b', 'w_br', 'w_o', 'g_norm2',
        'w_ff_gate', 'w_ff_up', 'w_ff_down', 'w_router', 'w_e_gate', 'w_e_up', 'w_e_down']
_OUTS = [(1, 128, 1024), (1, 128, 1024), (1, 2, 128, 128), (1, 2, 128, 32), (1, 2, 128, 4, 64), (1, 2, 128, 4, 64)]


def shape_constants():
    import numpy as np
    k = np.zeros((P, K_COLS), np.float32)
    n = np.arange(P)
    k[:, K_ID:K_ID + P] = np.eye(P)
    k[:, K_UP:K_UP + P] = n[:, None] < n[None, :]
    k[:, K_IOTA:K_IOTA + P] = n[None, :]
    cq = n % GRID_W
    start = np.clip(cq - 8, 0, GRID_W - 16)
    ok = (cq[None, :] >= start[:, None]) & (cq[None, :] < start[:, None] + 16)
    k[:, K_MASK:K_MASK + P] = np.where(ok, 0.0, -1e30)
    k[n, K_FLIP + (n // 64) * 64 + 63 - cq] = 1.0
    inv = np.float32(10000.0) ** (-np.arange(8, dtype=np.float32) / np.float32(8))
    for a, pos in enumerate((n // GRID_W, n % GRID_W)):
        ang = pos.astype(np.float32)[:, None] * inv[None, :]
        k[:, K_COS + 8 * a:K_COS + 8 * a + 8] = np.cos(ang)
        k[:, K_SIN + 8 * a:K_SIN + 8 * a + 8] = np.sin(ang)
    k[0:4, K_FOLD:K_FOLD + 2] = np.array([[1, 0], [0, 1], [1, 0], [0, 1]])
    e = np.arange(8)
    k[:, K_BEFORE:K_BEFORE + 64] = (e[None, :] < e[:, None]).reshape(1, 64)
    k[:, K_EXP:K_EXP + 8] = e
    k[:, K_LEFT:K_LEFT + 8] = 8 - e
    return k


def kernel(**inputs):
    import numpy as _np
    import concourse.bacc as _bacc
    from concourse import mybir as _mybir
    from concourse.bass_utils import run_bass_kernel_spmd as _run

    nc = _bacc.Bacc("TRN2", target_bir_lowering=False, num_devices=1)
    arrays, args = {}, []
    for name in _INS + ["shape_consts"]:
        a = shape_constants() if name == "shape_consts" else _np.ascontiguousarray(inputs[name])
        arrays[f"in_{name}_dram"] = a
        args.append(nc.dram_tensor(f"in_{name}_dram", a.shape, _mybir.dt.from_np(a.dtype), kind="ExternalInput").ap())
    for i, shape in enumerate(_OUTS):
        dt = _mybir.dt.from_np(_np.dtype("float32"))
        args.append(nc.dram_tensor(f"out_{i}_dram", shape, dt, kind="ExternalOutput").ap())
    build(nc, *args)
    r = _run(nc, [arrays], core_ids=[0])
    return tuple(r.results[0][f"out_{i}_dram"] for i in range(len(_OUTS)))
```

```python
import concourse.bass as bass
from concourse import mybir
from contextlib import ExitStack

F32 = mybir.dt.float32
F32R = mybir.dt.float32r
I32 = mybir.dt.int32
ALU = mybir.AluOpType
ACT = mybir.ActivationFunctionType
AX = mybir.AxisListType

P = 128
D = 1024
KT = D // P
TOK = 128
NT = 2 * TOK
DEPTH = 2
GRID_W = 64
HEADS = 4
QL, KVL, ROPE, NOPE = 256, 128, 32, 64
QK = NOPE + ROPE
HD = 64
BW = 256
CFK, SCK = 31, 3
DFF = 3584
CHUNKS = DFF // 512
NEXP = 8
CAP = 128
OVER = 512 // (CAP + 1)
ITEMS = NEXP + OVER
EPS = 1e-6
RAW = 3
HALF = 2048
PIECE = HALF // 2
PIECES = 4

C_QA, C_SC, C_NA, C_CF, C_GATE = 0, 416, 1184, 1952, 2464

V_N1, V_N2, V_QA, V_CFB, V_LNG, V_LNB, V_SC, V_CF = 0, 8, 16, 18, 20, 22, 24, 30
V_ROWS = V_CF + 2 * CFK

K_ID, K_UP, K_IOTA, K_MASK, K_FLIP = 0, 128, 256, 384, 512
K_COS, K_SIN, K_FOLD, K_BEFORE, K_EXP, K_LEFT = 640, 656, 672, 674, 738, 746
K_COLS = 754

M_TOK, M_SC, M_CF, M_GATE, M_BR, M_O, M_HALVES = 0, 5, 8, 10, 26, 30, 34


def ffn_order():
    order = []
    for c in range(CHUNKS):
        order += [("gate", c), ("up", c)]
        if c:
            order.append(("down", c - 1))
    order.append(("down", CHUNKS - 1))
    return order


FFN = ffn_order()
FFN_HALVES = 2 * len(FFN)
FFN_PIECES = 2 * FFN_HALVES
I_SCATTER = {2: [(0, 5), (1, 6)], 4: [(2, 7), (3, 5)]}
I_TURN = 6
I_SELECT = 20
I_GATHER = 2 * FFN.index(("up", CHUNKS - 1)) + 1


def plan_slots():
    slots = []
    for l in range(DEPTH):
        slots += [("ada", l, c, 2) for c in range(12)]
        slots += [("tok", l, 0, 2), ("na_qk", l, 0, 2), ("na_v", l, 0, 1),
                  ("sc", l, 0, 2), ("sc", l, 1, 1), ("cf", l, 0, 2)]
        slots += [("gates", l, c, 2) for c in range(8)]
        slots += [("branch", l, c, 2) for c in range(2)] + [("out", l, c, 2) for c in range(2)]
        if l == 0:
            slots += [(kind, 0, c, 2) for kind, c in FFN]
    return slots


SLOTS = plan_slots()
SLOT_OF = []
FIRST_HALF = []
for _s, _slot in enumerate(SLOTS):
    FIRST_HALF.append(len(SLOT_OF))
    SLOT_OF += [(_s, _h) for _h in range(_slot[3])]
HALVES = len(SLOT_OF)
PHASE = {(k, l): min(s for s, x in enumerate(SLOTS) if x[0] == k and x[1] == l) for k, l, _, _ in SLOTS}


def first_half(kind, layer):
    return FIRST_HALF[PHASE[(kind, layer)]]


def build(nc, x_prompt, x_sample, cache_mla_ckv, cache_mla_kpe, cache_na_k, cache_na_v, c, c_ctx,
          w_ada, b_ada, g_norm1, w_in, g_qa, w_uq, g_kva, w_ukv, g_mla_q, g_mla_k, sc_w,
          g_na_q, g_na_k, na_rpb, cf_w, cf_b, cf_ln_g, cf_ln_b, w_br, w_o, g_norm2,
          w_ff_gate, w_ff_up, w_ff_down, w_router, w_e_gate, w_e_up, w_e_down, shape_consts,
          y_prompt, y_sample, new_ckv, new_kpe, new_na_k, new_na_v):
    with ExitStack() as ctx:
        def sb(name, shape, dt=F32):
            return ctx.enter_context(nc.sbuf_tensor(name, shape, dt))

        def sem(name):
            return ctx.enter_context(nc.semaphore(name))

        raw = sb("raw", [P, RAW, 2 * HALF])
        whi = sb("whi", [P, PIECES, PIECE], F32R)
        wlo = sb("wlo", [P, PIECES, PIECE], F32R)
        hT_hi = sb("hT_hi", [P, KT, NT], F32R)
        hT_lo = sb("hT_lo", [P, KT, NT], F32R)
        br_hi = sb("br_hi", [P, 8, NT], F32R)
        br_lo = sb("br_lo", [P, 8, NT], F32R)
        xT = sb("xT", [P, KT, NT])
        big = sb("big", [P, 8192])
        tokA = sb("tokA", [P, 2, 416])
        tokN = sb("tokN", [P, 2, 768])
        qk = sb("qk", [P, 1920])
        KV = sb("KV", [P, 3, 512])
        QT = sb("QT", [P, 2, HEADS, TOK])
        KTt = sb("KTt", [P, 3, HEADS, TOK])
        bias = sb("bias", [P, HEADS, TOK])
        consts = sb("consts", [P, K_COLS])
        ones = sb("ones", [P, P])
        wuq = sb("wuq", [P, 2, 384])
        wukv = sb("wukv", [P, 512])
        vrow = sb("vrow", [P, P])
        vecT = sb("vecT", [P, DEPTH, V_ROWS])
        badaT = sb("badaT", [P, DEPTH, 48])
        modT = sb("modT", [P, 48, 2])
        scaleT = sb("scaleT", [P, 2, KT, 2])
        gkv_b = sb("gkv_b", [P, KVL])
        gq_b = sb("gq_b", [P, QK])
        gk_b = sb("gk_b", [P, QK])
        gnq_b = sb("gnq_b", [P, HD])
        gnk_b = sb("gnk_b", [P, HD])
        scpad = sb("scpad", [P, 2, 2, TOK + 2])
        cfpad = sb("cfpad", [P, 2, 2, TOK + 30])
        conv = sb("conv", [P, 2, NT])
        small = sb("small", [P, 192])
        cond_hl = sb("cond_hl", [P, KT, 4], F32R)
        itab = sb("itab", [1, 16], I32)
        minus_half = sb("minus_half", [P, 1])
        ps = ctx.enter_context(nc.psum_tensor("ps", [P, 8, 512], F32))

        ident = consts[:, K_ID:K_ID + P]

        sq = big[:, 0:2048].rearrange("p (k t) -> p k t", k=KT)
        hF = big[:, 2048:4096].rearrange("p (k t) -> p k t", k=KT)
        xtok = big[:, 0:2048].rearrange("p (g d) -> p g d", g=2)
        rstd = big[:, 4096:4352]
        gates = big[:, :].rearrange("p (n j t) -> p n j t", n=4, j=8)
        bc = big[:, 6144:7168].rearrange("p (b t) -> p b t", b=4)
        cf = big[:, 7168:8192].rearrange("p (b t) -> p b t", b=4)
        ff_act = big[:, 0:1024].rearrange("p (b n) -> p b n", b=2)
        ff_hid = big[:, 1024:2048].rearrange("p (b n) -> p b n", b=2)
        h2tok = big[:, 4096:6144].rearrange("p (g d) -> p g d", g=2)
        fT = big[:, 6144:8192].rearrange("p (k t) -> p k t", k=KT)
        y_tok = big[:, 2048:3072]
        sel = big[:, 3072:3328].rearrange("p (t s) -> p t s", t=2)
        selg = big[:, 3328:3584].rearrange("p (t s) -> p t s", t=2)
        selT = big[:, 3584:3840]
        arow = tokN[0:4, :, :].rearrange("p g n -> p (g n)")[:, 0:1024].rearrange("p (a n) -> p a n", a=2)
        Q = qk[:, 0:768].rearrange("p (g h d) -> p g h d", g=2, h=HEADS)
        Kn = qk[:, 768:1920].rearrange("p (s h d) -> p s h d", s=3, h=HEADS)
        heads_sq = qk[:, 768:1536]
        Pr = qk[:, 0:1536].rearrange("p (s h d) -> p s h d", s=3, h=HEADS)
        QTf = QT[:, :, :, :].rearrange("p g h t -> p (g h t)")
        KTf = KTt[:, :, :, :].rearrange("p s h t -> p (s h t)")
        qaT = QTf[:, 0:512].rearrange("p (a t) -> p a t", a=2)
        ckvT = KTf[:, 0:384]
        sbias = KV[:, 0, :]
        O = tokA[:, :, 0:256]
        ckc = qk[:, 1536:1664]
        kpc = small[:, 128:160]
        nakc = KV[:, 1, 0:256]
        navc = KV[:, 1, 256:512]
        ropet = big[:, 1024:1536].rearrange("p (a n) -> p a n", a=8)
        hank = KV[:, 2, :].rearrange("p (h k) -> p h k", h=HEADS)
        na_sq = big[:, 0:1024].rearrange("p (g d) -> p g d", g=2)
        ln_sq = QTf[:, 0:512]
        ln_sd = QTf[:, 512:768]
        wr = qk[:, 0:64].rearrange("p (k e) -> p k e", k=KT)
        lg = qk[:, 64:80].rearrange("p (g e) -> p g e", g=2)
        lg2 = qk[:, 80:96].rearrange("p (g e) -> p g e", g=2)
        oh1 = qk[:, 96:112].rearrange("p (g e) -> p g e", g=2)
        oh2 = qk[:, 112:128].rearrange("p (g e) -> p g e", g=2)
        tmp = qk[:, 128:144].rearrange("p (g e) -> p g e", g=2)
        tq = qk[:, 144:160]
        ov = qk[:, 168:176]
        rank = qk[:, 176:184]
        mask = qk[:, 1010:1026].rearrange("p (g e) -> p g e", g=2)
        ohk = qk[:, 184:184 + 8 * OVER].rearrange("p (k e) -> p k e", k=OVER)
        w64 = qk[:, 300:364].rearrange("p (a e) -> p a e", a=8)
        tab = qk[:, 400:400 + 6 * (ITEMS + 1)].rearrange("p (q t i) -> p q t i", q=3, t=2)
        wide = qk[:, 600:600 + 16 * OVER].rearrange("p (t k e) -> p t k e", t=2, k=OVER)
        eidx = qk[:, 900:900 + OVER + 2]
        stage = qk[:, 1000:1006].rearrange("p (q t) -> p q t", q=3)

        raw_landed = [sem(f"raw_landed{i}") for i in range(RAW)]
        (hi_piece, lo_piece, piece_used, consts_in, x_in, cond_in, vrow_in, small_in,          nacache_in, cache_in, router_in, setup, pool_pow, dve_link, cond_turned, cond_th, cond_ready, cond_hi,
         cond_lo, v_turned, v_kept, x_turned, x_kept, ada_kept, ada_folded, mod_done,
         sq_done, stat_done, ms_done, sd_done, hF_done, h_hi, h_lo, drained, xv_read, 
         proj_read, merged_f, merged_hi, merged_lo, wo_read) = map(sem, (
             "hi_piece lo_piece piece_used consts_in x_in cond_in vrow_in small_in "
             "nacache_in cache_in router_in setup pool_pow dve_link cond_turned cond_th cond_ready cond_hi "
             "cond_lo v_turned v_kept x_turned x_kept ada_kept ada_folded mod_done "
             "sq_done stat_done ms_done sd_done hF_done h_hi h_lo drained xv_read  "
             "proj_read merged_f merged_hi merged_lo wo_read").split())
        (stats_in, qa_normed, na_ready, hank_in, bias_turned, bias_kept, latent_turned, latent_kept,
         qkv_done, qkv_kept, qk_ready, heads_turned, heads_kept, scores_done, max_done, exp_done,
         probs_turned, probs_kept, o_done, o_scaled, o_turned, o_hi, o_lo, b_ready, b_hi, b_lo, cf_used,
         conv_v, conv_ready, ln_sum, ln_sq_done, ln_sqsum, ln_ms, ln_sdone, ln_z, ln_th, ln_o, d_hi, d_lo,
         stored) = map(sem, (
             "stats_in qa_normed na_ready hank_in bias_turned bias_kept latent_turned latent_kept "
             "qkv_done qkv_kept qk_ready heads_turned heads_kept scores_done max_done exp_done "
             "probs_turned probs_kept o_done o_scaled o_turned o_hi o_lo b_ready b_hi b_lo cf_used "
             "conv_v conv_ready ln_sum ln_sq_done ln_sqsum ln_ms ln_sdone ln_z ln_th ln_o d_hi d_lo "
             "stored").split())
        (ff_act_done, ff_hid_done, ff_hi, ff_lo, ff_read, lg_done, h2_turned, h2_kept,
         mask_done, pos_done, tab_done, staged, sel_done, selT_t, selT_kept, xe_t, xe_hi, xe_lo,          e_act, e_hid, e_turn, e_hi, e_lo, y_kept, sc_fill, moe_done, fin_t, fin_kept, pair_exp, item_added, y_cleared, y_stored) = map(sem, (
             "ff_act_done ff_hid_done ff_hi ff_lo ff_read lg_done h2_turned h2_kept "
             "mask_done pos_done tab_done staged sel_done selT_t selT_kept xe_t xe_hi xe_lo "
             "e_act e_hid e_turn e_hi e_lo y_kept sc_fill moe_done fin_t fin_kept pair_exp item_added y_cleared y_stored").split())

        def cols(w, l, a, n):
            return w[l, :, a:a + n].rearrange("(k p) n -> p k n", p=P)

        def slot_parts(kind, l, i):
            if kind == "ada":
                return (8, 512), cols(w_ada, l, 512 * i, 512)
            if kind == "tok":
                return (8, 416), cols(w_in, l, C_QA, 416)
            if kind == "na_qk":
                return (8, 512), cols(w_in, l, C_NA, 512)
            if kind == "na_v":
                return (8, 256), cols(w_in, l, C_NA + 512, 256)
            if kind == "sc":
                return (8, 256 if i else 512), cols(w_in, l, C_SC + 512 * i, 256 if i else 512)
            if kind == "cf":
                return (8, 512), cols(w_in, l, C_CF, 512)
            if kind == "gates":
                return (8, 512), cols(w_in, l, C_GATE + 512 * i, 512)
            if kind == "branch":
                return (8, 512), w_br[l].rearrange("n (k p) d -> p (n k) d", p=P)[:, :, 512 * i:512 * i + 512]
            if kind == "out":
                return (8, 512), cols(w_o, l, 512 * i, 512)
            if kind == "gate":
                return (8, 512), cols(w_ff_gate, 0, 512 * i, 512)
            if kind == "up":
                return (8, 512), cols(w_ff_up, 0, 512 * i, 512)
            return (4, 1024), w_ff_down[0, 512 * i:512 * i + 512, :].rearrange("(k p) n -> p k n", p=P)

        def piece_views(kind, i, h, c_, raw_slot, buf, item=False):
            width = {"tok": 416, "na_v": 256, "down": 1024}.get(kind, 256 if kind == "sc" and i else 512)
            depth = 4 if kind == "down" else 8
            whole = raw[:, raw_slot, 0:depth * width].rearrange("p (k n) -> p k n", k=depth)
            n = 2 * h + c_
            if kind == "down":
                k, w, part = 1, 1024, whole[:, n:n + 1, :]
            elif kind in ("ada", "tok", "na_qk") or item:
                k, w, part = 2, width, whole[:, 2 * n:2 * n + 2, :]
            else:
                k, w, part = 8, P, whole[:, :, P * n:P * n + P]
            return (part,) + tuple(x[:, buf, 0:k * w].rearrange("p (k n) -> p k n", k=k) for x in (whi, wlo))

        def piece(H, c_):
            s, h = SLOT_OF[H]
            kind, _, i, _ = SLOTS[s]
            return piece_views(kind, i, h, c_, s % RAW, (2 * H + c_) % PIECES)

        def item_piece(hh, c_):
            kind, _ = FFN[hh // 2]
            return piece_views(kind, 0, hh % 2, c_, (len(SLOTS) + hh // 2) % RAW,
                               (2 * (HALVES + hh) + c_) % PIECES, item=True)

        ada0 = {l: first_half("ada", l) for l in range(DEPTH)}
        mix0 = {l: first_half("tok", l) for l in range(DEPTH)}
        ff0 = first_half("gate", 0)

        def filled(l, f):
            return 2 * (mix0[l] + (2 if f < 2 else 4 if f < 4 else f + 1))

        def ff_used(kind, ch):
            return 2 * (ff0 + 2 * FFN.index((kind, ch)) + 2)

        block = ctx.enter_context(nc.Block())

        @block.sync
        def _(sp):
            for s, (kind, l, i, n) in enumerate(SLOTS):
                (k, w), src = slot_parts(kind, l, i)
                if s >= RAW:
                    sp.wait_ge(lo_piece, 2 * (FIRST_HALF[s - RAW] + SLOTS[s - RAW][3]))
                dst = raw[:, s % RAW, 0:k * w].rearrange("p (k n) -> p k n", k=k)
                sp.dma_start(dst, src).then_inc(raw_landed[s % RAW], 16)

            def item_loads(e, done):
                for j, (kind, ch) in enumerate(FFN):
                    if kind == "down":
                        src = w_e_down[0, bass.ds(e, 1), 512 * ch:512 * ch + 512, :].rearrange(
                            "a (k p) n -> p (a k) n", p=P)
                        k = 4
                    else:
                        w = w_e_gate if kind == "gate" else w_e_up
                        src = w[0, bass.ds(e, 1), :, 512 * ch:512 * ch + 512].rearrange(
                            "a (k p) n -> p (a k) n", p=P)
                        k = 8
                    slot = (len(SLOTS) + j) % RAW
                    sp.wait_ge(lo_piece, done + 2 * (HALVES + 2 * (j - RAW + 1)))
                    sp.dma_start(raw[:, slot, :].rearrange("p (k n) -> p k n", k=k), src)\
                        .then_inc(raw_landed[slot], 16)

            with sp.Fori(0, NEXP) as i:
                item_loads(i, i * FFN_PIECES)
            sp.wait_ge(tab_done, 1)
            n_over = sp.value_load(itab[0:1, 1:2], min_val=0, max_val=OVER)
            with sp.If(n_over > 0):
                with sp.Fori(0, n_over) as j:
                    e = sp.value_load(itab[0:1, bass.ds(j + 2, 1)], min_val=0, max_val=NEXP - 1)
                    item_loads(e, (j + NEXP) * FFN_PIECES)
            sp.wait_ge(fin_kept, 4)
            sp.dma_start(y_prompt[0], xtok[:, 0, :]).then_inc(y_stored, 16)
            sp.dma_start(y_sample[0], xtok[:, 1, :]).then_inc(y_stored, 16)
            sp.wait_ge(y_stored, 32)
            sp.wait_ge(stored, 64 * DEPTH)

        @block.gpsimd
        def _(pool):
            pool.dma_start(consts[:, :], shape_consts).then_inc(consts_in, 16)
            pool.dma_start(vrow[0:8, :], c_ctx.rearrange("(k p) -> k p", p=P)).then_inc(cond_in, 16)
            pool.dma_start(vrow[8:16, :], c[0].rearrange("(k p) -> k p", p=P)).then_inc(cond_in, 16)
            pool.dma_start(xtok[:, 0, :], x_prompt[0]).then_inc(x_in, 16)
            pool.dma_start(xtok[:, 1, :], x_sample[0]).then_inc(x_in, 16)
            pool.memset(ones[:, :], 1.0).then_inc(setup, 1)
            pool.memset(minus_half[:, :], -0.5).then_inc(setup, 1)
            pool.memset(scpad[:, :, :, :], 0.0).then_inc(setup, 1)
            pool.memset(cfpad[:, :, :, :], 0.0).then_inc(setup, 1)

            for l in range(DEPTH):
                if l:
                    pool.wait_ge(v_turned, 2)
                else:
                    pool.wait_ge(cond_turned, 1)
                for src, at, n in ((g_norm1[l], V_N1, 8), (g_norm2[l], V_N2, 8), (g_qa[l], V_QA, 2),
                                   (cf_b[l], V_CFB, 2), (cf_ln_g[l], V_LNG, 2), (cf_ln_b[l], V_LNB, 2)):
                    pool.dma_start(vrow[at:at + n, :], src.rearrange("(k p) -> k p", p=P)).then_inc(vrow_in, 16)
                pool.dma_start(vrow[V_SC:V_SC + 2 * SCK, :], sc_w[l].rearrange("a (k p) -> (a k) p", p=P))\
                    .then_inc(vrow_in, 16)
                pool.dma_start(vrow[V_CF:V_ROWS, :], cf_w[l].rearrange("a (k p) -> (a k) p", p=P))\
                    .then_inc(vrow_in, 16)
                pool.wait_ge(v_turned, 2 * l + 1)
                pool.dma_start(vrow[0:48, :], b_ada[l].rearrange("(k p) -> k p", p=P)).then_inc(vrow_in, 16)

            for l in range(DEPTH):
                if l:
                    pool.wait_ge(piece_used, 2 * (mix0[l - 1] + M_HALVES))
                for dst, src in ((wuq[:, :, :], w_uq[l].rearrange("(k p) n -> p k n", p=P)),
                                 (wukv[:, :], w_ukv[l]),
                                 (gkv_b[:, :], g_kva[l].partition_broadcast(P)),
                                 (gq_b[:, :], g_mla_q[l].partition_broadcast(P)),
                                 (gk_b[:, :], g_mla_k[l].partition_broadcast(P)),
                                 (gnq_b[:, :], g_na_q[l].partition_broadcast(P)),
                                 (gnk_b[:, :], g_na_k[l].partition_broadcast(P))):
                    pool.dma_start(dst, src).then_inc(small_in, 16)
                pool.dma_start(ckc, cache_mla_ckv[0, l]).then_inc(cache_in, 16)
                pool.dma_start(kpc, cache_mla_kpe[0, l]).then_inc(cache_in, 16)
                for rq in range(2):
                    for rk in range(2):
                        src = bass.AP(na_rpb.tensor, l * 1860 + (rk - rq + 7) * 31 + 15 - (GRID_W - 1),
                                      [[1, GRID_W], [465, HEADS], [1, GRID_W]])
                        pool.dma_start(hank[rq * 64:rq * 64 + 64, :, rk * 64:rk * 64 + 64], src)\
                            .then_inc(hank_in, 16)
                if l == 0:
                    pool.wait_ge(setup, 2)
                pool.wait_ge(stats_in, 3 * l + 1)
                pool.tensor_tensor(small[:, 0:4], small[:, 0:4], minus_half[:, :].to_broadcast([P, 4]),
                                   ALU.pow).then_inc(pool_pow, 1)
                pool.wait_ge(qa_normed, l + 1)
                pool.dma_start(new_ckv[0, l], tokA[:, 0, 256:384]).then_inc(stored, 16)
                pool.dma_start(new_kpe[0, l], tokA[:, 0, 384:416]).then_inc(stored, 16)
                pool.wait_ge(stats_in, 3 * l + 2)
                pool.tensor_tensor(small[:, 8:28], small[:, 8:28], minus_half[:, :].to_broadcast([P, 20]),
                                   ALU.pow).then_inc(pool_pow, 1)
                pool.wait_ge(stats_in, 3 * l + 3)
                pool.tensor_tensor(small[:, 32:48], small[:, 32:48], minus_half[:, :].to_broadcast([P, 16]),
                                   ALU.pow).then_inc(pool_pow, 1)
                pool.wait_ge(na_ready, l + 1)
                pool.dma_start(new_na_k[0, l].rearrange("s h d -> s (h d)"), tokN[:, 0, 256:512])\
                    .then_inc(stored, 16)
                pool.dma_start(new_na_v[0, l].rearrange("s h d -> s (h d)"), tokN[:, 0, 512:768])\
                    .then_inc(stored, 16)
                pool.wait_ge(o_done, 2 * l + 1)
                pool.dma_start(nakc, cache_na_k[0, l].rearrange("s h d -> s (h d)")).then_inc(nacache_in, 16)
                pool.dma_start(navc, cache_na_v[0, l].rearrange("s h d -> s (h d)")).then_inc(nacache_in, 16)
            pool.wait_ge(piece_used, 2 * (mix0[DEPTH - 1] + M_HALVES))
            pool.dma_start(wr, w_router[0].rearrange("(k p) e -> p k e", p=P)).then_inc(router_in, 16)

        @block.scalar
        def _(act):
            def flat2(a):
                return a.rearrange("p a b -> p (a b)")

            def flat3(a):
                return a.rearrange("p a b c -> p (a b c)")

            def hi(H):
                s, _ = SLOT_OF[H]
                act.wait_ge(raw_landed[s % RAW], 16 * (s // RAW + 1))
                for c_ in range(2):
                    part, h, _ = piece(H, c_)
                    if 2 * H + c_ >= PIECES:
                        act.wait_ge(piece_used, 2 * H + c_ - PIECES + 1)
                    act.activation(h, part, ACT.Copy).then_inc(hi_piece, 1)

            act.wait_ge(cond_turned, 1)
            act.activation(small[:, 64:80], ps[:, 7, 0:16], ACT.Tanh, scale=0.5).then_inc(cond_th, 1)
            act.wait_ge(cond_ready, 1)
            act.activation(cond_hl[:, :, 0:2], small[:, 80:96].rearrange("p (g k) -> p k g", g=2), ACT.Copy)\
                .then_inc(cond_hi, 1)
            for b in range(4):
                act.wait_ge(x_turned, b + 1)
                act.activation(flat2(xT[:, 2 * b:2 * b + 2, :]), ps[:, b, :], ACT.Copy).then_inc(x_kept, 1)

            def norm(n):
                if n == 0:
                    act.wait_ge(x_kept, 4)
                elif n == 2:
                    act.wait_ge(ff_read, 1)
                else:
                    act.wait_ge(wo_read, 4 * (n // 2 + 1))
                act.activation(sq, xT[:, :, :], ACT.Square).then_inc(sq_done, 1)
                act.wait_ge(ms_done, n + 1)
                act.activation(rstd, rstd, ACT.Sqrt).then_inc(sd_done, 1)
                for k in range(2):
                    act.wait_ge(hF_done, 2 * n + k + 1)
                    act.activation(hT_hi[:, 4 * k:4 * k + 4, :], hF[:, 4 * k:4 * k + 4, :], ACT.Copy)\
                        .then_inc(h_hi, 1)

            def evac(l, f, dst, func=ACT.Copy, n=512, scale=1.0):
                act.wait_ge(piece_used, filled(l, f))
                act.activation(dst, ps[:, f % 4, 0:n], func, scale=scale).then_inc(drained, 1)

            def keep_heads(u, d, first):
                act.wait_ge(heads_turned, 2 * u + (1 if first else 2))
                if first:
                    for g in range(2):
                        act.activation(QTf[0:d, 512 * g:512 * g + 512], ps[0:d, 4 + g, :], ACT.Copy)\
                            .then_inc(heads_kept, 1)
                    for s in range(2):
                        act.activation(KTf[0:d, 512 * s:512 * s + 512], ps[0:d, 6 + s, :], ACT.Copy)\
                            .then_inc(heads_kept, 1)
                else:
                    act.activation(KTf[0:d, 1024:1536], ps[0:d, 4, :], ACT.Copy).then_inc(heads_kept, 1)

            def exps(u, scale):
                act.wait_ge(max_done, u + 1)
                for s in range(3):
                    for h in range(HEADS):
                        b = HEADS * s + h
                        src = sbias[:, TOK * h:TOK * h + TOK] if u % 2 and s == 1 else \
                            ps[:, 5 + s, TOK * h:TOK * h + TOK]
                        act.activation(Pr[:, s, h, :], src, ACT.Exp, bias=small[:, 60 + b:61 + b], scale=scale,
                                       accum_out=small[:, 76 + b:77 + b]).then_inc(exp_done, 1)

            def keep_probs(u):
                act.wait_ge(probs_turned, u + 1)
                for s in range(3):
                    act.activation(KTf[:, 512 * s:512 * s + 512], ps[:, 5 + s, :], ACT.Copy)\
                        .then_inc(probs_kept, 1)

            def out_hi(u):
                act.wait_ge(o_turned, u + 1)
                act.activation(flat2(br_hi[:, 4 * (u % 2):4 * (u % 2) + 2, :]), ps[:, 4, :], ACT.Copy)\
                    .then_inc(o_hi, 1)

            def mixer_task(l, h):
                if h == 1:
                    for g in range(2):
                        evac(l, g, tokA[:, g, :], n=416)
                if h == 3:
                    for g in range(2):
                        evac(l, 2 + g, tokN[:, g, 0:512])
                    act.wait_ge(latent_turned, l + 1)
                    for k in range(2):
                        act.activation(qaT[:, k, :], ps[:, 4, 256 * k:256 * k + 256], ACT.Copy,
                                       scale=vecT[:, l, V_QA + k:V_QA + k + 1]).then_inc(latent_kept, 1)
                    act.activation(ckvT, ps[:, 5, 0:384], ACT.Copy).then_inc(latent_kept, 1)
                if h == 4:
                    evac(l, 4, tokN[:, :, 512:768])
                    act.wait_ge(qkv_done, 2 * l + 1)
                    for g in range(2):
                        act.activation(qk[:, 384 * g:384 * g + 384], ps[:, 6 + g, 0:384], ACT.Copy)\
                            .then_inc(qkv_kept, 1)
                    for s in range(2):
                        act.activation(KV[:, s, :], ps[:, 4 + s, :], ACT.Copy).then_inc(qkv_kept, 1)
                if h == 5:
                    act.wait_ge(qkv_done, 2 * l + 2)
                    act.activation(KV[:, 2, :], ps[:, 4, :], ACT.Copy).then_inc(qkv_kept, 1)
                if h in (5, 6):
                    evac(l, h, flat2(bc[:, 2 * (h - 5):2 * (h - 5) + 2, :]))
                if h == 8:
                    evac(l, 8, flat2(cf[:, 0:2, :]))
                    keep_heads(2 * l, QK, True)
                if h == 9:
                    evac(l, 9, flat2(cf[:, 2:4, :]), ACT.Tanh, scale=0.5)
                    keep_heads(2 * l, QK, False)
                if M_GATE <= h < M_BR:
                    n, j = divmod(2 * (h - M_GATE), 8)
                    if h == M_GATE:
                        act.wait_ge(stats_in, 3 * l + 3)
                    if h == M_GATE + 12:
                        act.wait_ge(b_lo, l + 1)
                        act.wait_ge(cf_used, l + 1)
                    evac(l, h, flat2(gates[:, n, j:j + 2, :]), ACT.Tanh, scale=0.5)
                if h == 11:
                    exps(2 * l, QK ** -0.5)
                if h == 12:
                    keep_probs(2 * l)
                    act.wait_ge(b_ready, l + 1)
                    act.activation(br_hi[:, 2:4, :], bc[:, 0:2, :], ACT.Copy).then_inc(b_hi, 1)
                if h == 14:
                    out_hi(2 * l)
                if h == 15:
                    keep_heads(2 * l + 1, HD, True)
                if h == 16:
                    keep_heads(2 * l + 1, HD, False)
                if h == 18:
                    exps(2 * l + 1, 1.0)
                if h == 19:
                    keep_probs(2 * l + 1)
                if h == 21:
                    out_hi(2 * l + 1)
                if h == 23:
                    act.wait_ge(ln_ms, l + 1)
                    act.activation(ln_sd, ln_sd, ACT.Sqrt).then_inc(ln_sdone, 1)
                if h == 24:
                    act.wait_ge(ln_z, l + 1)
                    act.activation(ln_sq, flat2(conv[:, :, :]), ACT.Tanh, scale=0.5).then_inc(ln_th, 1)
                    act.wait_ge(ln_o, l + 1)
                    act.activation(flat2(br_hi[:, 6:8, :]), ln_sq, ACT.Copy, scale=0.5).then_inc(d_hi, 1)
                if M_BR <= h < M_O:
                    for j in (2 * (h - M_BR), 2 * (h - M_BR) + 1):
                        act.wait_ge(merged_f, 8 * l + j + 1)
                        act.activation(hT_hi[:, j, :], gates[:, 0, j, :], ACT.Copy, scale=0.5)\
                            .then_inc(merged_hi, 1)

            for l in range(DEPTH):
                if l:
                    act.wait_ge(stored, 64 * l)
                for h in range(24):
                    hi(ada0[l] + h)
                    if l == 0 and h in (7, 9, 11, 13):
                        m = (h - 7) // 2
                        dst, n = (badaT[:, m // 2, :], 48) if m % 2 else (vecT[:, m // 2, :], V_ROWS)
                        act.wait_ge(v_turned, m + 1)
                        act.activation(dst, ps[:, 6 - m % 2, 0:n], ACT.Copy).then_inc(v_kept, 1)
                    if h >= 2 and h % 2 == 0:
                        c_ = h // 2 - 1
                        act.wait_ge(piece_used, 2 * (ada0[l] + 2 * c_ + 2))
                        if c_ >= 2:
                            act.wait_ge(ada_folded, 12 * l + c_ - 1)
                        act.activation(arow[:, c_ % 2, :], ps[0:4, c_ % 2, :], ACT.Copy).then_inc(ada_kept, 1)
                act.wait_ge(piece_used, 2 * (ada0[l] + 24))
                act.wait_ge(ada_folded, 12 * l + 10)
                act.activation(arow[:, 1, :], ps[0:4, 1, :], ACT.Copy).then_inc(ada_kept, 1)
                norm(2 * l)
                act.wait_ge(bias_turned, l + 1)
                act.activation(bias[:, :, :].rearrange("p h k -> p (h k)"), ps[:, 6, :], ACT.Copy)\
                    .then_inc(bias_kept, 1)
                for h in range(M_HALVES):
                    hi(mix0[l] + h)
                    if h:
                        mixer_task(l, h - 1)
                norm(2 * l + 1)
                if l == 0:
                    def ff_task(hh):
                        kind, ch = FFN[hh // 2]
                        q = hh % 2
                        if kind == "gate":
                            act.wait_ge(piece_used, 2 * (ff0 + hh + 1))
                            if ch:
                                act.wait_ge(ff_hid_done, 2 * ch - 1 + q)
                            act.activation(ff_act[:, q, :], ps[:, q, :], ACT.Silu).then_inc(ff_act_done, 1)
                        if kind == "up":
                            act.wait_ge(ff_hid_done, 2 * ch + q + 1)
                            if ch >= 2:
                                act.wait_ge(piece_used, ff_used("down", ch - 2))
                            a = 4 * (ch % 2) + 2 * q
                            act.activation(flat2(br_hi[:, a:a + 2, :]), ff_hid[:, q, :], ACT.Copy)\
                                .then_inc(ff_hi, 1)

                    for hh in range(FFN_HALVES):
                        hi(ff0 + hh)
                        if hh:
                            ff_task(hh - 1)
            for b in range(4):
                act.wait_ge(h2_turned, b + 1)
                act.activation(h2tok[:, b // 2, 512 * (b % 2):512 * (b % 2) + 512], ps[:, 4 + b, :], ACT.Copy)\
                    .then_inc(h2_kept, 1)

            act.wait_ge(mask_done, 1)
            act.activation(tq[:, 4:6], tq[:, 4:6], ACT.Exp).then_inc(pair_exp, 1)

            act.wait_ge(tab_done, 1)
            n_items = act.value_load(itab[0:1, 0:1], min_val=NEXP, max_val=ITEMS)

            def gathered_hi(n):
                act.wait_ge(xe_t, n)
                act.activation(flat2(hT_hi[:, 0:4, :]), flat2(ps[:, 5:7, :]), ACT.Copy).then_inc(xe_hi, 1)

            def keep_y(i):
                act.wait_ge(piece_used, i * FFN_PIECES + 2 * HALVES)
                act.activation(y_tok, flat2(ps[:, 3:5, :]), ACT.Copy).then_inc(y_kept, 1)

            gathered_hi(1)
            act.wait_ge(y_cleared, 1)
            with act.Fori(0, n_items) as i:
                def item_hi(hh):
                    slot = len(SLOTS) + hh // 2
                    act.wait_ge(raw_landed[slot % RAW], i * (16 * len(FFN) // RAW) + 16 * (slot // RAW + 1))
                    for c_ in range(2):
                        part, h, _ = item_piece(hh, c_)
                        act.wait_ge(piece_used, i * FFN_PIECES + (2 * (HALVES + hh) + c_ - PIECES + 1))
                        act.activation(h, part, ACT.Copy).then_inc(hi_piece, 1)

                def item_task(hh):
                    kind, ch = FFN[hh // 2]
                    if kind == "gate" and hh % 2:
                        act.wait_ge(piece_used, i * FFN_PIECES + 2 * (HALVES + hh + 1))
                        act.activation(ff_act[:, 0, :], ps[:, 0, :], ACT.Silu).then_inc(e_act, 1)
                    if (kind == "down" and hh % 2 == 0 and ch < CHUNKS - 1) or (kind == "up" and hh % 2 and ch == 0):
                        t = 0 if kind == "up" else ch + 1
                        act.wait_ge(e_turn, i * CHUNKS + (t + 1))
                        a = 2 * (t % 2)
                        if t >= 2:
                            act.wait_ge(piece_used, i * FFN_PIECES + 2 * (HALVES + 2 * FFN.index(("down", t - 2)) + 2))
                        act.activation(flat2(br_hi[:, a:a + 2, :]), ps[:, 2, :], ACT.Copy).then_inc(e_hi, 1)

                for hh in range(FFN_HALVES):
                    item_hi(hh)
                    if hh:
                        item_task(hh - 1)
                    if hh == 1:
                        keep_y(i)
                    if hh == I_TURN + 1:
                        act.wait_ge(selT_t, i + 1)
                        act.activation(selT, ps[:, 6, 0:256], ACT.Copy).then_inc(selT_kept, 1)
                    if hh == I_GATHER + 1:
                        gathered_hi(i + 2)
            keep_y(n_items)

            for b in range(4):
                act.wait_ge(fin_t, b + 1)
                act.activation(xtok[:, b // 2, 512 * (b % 2):512 * (b % 2) + 512], ps[:, b, :], ACT.Copy)\
                    .then_inc(fin_kept, 1)

        @block.vector
        def _(dve):
            links = [0]

            def link(ins):
                links[0] += 1
                ins.then_inc(dve_link, 1)
                dve.wait_ge(dve_link, links[0])

            tt, ts, stt = dve.tensor_tensor, dve.tensor_scalar, dve.scalar_tensor_tensor

            def lo(H):
                for c_ in range(2):
                    part, h, w = piece(H, c_)
                    dve.wait_ge(hi_piece, 2 * H + c_ + 1)
                    tt(w, part, h.bitcast(F32), ALU.subtract).then_inc(lo_piece, 1)

            dve.wait_ge(cond_th, 1)
            link(ts(small[:, 64:80], small[:, 64:80], 0.5, 0.5, ALU.mult, ALU.add))
            tt(small[:, 80:96], small[:, 64:80], ps[:, 7, 0:16], ALU.mult).then_inc(cond_ready, 1)
            dve.wait_ge(cond_hi, 1)
            tt(cond_hl[:, :, 2:4], small[:, 80:96].rearrange("p (g k) -> p k g", g=2),
               cond_hl[:, :, 0:2].bitcast(F32), ALU.subtract).then_inc(cond_lo, 1)

            def modulation(l):
                dve.wait_ge(ada_folded, 12 * (l + 1))
                if l == 0:
                    dve.wait_ge(v_kept, 2 * DEPTH)
                link(tt(modT[:, :, :], ps[:, 2, 0:96].rearrange("p (m g) -> p m g", g=2),
                        badaT[:, l, :].unsqueeze(2).to_broadcast([P, 48, 2]), ALU.add))
                for s, v in ((0, V_N1), (1, V_N2)):
                    ins = stt(scaleT[:, s, :, :], modT[:, 24 * s + 8:24 * s + 16, :], 1.0,
                              vecT[:, l, v:v + 8].unsqueeze(2).to_broadcast([P, 8, 2]), ALU.add, ALU.mult)
                ins.then_inc(mod_done, 1)

            def norm(n):
                s = n % 2
                dve.wait_ge(stat_done, n + 1)
                ts(rstd, ps[:, 4, 0:256], 1.0 / D, EPS, ALU.mult, ALU.add).then_inc(ms_done, 1)
                dve.wait_ge(sd_done, n + 1)
                link(dve.reciprocal(rstd, rstd))
                if s == 0:
                    dve.wait_ge(mod_done, n // 2 + 1)
                for k in range(0, KT, 4):
                    link(tt(hF[:, k:k + 4, :], xT[:, k:k + 4, :], rstd.unsqueeze(1).to_broadcast([P, 4, NT]),
                            ALU.mult))
                    for kk in range(k, k + 4):
                        for g in range(2):
                            part = hF[:, kk, TOK * g:TOK * g + TOK]
                            ins = ts(part, part, scaleT[:, s, kk, g:g + 1], modT[:, 24 * s + kk, g:g + 1],
                                     ALU.mult, ALU.add)
                    ins.then_inc(hF_done, 1)
                for k in range(2):
                    dve.wait_ge(h_hi, 2 * n + k + 1)
                    tt(hT_lo[:, 4 * k:4 * k + 4, :], hF[:, 4 * k:4 * k + 4, :],
                       hT_hi[:, 4 * k:4 * k + 4, :].bitcast(F32), ALU.subtract).then_inc(h_lo, 1)

            def wide_col(a, n):
                return a.unsqueeze(2).to_broadcast([P, a.shape[1], n])

            def latents(l):
                dve.wait_ge(drained, 25 * l + 2)
                s = qk[:, 0:768].rearrange("p (g d) -> p g d", g=2)
                link(tt(s, tokA[:, :, 0:384], tokA[:, :, 0:384], ALU.mult))
                dve.tensor_reduce(small[:, 0:2], s[:, :, 0:256], AX.X, ALU.add)
                link(dve.tensor_reduce(small[:, 2:4], s[:, :, 256:384], AX.X, ALU.add))
                ts(small[:, 0:2], small[:, 0:2], 1.0 / QL, EPS, ALU.mult, ALU.add)
                ts(small[:, 2:4], small[:, 2:4], 1.0 / KVL, EPS, ALU.mult, ALU.add).then_inc(stats_in, 1)
                dve.wait_ge(pool_pow, 3 * l + 1)
                tt(tokA[:, :, 0:256], tokA[:, :, 0:256], wide_col(small[:, 0:2], 256), ALU.mult)
                link(tt(tokA[:, :, 256:384], tokA[:, :, 256:384], wide_col(small[:, 2:4], 128), ALU.mult))
                dve.wait_ge(small_in, 112 * (l + 1))
                tt(tokA[:, :, 256:384], tokA[:, :, 256:384], gkv_b[:, :].unsqueeze(1).to_broadcast([P, 2, KVL]),
                   ALU.mult).then_inc(qa_normed, 1)

            def head_stats(l):
                dve.wait_ge(qkv_kept, 5 * l + 5)
                dve.wait_ge(cache_in, 32 * (l + 1))
                link(tt(heads_sq, qk[:, 0:768], qk[:, 0:768], ALU.mult))
                link(dve.tensor_reduce(small[:, 8:16], heads_sq.rearrange("p (a d) -> p a d", d=QK), AX.X, ALU.add))
                knope = KV[:, :, :].rearrange("p s (h d) -> p s h d", h=HEADS)[:, :, :, 0:NOPE]
                link(tt(heads_sq.rearrange("p (s h d) -> p s h d", s=3, h=HEADS), knope, knope, ALU.mult))
                link(dve.tensor_reduce(small[:, 16:28], heads_sq.rearrange("p (a d) -> p a d", d=NOPE), AX.X,
                                       ALU.add))
                kpe = tokA[:, :, 384:416]
                tt(heads_sq[:, 0:64].rearrange("p (g d) -> p g d", g=2), kpe, kpe, ALU.mult)
                link(tt(heads_sq[:, 64:96], kpc, kpc, ALU.mult))
                link(dve.tensor_reduce(small[:, 112:115], heads_sq[:, 0:96].rearrange("p (s d) -> p s d", s=3),
                                       AX.X, ALU.add))
                kss = small[:, 16:28].rearrange("p (s h) -> p s h", s=3)
                link(tt(kss, kss, wide_col(small[:, 112:115], HEADS), ALU.add))
                ts(small[:, 8:28], small[:, 8:28], 1.0 / QK, EPS, ALU.mult, ALU.add).then_inc(stats_in, 1)

            def head_norm(l):
                dve.wait_ge(pool_pow, 3 * l + 2)
                q = qk[:, 0:768].rearrange("p (a d) -> p a d", d=QK)
                kn = qk[:, 768:1920].rearrange("p (a d) -> p a d", d=QK)
                tt(q, q, wide_col(small[:, 8:16], QK), ALU.mult)
                rs = small[:, 16:28].rearrange("p (s h) -> p s h", s=3)
                tt(Kn[:, :, :, 0:NOPE], KV[:, :, :].rearrange("p s (h d) -> p s h d", h=HEADS)[:, :, :, 0:NOPE],
                   rs.unsqueeze(3).to_broadcast([P, 3, HEADS, NOPE]), ALU.mult)
                tt(Kn[:, 0:2, :, NOPE:QK], tokA[:, :, 384:416].unsqueeze(2).to_broadcast([P, 2, HEADS, ROPE]),
                   rs[:, 0:2, :].unsqueeze(3).to_broadcast([P, 2, HEADS, ROPE]), ALU.mult)
                link(tt(Kn[:, 2, :, NOPE:QK], kpc.unsqueeze(1).to_broadcast([P, HEADS, ROPE]),
                        wide_col(small[:, 24:28], ROPE), ALU.mult))
                tt(q, q, gq_b[:, :].unsqueeze(1).to_broadcast([P, 8, QK]), ALU.mult)
                link(tt(kn, kn, gk_b[:, :].unsqueeze(1).to_broadcast([P, 12, QK]), ALU.mult))

            def rope(l):
                def trig(at):
                    return consts[:, at:at + 16].rearrange("p (a f) -> p a f", a=2).unsqueeze(1)\
                        .to_broadcast([P, HEADS, 2, 8])
                cos, sin = trig(K_COS), trig(K_SIN)
                parts = []
                for n, x in enumerate((Q[:, 1, :, NOPE:QK], Kn[:, 1, :, NOPE:QK])):
                    v = x.rearrange("p h (a b f) -> p h a b f", a=2, b=2)
                    x1, x2 = v[:, :, :, 0, :], v[:, :, :, 1, :]
                    t = [ropet[:, 4 * n + m, :].rearrange("p (h a f) -> p h a f", h=HEADS, a=2) for m in range(4)]
                    tt(t[0], x1, cos, ALU.mult)
                    tt(t[1], x2, sin, ALU.mult)
                    tt(t[2], x1, sin, ALU.mult)
                    ins = tt(t[3], x2, cos, ALU.mult)
                    parts.append((x1, x2, t))
                link(ins)
                for x1, x2, t in parts:
                    tt(x1, t[0], t[1], ALU.subtract)
                    ins = tt(x2, t[2], t[3], ALU.add)
                ins.then_inc(qk_ready, 1)

            def na_stats(l):
                dve.wait_ge(drained, 25 * l + 5)
                link(tt(na_sq, tokN[:, :, 0:512], tokN[:, :, 0:512], ALU.mult))
                link(dve.tensor_reduce(small[:, 32:48], big[:, 0:1024].rearrange("p (a d) -> p a d", d=HD), AX.X,
                                       ALU.add))
                ts(small[:, 32:48], small[:, 32:48], 1.0 / HD, EPS, ALU.mult, ALU.add).then_inc(stats_in, 1)

            def na_norm(l):
                dve.wait_ge(pool_pow, 3 * l + 3)
                x = tokN[:, :, 0:512].rearrange("p g (a d) -> p g a d", d=HD)
                rs = small[:, 32:48].rearrange("p (g a) -> p g a", g=2).unsqueeze(3).to_broadcast([P, 2, 8, HD])
                link(tt(x, x, rs, ALU.mult))
                link(ts(gnq_b[:, :], gnq_b[:, :], HD ** -0.5, None, ALU.mult))
                for a, gain in ((0, gnq_b), (4, gnk_b)):
                    y = x[:, :, a:a + 4, :]
                    ins = tt(y, y, gain[:, :].unsqueeze(1).unsqueeze(1).to_broadcast([P, 2, 4, HD]), ALU.mult)
                ins.then_inc(na_ready, 1)

            def softmax_max(u, scale):
                dve.wait_ge(scores_done, u + 1)
                if u % 2:
                    dve.wait_ge(bias_kept, u // 2 + 1)
                    if u // 2 == 0:
                        dve.wait_ge(consts_in, 16)
                    link(tt(sbias, ps[:, 6, :], bias[:, :, :].rearrange("p h k -> p (h k)"), ALU.add))
                    m = sbias.rearrange("p (h k) -> p h k", h=HEADS)
                    link(tt(m, m, consts[:, K_MASK:K_MASK + TOK].unsqueeze(1).to_broadcast([P, HEADS, TOK]),
                            ALU.add))
                for s in range(3):
                    src = sbias if u % 2 and s == 1 else ps[:, 5 + s, :]
                    ins = dve.tensor_reduce(small[:, 92 + 4 * s:96 + 4 * s],
                                            src.rearrange("p (h k) -> p h k", h=HEADS), AX.X, ALU.max)
                link(ins)
                link(tt(small[:, 96:100], small[:, 96:100], small[:, 100:104], ALU.max))
                ts(small[:, 60:68], small[:, 92:100], -scale, None, ALU.mult)
                ts(small[:, 68:72], small[:, 96:100], -scale, None, ALU.mult).then_inc(max_done, 1)

            def scale_out(u):
                dve.wait_ge(exp_done, 12 * (u + 1))
                link(tt(small[:, 80:84], small[:, 80:84], small[:, 84:88], ALU.add))
                link(dve.reciprocal(small[:, 104:112], small[:, 76:84]))
                dve.wait_ge(o_done, u + 1)
                tt(O.rearrange("p g (h d) -> p g h d", h=HEADS),
                   ps[:, 4, :].rearrange("p (g h d) -> p g h d", g=2, h=HEADS),
                   small[:, 104:112].rearrange("p (g h) -> p g h", g=2).unsqueeze(3)
                   .to_broadcast([P, 2, HEADS, HD]), ALU.mult).then_inc(o_scaled, 1)

            def out_lo(u):
                a = 4 * (u % 2)
                dve.wait_ge(o_hi, u + 1)
                tt(br_lo[:, a:a + 2, :].rearrange("p a b -> p (a b)"), ps[:, 4, :],
                   br_hi[:, a:a + 2, :].bitcast(F32).rearrange("p a b -> p (a b)"), ALU.subtract)\
                    .then_inc(o_lo, 1)

            def two(a):
                return a.rearrange("p (g t) -> p g t", g=2)

            conv_ops = [0]

            def tap(l, pad, taps, row, k, tile):
                src = pad[:, tile, :, k:k + TOK]
                dst = two(conv[:, tile, :])
                w = vecT[:, l, row + 2 * k + tile:row + 2 * k + tile + 1]
                if k:
                    dve.wait_ge(conv_v, conv_ops[0] - 1)
                    ins = stt(dst, src, w, dst, ALU.mult, ALU.add)
                else:
                    ins = ts(dst, src, w, None, ALU.mult)
                ins.then_inc(conv_v, 1)
                conv_ops[0] += 1

            def branch_b(l):
                for k in range(SCK):
                    for tile in range(2):
                        tap(l, scpad, SCK, V_SC, k, tile)
                dve.wait_ge(conv_v, conv_ops[0])
                tt(bc[:, 0:2, :], bc[:, 0:2, :], conv[:, :, :], ALU.mult).then_inc(b_ready, 1)

            def branch_d(l, first, last):
                for n in range(first, last):
                    tap(l, cfpad, CFK, V_CF, n // 2, n % 2)

            def mixer_task(l, h):
                if h == 1:
                    latents(l)
                if h == 5:
                    head_stats(l)
                if h == 6:
                    na_stats(l)
                    head_norm(l)
                if h == 7:
                    rope(l)
                    dve.wait_ge(drained, 25 * l + 7)
                    dve.wait_ge(piece_used, filled(l, 7))
                    if l == 0:
                        dve.wait_ge(setup, 4)
                    tt(scpad[:, :, :, 1:1 + TOK], ps[:, 3, :].rearrange("p (a g t) -> p a g t", a=2, g=2),
                       bc[:, 2:4, :].rearrange("p a (g t) -> p a g t", g=2), ALU.mult).then_inc(xv_read, 1)
                if h == 8:
                    dve.wait_ge(xv_read, l + 1)
                    na_norm(l)
                    branch_b(l)
                if h == 10:
                    softmax_max(2 * l, QK ** -0.5)
                if h == 11:
                    dve.wait_ge(drained, 25 * l + 9)
                    for tile in range(2):
                        ins = stt(cfpad[:, tile, :, 15:15 + TOK], two(cf[:, 2 + tile, :]), 1.0,
                                  two(cf[:, tile, :]), ALU.add, ALU.mult)
                    ins.then_inc(cf_used, 1)
                    dve.wait_ge(cf_used, l + 1)
                    dve.wait_ge(b_ready, l + 1)
                    branch_d(l, 0, 6)
                if h == 12:
                    dve.wait_ge(b_hi, l + 1)
                    tt(br_lo[:, 2:4, :], bc[:, 0:2, :], br_hi[:, 2:4, :].bitcast(F32), ALU.subtract)\
                        .then_inc(b_lo, 1)
                    branch_d(l, 6, 12)
                if h == 13:
                    scale_out(2 * l)
                    branch_d(l, 12, 18)
                if h == 14:
                    out_lo(2 * l)
                    branch_d(l, 18, 24)
                if h == 15:
                    branch_d(l, 24, 32)
                if h == 16:
                    branch_d(l, 32, 40)
                if h == 17:
                    softmax_max(2 * l + 1, 1.0)
                if h == 18:
                    branch_d(l, 40, 48)
                if h == 19:
                    branch_d(l, 48, 56)
                if h == 20:
                    scale_out(2 * l + 1)
                    branch_d(l, 56, 62)
                if h == 21:
                    out_lo(2 * l + 1)
                    dve.wait_ge(conv_v, conv_ops[0])
                    for tile in range(2):
                        ins = ts(conv[:, tile, :], conv[:, tile, :], 0.5, vecT[:, l, V_CFB + tile:V_CFB + tile + 1],
                                 ALU.mult, ALU.add)
                    ins.then_inc(conv_ready, 1)
                if h == 22:
                    dve.wait_ge(ln_sum, l + 1)
                    dve.wait_ge(conv_ready, l + 1)
                    for tile in range(2):
                        ins = stt(conv[:, tile, :], ps[:, 5, 0:256], -1.0 / BW, conv[:, tile, :], ALU.mult, ALU.add)
                    link(ins)
                    tt(ln_sq, conv[:, :, :].rearrange("p a t -> p (a t)"),
                       conv[:, :, :].rearrange("p a t -> p (a t)"), ALU.mult).then_inc(ln_sq_done, 1)
                if h == 23:
                    dve.wait_ge(ln_sqsum, l + 1)
                    ts(ln_sd, ps[:, 6, 0:256], 1.0 / BW, EPS, ALU.mult, ALU.add).then_inc(ln_ms, 1)
                if h == 24:
                    dve.wait_ge(ln_sdone, l + 1)
                    link(dve.reciprocal(ln_sd, ln_sd))
                    link(tt(conv[:, :, :], conv[:, :, :], ln_sd.unsqueeze(1).to_broadcast([P, 2, NT]), ALU.mult))
                    for tile in range(2):
                        ins = ts(conv[:, tile, :], conv[:, tile, :], vecT[:, l, V_LNG + tile:V_LNG + tile + 1],
                                 vecT[:, l, V_LNB + tile:V_LNB + tile + 1], ALU.mult, ALU.add)
                    ins.then_inc(ln_z, 1)
                    dve.wait_ge(ln_th, l + 1)
                    stt(ln_sq, ln_sq, 1.0, conv[:, :, :].rearrange("p a t -> p (a t)"), ALU.add, ALU.mult)\
                        .then_inc(ln_o, 1)
                    dve.wait_ge(d_hi, l + 1)
                    stt(br_lo[:, 6:8, :].rearrange("p a t -> p (a t)"), ln_sq, 0.5,
                        br_hi[:, 6:8, :].bitcast(F32).rearrange("p a t -> p (a t)"), ALU.mult, ALU.subtract)\
                        .then_inc(d_lo, 1)
                if M_BR <= h < M_O:
                    for j in (2 * (h - M_BR), 2 * (h - M_BR) + 1):
                        dve.wait_ge(piece_used, 2 * (mix0[l] + h) + j % 2 + 1)
                        dve.wait_ge(drained, 25 * (l + 1))
                        for b in range(2):
                            g2 = gates[:, 2 * b:2 * b + 2, j, :]
                            ins = stt(g2, g2, 1.0, ps[:, 2 * (j % 2) + b, :].rearrange("p (n t) -> p n t", n=2),
                                      ALU.add, ALU.mult)
                        ins.then_inc(proj_read, 1)
                        dve.wait_ge(proj_read, 8 * l + j + 1)
                        link(tt(gates[:, 0:2, j, :], gates[:, 0:2, j, :], gates[:, 2:4, j, :], ALU.add))
                        tt(gates[:, 0, j, :], gates[:, 0, j, :], gates[:, 1, j, :], ALU.add).then_inc(merged_f, 1)
                        dve.wait_ge(merged_hi, 8 * l + j + 1)
                        stt(hT_lo[:, j, :], gates[:, 0, j, :], 0.5, hT_hi[:, j, :].bitcast(F32), ALU.mult,
                            ALU.subtract).then_inc(merged_lo, 1)
                if M_O <= h:
                    dve.wait_ge(piece_used, 2 * (mix0[l] + h + 1))
                    for jj in range(2):
                        j = 2 * (h - M_O) + jj
                        for g in range(2):
                            r = xT[:, j, TOK * g:TOK * g + TOK]
                            a = 256 * jj + TOK * g
                            ins = stt(r, ps[:, h - M_O, a:a + TOK], modT[:, 16 + j, g:g + 1], r, ALU.mult, ALU.add)
                    ins.then_inc(wo_read, 1)

            def ff_task(hh):
                kind, ch = FFN[hh // 2]
                q = hh % 2
                if kind == "up":
                    n = 2 * ch + q + 1
                    dve.wait_ge(ff_act_done, n)
                    dve.wait_ge(piece_used, 2 * (ff0 + hh + 1))
                    if ch:
                        dve.wait_ge(ff_hi, n - 2)
                    tt(ff_hid[:, q, :], ff_act[:, q, :], ps[:, 2 + q, :], ALU.mult).then_inc(ff_hid_done, 1)
                    dve.wait_ge(ff_hi, n)
                    a = 4 * (ch % 2) + 2 * q
                    tt(br_lo[:, a:a + 2, :].rearrange("p a b -> p (a b)"), ff_hid[:, q, :],
                       br_hi[:, a:a + 2, :].bitcast(F32).rearrange("p a b -> p (a b)"), ALU.subtract)\
                        .then_inc(ff_lo, 1)

            for l in range(DEPTH):
                for h in range(24):
                    lo(ada0[l] + h)
                modulation(l)
                norm(2 * l)
                for h in range(M_HALVES):
                    lo(mix0[l] + h)
                    if h:
                        mixer_task(l, h - 1)
                mixer_task(l, M_HALVES - 1)
                dve.wait_ge(wo_read, 4 * (l + 1))
                norm(2 * l + 1)
                if l == 0:
                    for hh in range(FFN_HALVES):
                        lo(ff0 + hh)
                        if hh:
                            ff_task(hh - 1)
                    dve.wait_ge(piece_used, ff_used("down", CHUNKS - 1))
                    for j in range(KT):
                        for g in range(2):
                            r = xT[:, j, TOK * g:TOK * g + TOK]
                            a = 256 * (j % 2) + TOK * g
                            ins = stt(r, ps[:, 4 + j // 2, a:a + TOK], modT[:, 40 + j, g:g + 1], r,
                                      ALU.mult, ALU.add)
                    ins.then_inc(ff_read, 1)

            def col(a):
                return a.unsqueeze(2)

            left = consts[:, K_LEFT:K_LEFT + 8].unsqueeze(1).to_broadcast([P, 2, 8])
            dve.wait_ge(lg_done, 1)
            link(dve.tensor_copy(lg, ps[:, 0, 0:16].rearrange("p (g e) -> p g e", g=2)))

            def first_largest(logits, top, onehot):
                link(dve.tensor_reduce(top, logits, AX.X, ALU.max))
                link(tt(tmp, logits, col(top).to_broadcast([P, 2, 8]), ALU.is_ge))
                link(tt(tmp, tmp, left, ALU.mult))
                link(dve.tensor_reduce(tq[:, 8:10], tmp, AX.X, ALU.max))
                link(tt(onehot, left, col(tq[:, 8:10]).to_broadcast([P, 2, 8]), ALU.is_equal))

            first_largest(lg, tq[:, 0:2], oh1)
            link(stt(lg2, oh1, -1e30, lg, ALU.mult, ALU.add))
            first_largest(lg2, tq[:, 2:4], oh2)
            link(tt(tq[:, 4:6], tq[:, 2:4], tq[:, 0:2], ALU.subtract))
            tt(mask, oh1, oh2, ALU.add).then_inc(mask_done, 1)
            dve.wait_ge(pair_exp, 1)
            link(ts(tq[:, 6:8], tq[:, 4:6], 1.0, None, ALU.add))
            link(dve.reciprocal(tq[:, 6:8], tq[:, 6:8]))
            link(tt(tq[:, 4:6], tq[:, 4:6], tq[:, 6:8], ALU.mult))
            tt(oh1, oh1, col(tq[:, 6:8]).to_broadcast([P, 2, 8]), ALU.mult)
            link(tt(oh2, oh2, col(tq[:, 4:6]).to_broadcast([P, 2, 8]), ALU.mult))
            tt(tab[:, 2, :, 0:8], oh1, oh2, ALU.add)
            dve.tensor_copy(tab[:, 1, :, 0:8], mask)
            dve.wait_ge(pos_done, 1)
            dve.tensor_copy(tab[:, 0, :, 0:8], ps[:, 1, 0:16].rearrange("p (g e) -> p g e", g=2))
            link(ts(ov, ps[:, 1, 16:24], float(CAP), None, ALU.is_gt))
            link(tt(w64, consts[:, K_BEFORE:K_BEFORE + 64].rearrange("p (a e) -> p a e", a=8),
                    ov.unsqueeze(1).to_broadcast([P, 8, 8]), ALU.mult))
            link(dve.tensor_reduce(rank, w64, AX.X, ALU.add))
            for k in range(OVER):
                ins = stt(ohk[:, k, :], rank, float(k), ov, ALU.is_equal, ALU.mult)
            link(ins)
            for q in range(3):
                a = tab[:, q, :, 0:8]
                if q == 0:
                    link(ts(tmp, a, float(-CAP), None, ALU.add))
                    a = tmp
                for t in range(2):
                    link(tt(wide[:, t, :, :], ohk, a[:, t, :].unsqueeze(1).to_broadcast([P, OVER, 8]), ALU.mult))
                link(dve.tensor_reduce(tab[:, q, :, NEXP:ITEMS], wide, AX.X, ALU.add))
            link(tt(wide[:, 0, :, :], ohk, consts[:, K_EXP:K_EXP + 8].unsqueeze(1).to_broadcast([P, OVER, 8]),
                    ALU.mult))
            dve.tensor_reduce(eidx[:, 2:2 + OVER], wide[:, 0, :, :], AX.X, ALU.add)
            link(dve.tensor_reduce(eidx[:, 1:2], ov, AX.X, ALU.add))
            link(ts(eidx[:, 0:1], eidx[:, 1:2], float(NEXP), None, ALU.add))
            dve.memset(fT, 0.0)
            dve.memset(tab[:, :, :, ITEMS:ITEMS + 1], 0.0)
            dve.tensor_copy(itab[0:1, 0:OVER + 2], eidx[0:1, :]).then_inc(tab_done, 1)

            dve.wait_ge(tab_done, 1)
            n_items = dve.value_load(itab[0:1, 0:1], min_val=NEXP, max_val=ITEMS)
            iota = consts[:, K_IOTA:K_IOTA + P]

            def select(n):
                dve.tensor_copy(stage, tab[:, :, :, bass.ds(n, 1)].rearrange("p q t i -> p q (t i)"))\
                    .then_inc(staged, 1)
                dve.wait_ge(staged, n + 1)
                for t in range(2):
                    ts(sel[:, t, :], iota, stage[:, 0, t:t + 1], stage[:, 1, t:t + 1], ALU.is_equal, ALU.mult)
                    ins = ts(selg[:, t, :], iota, stage[:, 0, t:t + 1], stage[:, 2, t:t + 1], ALU.is_equal,
                             ALU.mult)
                ins.then_inc(sel_done, 1)

            def gathered_lo(n):
                dve.wait_ge(xe_hi, n)
                tt(hT_lo[:, 0:4, :].rearrange("p a b -> p (a b)"), ps[:, 5:7, :].rearrange("p a b -> p (a b)"),
                   hT_hi[:, 0:4, :].bitcast(F32).rearrange("p a b -> p (a b)"), ALU.subtract).then_inc(xe_lo, 1)

            def add_scattered(hh, i):
                for r, bank in I_SCATTER[hh]:
                    dve.wait_ge(sc_fill, i * 4 + (r + 1))
                    f = fT[:, 2 * r:2 * r + 2, :].rearrange("p a b -> p (a b)")
                    tt(f, ps[:, bank, :], f, ALU.add).then_inc(item_added, 1)

            dve.memset(ps[:, 3:5, :], 0.0).then_inc(y_cleared, 1)
            dve.memset(selT, 0.0).then_inc(selT_kept, 1)
            select(0)
            gathered_lo(1)
            with dve.Fori(0, n_items) as i:
                def item_lo(hh):
                    for c_ in range(2):
                        part, h, w = item_piece(hh, c_)
                        dve.wait_ge(hi_piece, i * FFN_PIECES + (2 * (HALVES + hh) + c_ + 1))
                        tt(w, part, h.bitcast(F32), ALU.subtract).then_inc(lo_piece, 1)

                def item_task(hh):
                    kind, ch = FFN[hh // 2]
                    if kind == "up" and hh % 2:
                        dve.wait_ge(e_act, i * CHUNKS + (ch + 1))
                        dve.wait_ge(piece_used, i * FFN_PIECES + 2 * (HALVES + hh + 1))
                        tt(ff_hid[:, 0, :], ff_act[:, 0, :], ps[:, 1, :], ALU.mult).then_inc(e_hid, 1)
                    if (kind == "down" and hh % 2 == 0 and ch < CHUNKS - 1) or (kind == "up" and hh % 2 and ch == 0):
                        t = 0 if kind == "up" else ch + 1
                        dve.wait_ge(e_hi, i * CHUNKS + (t + 1))
                        a = 2 * (t % 2)
                        tt(br_lo[:, a:a + 2, :].rearrange("p a b -> p (a b)"), ps[:, 2, :],
                           br_hi[:, a:a + 2, :].bitcast(F32).rearrange("p a b -> p (a b)"), ALU.subtract)\
                            .then_inc(e_lo, 1)

                for hh in range(FFN_HALVES):
                    item_lo(hh)
                    if hh:
                        item_task(hh - 1)
                    if hh - 1 in I_SCATTER:
                        add_scattered(hh - 1, i)
                    if hh == I_SELECT:
                        dve.wait_ge(selT_t, i + 1)
                        dve.wait_ge(xe_t, i + 1)
                        select(i + 1)
                    if hh == I_GATHER + 1:
                        gathered_lo(i + 2)
            for hh in I_SCATTER:
                add_scattered(hh, n_items)
            dve.wait_ge(item_added, n_items * 4 + 4)
            for j in range(KT):
                for g in range(2):
                    r = xT[:, j, TOK * g:TOK * g + TOK]
                    ins = stt(r, fT[:, j, TOK * g:TOK * g + TOK], modT[:, 40 + j, g:g + 1], r, ALU.mult, ALU.add)
            ins.then_inc(moe_done, 1)

        @block.tensor
        def _(pe):
            mm = pe.matmul

            def mm3(out, a_hi, a_lo, b_hi, b_lo, start, stop, shared=False):
                mm(out, a_hi, b_hi, start=start, stop=False, skip_group_check=shared)
                mm(out, a_hi, b_lo, start=False, stop=False, skip_group_check=shared)
                return mm(out, a_lo, b_hi, start=False, stop=stop, skip_group_check=shared)

            def turn(out, x):
                return pe.transpose(out, x, ident[0:x.shape[0], 0:x.shape[0]])

            def tok(g):
                return slice(TOK * g, TOK * g + TOK)

            pe.wait_ge(consts_in, 16)
            pe.wait_ge(cond_in, 32)
            turn(ps[:, 7, 0:16], vrow[0:16, :]).then_inc(cond_turned, 1)
            pe.wait_ge(x_in, 32)
            for b in range(4):
                for k in (2 * b, 2 * b + 1):
                    for g in range(2):
                        a = 256 * (k % 2) + TOK * g
                        ins = turn(ps[:, b, a:a + TOK], xtok[:, g, P * k:P * k + P])
                ins.then_inc(x_turned, 1)

            def ada_fold(l, c_):
                pe.wait_ge(ada_kept, 12 * l + c_ + 1)
                for q in range(4):
                    a = 2 * (4 * c_ + q)
                    ins = mm(ps[:, 2, a:a + 2], arow[0:4, c_ % 2, P * q:P * q + P],
                             consts[0:4, K_FOLD:K_FOLD + 2], start=True, stop=True)
                ins.then_inc(ada_folded, 1)

            def ada(l):
                if l == 0:
                    pe.wait_ge(cond_lo, 1)
                    pe.wait_ge(x_kept, 4)
                for h in range(24):
                    c_, q = divmod(h, 2)
                    if q == 0 and c_ >= 2:
                        pe.wait_ge(ada_kept, 12 * l + c_ - 1)
                    for n in range(2):
                        pe.wait_ge(lo_piece, 2 * (ada0[l] + h) + n + 1)
                        _, wh, wl = piece(ada0[l] + h, n)
                        for k in range(2):
                            kk = 4 * q + 2 * n + k
                            x = cond_hl[:, kk, :]
                            mm(ps[0:4, c_ % 2, :], x, wh[:, k, :], start=(kk == 0), stop=False)
                            ins = mm(ps[0:4, c_ % 2, :], x, wl[:, k, :], start=False, stop=(kk == KT - 1))
                        ins.then_inc(piece_used, 1)
                    if q:
                        if c_:
                            ada_fold(l, c_ - 1)
                    if l == 0 and h in (5, 7, 9, 11):
                        m = (h - 5) // 2
                        n = V_ROWS if m % 2 == 0 else 48
                        pe.wait_ge(vrow_in, 16 * (9 * (m // 2) + (9 if m % 2 else 8)))
                        if m >= 2:
                            pe.wait_ge(v_kept, m - 1)
                        turn(ps[:, 6 - m % 2, 0:n], vrow[0:n, :]).then_inc(v_turned, 1)
                ada_fold(l, 11)

            def stat(n):
                pe.wait_ge(sq_done, n + 1)
                if n == 0:
                    pe.wait_ge(setup, 4)
                for k in range(KT):
                    ins = mm(ps[:, 4, 0:NT], ones[:, :], sq[:, k, :], start=(k == 0), stop=(k == KT - 1))
                ins.then_inc(stat_done, 1)

            def free_bank(l, f):
                if f - 4 == 7:
                    pe.wait_ge(xv_read, l + 1)
                elif f >= 4:
                    pe.wait_ge(drained, 25 * l + (f - 3 if f - 4 < 7 else f - 4))

            def heads(u, d, q, k, first):
                if first:
                    for g in range(2):
                        for h in range(HEADS):
                            turn(ps[0:d, 4 + g, TOK * h:TOK * h + TOK], q(g, h))
                    for s in range(2):
                        for h in range(HEADS):
                            ins = turn(ps[0:d, 6 + s, TOK * h:TOK * h + TOK], k(s, h))
                else:
                    pe.wait_ge(heads_kept, 5 * u + 1)
                    for h in range(HEADS):
                        ins = turn(ps[0:d, 4, TOK * h:TOK * h + TOK], k(2, h))
                ins.then_inc(heads_turned, 1)

            def scores(u, d):
                pe.wait_ge(heads_kept, 5 * (u + 1))
                for s in range(3):
                    for h in range(HEADS):
                        ins = mm(ps[:, 5 + s, TOK * h:TOK * h + TOK], QT[0:d, min(s, 1), h, :], KTt[0:d, s, h, :],
                                 start=True, stop=True)
                ins.then_inc(scores_done, 1)

            def turn_probs(u):
                pe.wait_ge(exp_done, 12 * (u + 1))
                for s in range(3):
                    for h in range(HEADS):
                        ins = turn(ps[:, 5 + s, TOK * h:TOK * h + TOK], Pr[:, s, h, :])
                ins.then_inc(probs_turned, 1)

            def weigh(u, v):
                pe.wait_ge(probs_kept, 3 * (u + 1))
                for g in range(2):
                    for h in range(HEADS):
                        o = ps[:, 4, 256 * g + HD * h:256 * g + HD * h + HD]
                        for s in ((0,), (1, 2))[g]:
                            ins = mm(o, KTt[:, s, h, :], v(s, h), start=(s < 2), stop=(s != 1))
                ins.then_inc(o_done, 1)

            def turn_out(u):
                pe.wait_ge(o_scaled, u + 1)
                for k in range(2):
                    for g in range(2):
                        a = NT * k + TOK * g
                        ins = turn(ps[:, 4, a:a + TOK], tokA[:, g, P * k:P * k + P])
                ins.then_inc(o_turned, 1)

            def mla_q(g, h):
                return Q[:, g, h, :]

            def mla_k(s, h):
                return Kn[:, s, h, :]

            def mla_v(s, h):
                return KV[:, s, 128 * h + NOPE:128 * h + 128]

            def na_q(g, h):
                return tokN[:, g, HD * h:HD * h + HD]

            def na_k(s, h):
                return tokN[:, s, 256 + HD * h:256 + HD * h + HD] if s < 2 else nakc[:, HD * h:HD * h + HD]

            def na_v(s, h):
                return tokN[:, s, 512 + HD * h:512 + HD * h + HD] if s < 2 else navc[:, HD * h:HD * h + HD]

            def attention_step(l, h):
                if h == 3:
                    pe.wait_ge(qa_normed, l + 1)
                    pe.wait_ge(cache_in, 32 * (l + 1))
                    for k in range(2):
                        for g in range(2):
                            a = NT * k + TOK * g
                            turn(ps[:, 4, a:a + TOK], tokA[:, g, P * k:P * k + P])
                    for s in range(3):
                        ins = turn(ps[:, 5, TOK * s:TOK * s + TOK], tokA[:, s, 256:384] if s < 2 else ckc)
                    ins.then_inc(latent_turned, 1)
                if h == 4:
                    pe.wait_ge(latent_kept, 3 * (l + 1))
                    pe.wait_ge(small_in, 112 * (l + 1))
                    pe.wait_ge(bias_kept, l + 1)
                    for g in range(2):
                        for k in range(2):
                            mm(ps[:, 6 + g, 0:384], qaT[:, k, tok(g)], wuq[:, k, :], start=(k == 0), stop=(k == 1))
                    for s in range(2):
                        ins = mm(ps[:, 4 + s, :], ckvT[:, tok(s)], wukv[:, :], start=True, stop=True)
                    ins.then_inc(qkv_done, 1)
                if h == 5:
                    pe.wait_ge(qkv_kept, 5 * l + 4)
                    mm(ps[:, 4, :], ckvT[:, 256:384], wukv[:, :], start=True, stop=True).then_inc(qkv_done, 1)
                if h == 8:
                    pe.wait_ge(qk_ready, l + 1)
                    heads(2 * l, QK, mla_q, mla_k, True)
                if h == 9:
                    heads(2 * l, QK, mla_q, mla_k, False)
                if h == 10:
                    scores(2 * l, QK)
                if h == 12:
                    turn_probs(2 * l)
                if h == 13:
                    weigh(2 * l, mla_v)
                if h == 14:
                    turn_out(2 * l)
                if h == 15:
                    pe.wait_ge(na_ready, l + 1)
                    pe.wait_ge(o_lo, 2 * l + 1)
                    heads(2 * l + 1, HD, na_q, na_k, True)
                if h == 16:
                    pe.wait_ge(nacache_in, 32 * (l + 1))
                    heads(2 * l + 1, HD, na_q, na_k, False)
                if h == 17:
                    scores(2 * l + 1, HD)
                if h == 19:
                    turn_probs(2 * l + 1)
                if h == 20:
                    weigh(2 * l + 1, na_v)
                if h == 21:
                    turn_out(2 * l + 1)
                if h == 22:
                    pe.wait_ge(conv_ready, l + 1)
                    for tile in range(2):
                        ins = mm(ps[:, 5, 0:NT], ones[:, :], conv[:, tile, :], start=(tile == 0), stop=(tile == 1))
                    ins.then_inc(ln_sum, 1)
                if h == 23:
                    pe.wait_ge(ln_sq_done, l + 1)
                    for tile in range(2):
                        ins = mm(ps[:, 6, 0:NT], ones[:, :], ln_sq[:, NT * tile:NT * tile + NT],
                                 start=(tile == 0), stop=(tile == 1))
                    ins.then_inc(ln_sqsum, 1)

            def mixer_half(l, h):
                H = mix0[l] + h
                kind, _, i, _ = SLOTS[SLOT_OF[H][0]]
                q = SLOT_OF[H][1]
                if kind == "na_v" or kind in ("sc", "cf", "gates"):
                    free_bank(l, h)
                if h == M_BR:
                    pe.wait_ge(drained, 25 * (l + 1))
                    pe.wait_ge(b_lo, l + 1)
                    pe.wait_ge(d_lo, l + 1)
                    pe.wait_ge(o_lo, 2 * l + 2)
                if h == M_O:
                    pe.wait_ge(merged_lo, 8 * (l + 1))
                for c_ in range(2):
                    pe.wait_ge(lo_piece, 2 * H + c_ + 1)
                    _, wh, wl = piece(H, c_)
                    if kind in ("tok", "na_qk"):
                        for g in range(2):
                            bank, n = (2 + g, 512) if kind == "na_qk" else (g, 416)
                            for k in range(2):
                                kk = 4 * q + 2 * c_ + k
                                ins = mm3(ps[:, bank, 0:n], hT_hi[:, kk, tok(g)], hT_lo[:, kk, tok(g)],
                                          wh[:, k, :], wl[:, k, :], kk == 0, kk == KT - 1)
                    elif kind == "na_v":
                        for g in range(2):
                            a = 256 * g + P * c_
                            for k in range(KT):
                                ins = mm3(ps[:, 0, a:a + P], hT_hi[:, k, tok(g)], hT_lo[:, k, tok(g)],
                                          wh[:, k, :], wl[:, k, :], k == 0, k == KT - 1)
                    elif kind == "branch":
                        j = 2 * (h - M_BR) + c_
                        if j >= 2:
                            pe.wait_ge(proj_read, 8 * l + j - 1)
                        for n in range(4):
                            for k in range(2):
                                ins = mm3(ps[:, 2 * c_ + n // 2, NT * (n % 2):NT * (n % 2) + NT],
                                          wh[:, 2 * n + k, :], wl[:, 2 * n + k, :],
                                          br_hi[:, 2 * n + k, :], br_lo[:, 2 * n + k, :], k == 0, k == 1)
                    else:
                        bank = h - M_O if kind == "out" else h % 4
                        for k in range(KT):
                            ins = mm3(ps[:, bank, NT * c_:NT * c_ + NT], wh[:, k, :], wl[:, k, :],
                                      hT_hi[:, k, :], hT_lo[:, k, :], k == 0, k == KT - 1)
                    ins.then_inc(piece_used, 1)

            def ff(hh):
                kind, ch = FFN[hh // 2]
                q = hh % 2
                if kind == "down":
                    pe.wait_ge(ff_lo, 2 * ch + q + 1)
                elif ch:
                    pe.wait_ge(ff_hid_done if kind == "up" else ff_act_done, 2 * ch - 1 + q)
                for c_ in range(2):
                    pe.wait_ge(lo_piece, 2 * (ff0 + hh) + c_ + 1)
                    _, wh, wl = piece(ff0 + hh, c_)
                    if kind == "down":
                        x = 4 * (ch % 2) + 2 * q + c_
                        first, last = (ch, q, c_) == (0, 0, 0), (ch, q, c_) == (CHUNKS - 1, 1, 1)
                        for j in range(KT):
                            ins = mm3(ps[:, 4 + j // 2, NT * (j % 2):NT * (j % 2) + NT],
                                      wh[:, 0, P * j:P * j + P], wl[:, 0, P * j:P * j + P],
                                      br_hi[:, x, :], br_lo[:, x, :], first and j % 2 == 0, last, shared=True)
                    else:
                        bank = 2 * (kind == "up") + q
                        for k in range(KT):
                            ins = mm3(ps[:, bank, NT * c_:NT * c_ + NT], wh[:, k, :], wl[:, k, :],
                                      hT_hi[:, k, :], hT_lo[:, k, :], k == 0, k == KT - 1)
                    ins.then_inc(piece_used, 1)

            for l in range(DEPTH):
                ada(l)
                stat(2 * l)
                pe.wait_ge(hank_in, 64 * (l + 1))
                mm(ps[:, 6, :], consts[:, K_FLIP:K_FLIP + P], KV[:, 2, :], start=True, stop=True)\
                    .then_inc(bias_turned, 1)
                pe.wait_ge(h_lo, 4 * l + 2)
                for h in range(M_HALVES):
                    mixer_half(l, h)
                    attention_step(l, h)
                stat(2 * l + 1)
                pe.wait_ge(h_lo, 4 * l + 4)
                if l == 0:
                    for hh in range(FFN_HALVES):
                        ff(hh)

            pe.wait_ge(router_in, 16)
            for g in range(2):
                for k in range(KT):
                    ins = mm(ps[:, 0, 8 * g:8 * g + 8], hF[:, k, tok(g)], wr[:, k, :], start=(k == 0),
                             stop=(k == KT - 1))
            ins.then_inc(lg_done, 1)
            for b in range(4):
                for k in range(4 * (b % 2), 4 * (b % 2) + 4):
                    ins = turn(ps[:, 4 + b, P * (k % 4):P * (k % 4) + P], hF[:, k, tok(b // 2)])
                ins.then_inc(h2_turned, 1)
            pe.wait_ge(mask_done, 1)
            upper = consts[:, K_UP:K_UP + P]
            mm(ps[:, 1, 0:8], upper, mask[:, 0, :], start=True, stop=True)
            mm(ps[:, 1, 8:16], ones[:, :], mask[:, 0, :], start=True, stop=False)
            mm(ps[:, 1, 8:16], upper, mask[:, 1, :], start=False, stop=True)
            mm(ps[:, 1, 16:24], ones[:, :], mask[:, 0, :], start=True, stop=False)
            mm(ps[:, 1, 16:24], ones[:, :], mask[:, 1, :], start=False, stop=True).then_inc(pos_done, 1)

            pe.wait_ge(h2_kept, 4)
            pe.wait_ge(tab_done, 1)
            n_items = pe.value_load(itab[0:1, 0:1], min_val=NEXP, max_val=ITEMS)
            xe_h = hT_hi[:, 0:4, :].rearrange("p a (b s) -> p (a b) s", b=2)
            xe_l = hT_lo[:, 0:4, :].rearrange("p a (b s) -> p (a b) s", b=2)
            hd_h = br_hi[:, 0:4, :].rearrange("p a (b s) -> p (a b) s", b=2)
            hd_l = br_lo[:, 0:4, :].rearrange("p a (b s) -> p (a b) s", b=2)

            def gather(n):
                pe.wait_ge(sel_done, n)
                for k in range(KT):
                    for t in range(2):
                        ins = mm(ps[:, 5 + k // 4, P * (k % 4):P * (k % 4) + P], h2tok[:, t, P * k:P * k + P],
                                 sel[:, t, :], start=(t == 0), stop=(t == 1))
                ins.then_inc(xe_t, 1)

            def scatter(hh, i):
                for r, bank in I_SCATTER[hh]:
                    if r == 0:
                        pe.wait_ge(y_kept, i + 1)
                        pe.wait_ge(selT_kept, i + 1)
                    if r == 3:
                        pe.wait_ge(item_added, i * 4 + 1)
                    for jj in range(2):
                        j = 2 * r + jj
                        ins = mm(ps[:, bank, NT * jj:NT * jj + NT], y_tok[:, P * j:P * j + P], selT, start=True,
                                 stop=True)
                    ins.then_inc(sc_fill, 1)

            gather(1)
            with pe.Fori(0, n_items) as i:
                pe.wait_ge(xe_lo, i + 1)
                for hh in range(FFN_HALVES):
                    kind, ch = FFN[hh // 2]
                    q = hh % 2
                    if kind == "down":
                        pe.wait_ge(e_lo, i * CHUNKS + (ch + 1))
                        if ch == q == 0:
                            pe.wait_ge(y_kept, i + 1)
                    for c_ in range(2):
                        pe.wait_ge(lo_piece, i * FFN_PIECES + (2 * (HALVES + hh) + c_ + 1))
                        _, wh, wl = item_piece(hh, c_)
                        if kind == "down":
                            k = 2 * q + c_
                            x = 4 * (ch % 2) + k
                            for n in range(2):
                                a = slice(512 * n, 512 * n + 512)
                                ins = mm3(ps[:, 3 + n, :], hd_h[:, x, :], hd_l[:, x, :], wh[:, 0, a], wl[:, 0, a],
                                          (ch, k) == (0, 0), (ch, k) == (CHUNKS - 1, 3))
                        else:
                            for kk in range(2):
                                k = 4 * q + 2 * c_ + kk
                                ins = mm3(ps[:, 1 if kind == "up" else 0, :], xe_h[:, k, :], xe_l[:, k, :],
                                          wh[:, kk, :], wl[:, kk, :], k == 0, k == KT - 1)
                        ins.then_inc(piece_used, 1)
                    if (kind == "down" and not q and ch < CHUNKS - 1) or (kind == "up" and q and ch == 0):
                        t = 0 if kind == "up" else ch + 1
                        pe.wait_ge(e_hid, i * CHUNKS + (t + 1))
                        for k in range(4):
                            ins = turn(ps[:, 2, P * k:P * k + P], ff_hid[:, 0, P * k:P * k + P])
                        ins.then_inc(e_turn, 1)
                    if hh in I_SCATTER:
                        pe.wait_ge(xe_lo, i + 1)
                        scatter(hh, i)
                    if hh == I_TURN:
                        pe.wait_ge(item_added, i * 4 + 4)
                        for t in range(2):
                            ins = turn(ps[:, 6, TOK * t:TOK * t + TOK], selg[:, t, :])
                        ins.then_inc(selT_t, 1)
                    if hh == I_GATHER:
                        pe.wait_ge(selT_kept, i + 2)
                        gather(i + 2)
            pe.wait_ge(xe_lo, n_items + 1)
            for hh in I_SCATTER:
                scatter(hh, n_items)

            pe.wait_ge(moe_done, 1)
            for b in range(4):
                for k in range(4 * (b % 2), 4 * (b % 2) + 4):
                    ins = turn(ps[:, b, P * (k % 4):P * (k % 4) + P], xT[:, k, tok(b // 2)])
                ins.then_inc(fin_t, 1)


_INS = ['x_prompt', 'x_sample', 'cache_mla_ckv', 'cache_mla_kpe', 'cache_na_k', 'cache_na_v', 'c', 'c_ctx',
        'w_ada', 'b_ada', 'g_norm1', 'w_in', 'g_qa', 'w_uq', 'g_kva', 'w_ukv', 'g_mla_q', 'g_mla_k', 'sc_w',
        'g_na_q', 'g_na_k', 'na_rpb', 'cf_w', 'cf_b', 'cf_ln_g', 'cf_ln_b', 'w_br', 'w_o', 'g_norm2',
        'w_ff_gate', 'w_ff_up', 'w_ff_down', 'w_router', 'w_e_gate', 'w_e_up', 'w_e_down']
_OUTS = [(1, 128, 1024), (1, 128, 1024), (1, 2, 128, 128), (1, 2, 128, 32), (1, 2, 128, 4, 64), (1, 2, 128, 4, 64)]


def shape_constants():
    import numpy as np
    k = np.zeros((P, K_COLS), np.float32)
    n = np.arange(P)
    k[:, K_ID:K_ID + P] = np.eye(P)
    k[:, K_UP:K_UP + P] = n[:, None] < n[None, :]
    k[:, K_IOTA:K_IOTA + P] = n[None, :]
    cq = n % GRID_W
    start = np.clip(cq - 8, 0, GRID_W - 16)
    ok = (cq[None, :] >= start[:, None]) & (cq[None, :] < start[:, None] + 16)
    k[:, K_MASK:K_MASK + P] = np.where(ok, 0.0, -1e30)
    k[n, K_FLIP + (n // 64) * 64 + 63 - cq] = 1.0
    inv = np.float32(10000.0) ** (-np.arange(8, dtype=np.float32) / np.float32(8))
    for a, pos in enumerate((n // GRID_W, n % GRID_W)):
        ang = pos.astype(np.float32)[:, None] * inv[None, :]
        k[:, K_COS + 8 * a:K_COS + 8 * a + 8] = np.cos(ang)
        k[:, K_SIN + 8 * a:K_SIN + 8 * a + 8] = np.sin(ang)
    k[0:4, K_FOLD:K_FOLD + 2] = np.array([[1, 0], [0, 1], [1, 0], [0, 1]])
    e = np.arange(8)
    k[:, K_BEFORE:K_BEFORE + 64] = (e[None, :] < e[:, None]).reshape(1, 64)
    k[:, K_EXP:K_EXP + 8] = e
    k[:, K_LEFT:K_LEFT + 8] = 8 - e
    return k


def kernel(**inputs):
    import numpy as _np
    import concourse.bacc as _bacc
    from concourse import mybir as _mybir
    from concourse.bass_utils import run_bass_kernel_spmd as _run

    nc = _bacc.Bacc("TRN2", target_bir_lowering=False, num_devices=1)
    arrays, args = {}, []
    for name in _INS + ["shape_consts"]:
        a = shape_constants() if name == "shape_consts" else _np.ascontiguousarray(inputs[name])
        arrays[f"in_{name}_dram"] = a
        args.append(nc.dram_tensor(f"in_{name}_dram", a.shape, _mybir.dt.from_np(a.dtype), kind="ExternalInput").ap())
    for i, shape in enumerate(_OUTS):
        dt = _mybir.dt.from_np(_np.dtype("float32"))
        args.append(nc.dram_tensor(f"out_{i}_dram", shape, dt, kind="ExternalOutput").ap())
    build(nc, *args)
    r = _run(nc, [arrays], core_ids=[0])
    return tuple(r.results[0][f"out_{i}_dram"] for i in range(len(_OUTS)))
```

```python
import concourse.bass as bass
from concourse import mybir
from contextlib import ExitStack

F32 = mybir.dt.float32
F32R = mybir.dt.float32r
I32 = mybir.dt.int32
ALU = mybir.AluOpType
ACT = mybir.ActivationFunctionType
AX = mybir.AxisListType

P = 128
D = 1024
KT = D // P
TOK = 128
NT = 2 * TOK
DEPTH = 2
GRID_W = 64
HEADS = 4
QL, KVL, ROPE, NOPE = 256, 128, 32, 64
QK = NOPE + ROPE
HD = 64
BW = 256
CFK, SCK = 31, 3
DFF = 3584
CHUNKS = DFF // 512
NEXP = 8
CAP = 128
OVER = 512 // (CAP + 1)
ITEMS = NEXP + OVER
EPS = 1e-6
RAW = 3
HALF = 2048
PIECE = HALF // 2
PIECES = 4

C_QA, C_SC, C_NA, C_CF, C_GATE = 0, 416, 1184, 1952, 2464

V_N1, V_N2, V_QA, V_CFB, V_LNG, V_LNB, V_SC, V_CF = 0, 8, 16, 18, 20, 22, 24, 30
V_ROWS = V_CF + 2 * CFK

K_ID, K_UP, K_IOTA, K_MASK, K_FLIP = 0, 128, 256, 384, 512
K_COS, K_SIN, K_FOLD, K_BEFORE, K_EXP, K_LEFT = 640, 656, 672, 674, 738, 746
K_COLS = 754

M_TOK, M_SC, M_CF, M_GATE, M_BR, M_O, M_HALVES = 0, 5, 8, 10, 26, 30, 34


def ffn_order():
    order = []
    for c in range(CHUNKS):
        order += [("gate", c), ("up", c)]
        if c:
            order.append(("down", c - 1))
    order.append(("down", CHUNKS - 1))
    return order


FFN = ffn_order()
FFN_HALVES = 2 * len(FFN)
FFN_PIECES = 2 * FFN_HALVES
I_SCATTER = {2: [(0, 5), (1, 6)], 4: [(2, 7), (3, 5)]}
I_TURN = 6
I_SELECT = 20
I_GATHER = 2 * FFN.index(("up", CHUNKS - 1)) + 1


MIXER = [("tok", 0, 2), ("na_qk", 0, 2), ("na_v", 0, 1), ("sc", 0, 2), ("sc", 1, 1), ("cf", 0, 2)] \
    + [("gates", c, 2) for c in range(8)] + [("branch", c, 2) for c in range(2)] + [("out", c, 2) for c in range(2)]

ADA_FIRST = 4
ADA_MIX = {21: (4,), 23: (5,), 25: (6,), 29: (7, 8), 31: (9, 10), 33: (11,)}


def plan_slots():
    slots = [("ada", 0, c, 2) for c in range(ADA_FIRST)]
    for l in range(DEPTH):
        h = -1
        for kind, i, n in MIXER:
            slots.append((kind, l, i, n))
            h += n
            if l == 0:
                slots += [("ada", 0, c, 2) for c in ADA_MIX.get(h, ())]
        if l == 0:
            ada = 0
            for kind, c in FFN:
                slots.append((kind, 0, c, 2))
                if (kind == "up" and c) or (kind == "down" and c < CHUNKS - 1):
                    slots.append(("ada", 1, ada, 2))
                    ada += 1
    return slots


SLOTS = plan_slots()
SLOT_OF = []
FIRST_HALF = []
ROLE = []
MIX, FF, ADA = [[], []], [], [[], []]
for _s, (_kind, _l, _i, _n) in enumerate(SLOTS):
    FIRST_HALF.append(len(SLOT_OF))
    for _h in range(_n):
        _phase, _halves = ("ada", ADA[_l]) if _kind == "ada" else \
            ("ff", FF) if _kind in ("gate", "up", "down") else ("mix", MIX[_l])
        ROLE.append((_phase, _l, len(_halves)))
        _halves.append(len(SLOT_OF))
        SLOT_OF.append((_s, _h))
HALVES = len(SLOT_OF)
X_STAT, X_ROOT, V_TURN = 5, 7, [3, 6]


def merged_at(h):
    first = 2 * (h - M_BR) - 2
    return range(max(first, 0), KT if h == M_O - 1 else first + 2)


def tasks_at(H, c_):
    def late(done):
        return done >= 0 and ROLE[done][0] != "ada" and ROLE[done + 1][0] == "ada" and ROLE[done] != ("mix", 0, M_O + 3)
    done = H - 2 + c_
    return [done] if done >= 0 and late(done) != bool(c_) else []


def norm_before(H):
    phase, l, n = ROLE[H]
    return None if n or phase == "ada" else 2 * l + (phase == "ff")


def build(nc, x_prompt, x_sample, cache_mla_ckv, cache_mla_kpe, cache_na_k, cache_na_v, c, c_ctx,
          w_ada, b_ada, g_norm1, w_in, g_qa, w_uq, g_kva, w_ukv, g_mla_q, g_mla_k, sc_w,
          g_na_q, g_na_k, na_rpb, cf_w, cf_b, cf_ln_g, cf_ln_b, w_br, w_o, g_norm2,
          w_ff_gate, w_ff_up, w_ff_down, w_router, w_e_gate, w_e_up, w_e_down, shape_consts,
          y_prompt, y_sample, new_ckv, new_kpe, new_na_k, new_na_v):
    with ExitStack() as ctx:
        def sb(name, shape, dt=F32):
            return ctx.enter_context(nc.sbuf_tensor(name, shape, dt))

        def sem(name):
            return ctx.enter_context(nc.semaphore(name))

        raw = sb("raw", [P, RAW, 2 * HALF])
        whi = sb("whi", [P, PIECES, PIECE], F32R)
        wlo = sb("wlo", [P, PIECES, PIECE], F32R)
        hT_hi = sb("hT_hi", [P, KT, NT], F32R)
        hT_lo = sb("hT_lo", [P, KT, NT], F32R)
        br_hi = sb("br_hi", [P, 8, NT], F32R)
        br_lo = sb("br_lo", [P, 8, NT], F32R)
        xT = sb("xT", [P, KT, NT])
        big = sb("big", [P, 8192])
        tokA = sb("tokA", [P, 2, 416])
        tokN = sb("tokN", [P, 2, 768])
        qk = sb("qk", [P, 1920])
        KV = sb("KV", [P, 3, 512])
        QT = sb("QT", [P, 2, HEADS, TOK])
        KTt = sb("KTt", [P, 3, HEADS, TOK])
        bias = sb("bias", [P, HEADS, TOK])
        consts = sb("consts", [P, K_COLS])
        ones = sb("ones", [P, P])
        wuq = sb("wuq", [P, 2, 384])
        wukv = sb("wukv", [P, 512])
        vrow = sb("vrow", [P, P])
        vecT = sb("vecT", [P, DEPTH, V_ROWS])
        badaT = sb("badaT", [P, DEPTH, 48])
        modT = sb("modT", [P, DEPTH, 48, 2])
        scaleT = sb("scaleT", [P, 2, KT, 2])
        gkv_b = sb("gkv_b", [P, KVL])
        gq_b = sb("gq_b", [P, QK])
        gk_b = sb("gk_b", [P, QK])
        gnq_b = sb("gnq_b", [P, HD])
        gnk_b = sb("gnk_b", [P, HD])
        scpad = sb("scpad", [P, 2, 2, TOK + 2])
        cfpad = sb("cfpad", [P, 2, 2, TOK + 30])
        conv = sb("conv", [P, 2, NT])
        small = sb("small", [P, 192])
        cond_hl = sb("cond_hl", [P, KT, 4], F32R)
        itab = sb("itab", [1, 16], I32)
        minus_half = sb("minus_half", [P, 1])
        ps = ctx.enter_context(nc.psum_tensor("ps", [P, 8, 512], F32))

        ident = consts[:, K_ID:K_ID + P]

        sq = big[:, 0:2048].rearrange("p (k t) -> p k t", k=KT)
        hF = big[:, 2048:4096].rearrange("p (k t) -> p k t", k=KT)
        xtok = big[:, 0:2048].rearrange("p (g d) -> p g d", g=2)
        rstd = big[:, 4096:4352]
        gates = big[:, :].rearrange("p (n j t) -> p n j t", n=4, j=8)
        bc = big[:, 6144:7168].rearrange("p (b t) -> p b t", b=4)
        cf = big[:, 7168:8192].rearrange("p (b t) -> p b t", b=4)
        ff_act = big[:, 0:1024].rearrange("p (b n) -> p b n", b=2)
        ff_hid = big[:, 1024:2048].rearrange("p (b n) -> p b n", b=2)
        h2tok = big[:, 4096:6144].rearrange("p (g d) -> p g d", g=2)
        fT = big[:, 6144:8192].rearrange("p (k t) -> p k t", k=KT)
        y_tok = big[:, 2048:3072]
        sel = big[:, 3072:3328].rearrange("p (t s) -> p t s", t=2)
        selg = big[:, 3328:3584].rearrange("p (t s) -> p t s", t=2)
        selT = big[:, 3584:3840]
        arow = qk[0:4, 0:1024].rearrange("p (a n) -> p a n", a=2)
        Q = qk[:, 0:768].rearrange("p (g h d) -> p g h d", g=2, h=HEADS)
        Kn = qk[:, 768:1920].rearrange("p (s h d) -> p s h d", s=3, h=HEADS)
        heads_sq = qk[:, 768:1536]
        Pr = qk[:, 0:1536].rearrange("p (s h d) -> p s h d", s=3, h=HEADS)
        QTf = QT[:, :, :, :].rearrange("p g h t -> p (g h t)")
        KTf = KTt[:, :, :, :].rearrange("p s h t -> p (s h t)")
        qaT = QTf[:, 0:512].rearrange("p (a t) -> p a t", a=2)
        ckvT = KTf[:, 0:384]
        sbias = KV[:, 0, :]
        O = tokA[:, :, 0:256]
        ckc = qk[:, 1536:1664]
        kpc = small[:, 128:160]
        nakc = KV[:, 1, 0:256]
        navc = KV[:, 1, 256:512]
        ropet = big[:, 1024:1536].rearrange("p (a n) -> p a n", a=8)
        hank = KV[:, 2, :].rearrange("p (h k) -> p h k", h=HEADS)
        na_sq = big[:, 0:1024].rearrange("p (g d) -> p g d", g=2)
        ln_sq = QTf[:, 0:512]
        ln_sd = QTf[:, 512:768]
        wr = qk[:, 0:64].rearrange("p (k e) -> p k e", k=KT)
        lg = qk[:, 64:80].rearrange("p (g e) -> p g e", g=2)
        lg2 = qk[:, 80:96].rearrange("p (g e) -> p g e", g=2)
        oh1 = qk[:, 96:112].rearrange("p (g e) -> p g e", g=2)
        oh2 = qk[:, 112:128].rearrange("p (g e) -> p g e", g=2)
        tmp = qk[:, 128:144].rearrange("p (g e) -> p g e", g=2)
        tq = qk[:, 144:160]
        ov = qk[:, 168:176]
        rank = qk[:, 176:184]
        mask = qk[:, 1010:1026].rearrange("p (g e) -> p g e", g=2)
        ohk = qk[:, 184:184 + 8 * OVER].rearrange("p (k e) -> p k e", k=OVER)
        w64 = qk[:, 300:364].rearrange("p (a e) -> p a e", a=8)
        tab = qk[:, 400:400 + 6 * (ITEMS + 1)].rearrange("p (q t i) -> p q t i", q=3, t=2)
        wide = qk[:, 600:600 + 16 * OVER].rearrange("p (t k e) -> p t k e", t=2, k=OVER)
        eidx = qk[:, 900:900 + OVER + 2]
        stage = qk[:, 1000:1006].rearrange("p (q t) -> p q t", q=3)

        raw_landed = [sem(f"raw_landed{i}") for i in range(RAW)]
        (hi_piece, lo_piece, piece_used, consts_in, x_in, cond_in, vrow_in, small_in,
         nacache_in, cache_in, router_in, setup, pool_pow, dve_link, cond_turned, cond_th, cond_ready, cond_hi,
         cond_lo, v_turned, v_kept, x_turned, x_kept, ada_kept, ada_folded, mod_kept,
         sq_done, stat_done, ms_done, sd_done, hF_done, h_hi, h_lo, drained, xv_read,
         proj_read, pair_sum, merged_f, merged_hi, merged_lo, wo_read) = map(sem, (
             "hi_piece lo_piece piece_used consts_in x_in cond_in vrow_in small_in "
             "nacache_in cache_in router_in setup pool_pow dve_link cond_turned cond_th cond_ready cond_hi "
             "cond_lo v_turned v_kept x_turned x_kept ada_kept ada_folded mod_kept "
             "sq_done stat_done ms_done sd_done hF_done h_hi h_lo drained xv_read "
             "proj_read pair_sum merged_f merged_hi merged_lo wo_read").split())
        (stats_in, squared, qa_normed, na_ready, hank_in, bias_turned, bias_kept, latent_turned, latent_kept,
         qkv_done, qkv_kept, qk_ready, heads_turned, heads_kept, scores_done, max_done, exp_done,
         probs_turned, probs_kept, o_done, o_scaled, o_turned, o_hi, o_lo, b_ready, b_hi, b_lo, cf_used,
         conv_v, conv_ready, ln_sum, ln_sq_done, ln_sqsum, ln_ms, ln_sdone, ln_z, ln_th, ln_o, d_hi, d_lo,
         stored) = map(sem, (
             "stats_in squared qa_normed na_ready hank_in bias_turned bias_kept latent_turned latent_kept "
             "qkv_done qkv_kept qk_ready heads_turned heads_kept scores_done max_done exp_done "
             "probs_turned probs_kept o_done o_scaled o_turned o_hi o_lo b_ready b_hi b_lo cf_used "
             "conv_v conv_ready ln_sum ln_sq_done ln_sqsum ln_ms ln_sdone ln_z ln_th ln_o d_hi d_lo "
             "stored").split())
        (ff_act_done, ff_hid_done, ff_hi, ff_lo, ff_read, lg_done, h2_turned, h2_kept,
         mask_done, pos_done, tab_done, staged, sel_done, selT_t, selT_kept, xe_t, xe_hi, xe_lo,
         e_act, e_hid, e_turn, e_hi, e_lo, y_kept, sc_fill, moe_done, fin_t, fin_kept, pair_exp, item_added,
         y_cleared, sum_cleared, y_stored) = map(sem, (
             "ff_act_done ff_hid_done ff_hi ff_lo ff_read lg_done h2_turned h2_kept "
             "mask_done pos_done tab_done staged sel_done selT_t selT_kept xe_t xe_hi xe_lo "
             "e_act e_hid e_turn e_hi e_lo y_kept "
             "sc_fill moe_done fin_t fin_kept pair_exp item_added y_cleared sum_cleared y_stored").split())

        def cols(w, l, a, n):
            return w[l, :, a:a + n].rearrange("(k p) n -> p k n", p=P)

        def slot_parts(kind, l, i):
            if kind == "ada":
                return (8, 512), cols(w_ada, l, 512 * i, 512)
            if kind == "tok":
                return (8, 416), cols(w_in, l, C_QA, 416)
            if kind == "na_qk":
                return (8, 512), cols(w_in, l, C_NA, 512)
            if kind == "na_v":
                return (8, 256), cols(w_in, l, C_NA + 512, 256)
            if kind == "sc":
                return (8, 256 if i else 512), cols(w_in, l, C_SC + 512 * i, 256 if i else 512)
            if kind == "cf":
                return (8, 512), cols(w_in, l, C_CF, 512)
            if kind == "gates":
                return (8, 512), cols(w_in, l, C_GATE + 512 * i, 512)
            if kind == "branch":
                return (8, 512), w_br[l].rearrange("n (k p) d -> p (n k) d", p=P)[:, :, 512 * i:512 * i + 512]
            if kind == "out":
                return (8, 512), cols(w_o, l, 512 * i, 512)
            if kind == "gate":
                return (8, 512), cols(w_ff_gate, 0, 512 * i, 512)
            if kind == "up":
                return (8, 512), cols(w_ff_up, 0, 512 * i, 512)
            return (4, 1024), w_ff_down[0, 512 * i:512 * i + 512, :].rearrange("(k p) n -> p k n", p=P)

        def piece_views(kind, i, h, c_, raw_slot, buf, item=False):
            width = {"tok": 416, "na_v": 256, "down": 1024}.get(kind, 256 if kind == "sc" and i else 512)
            depth = 4 if kind == "down" else 8
            whole = raw[:, raw_slot, 0:depth * width].rearrange("p (k n) -> p k n", k=depth)
            n = 2 * h + c_
            if kind == "down":
                k, w, part = 1, 1024, whole[:, n:n + 1, :]
            elif kind in ("ada", "tok", "na_qk") or item:
                k, w, part = 2, width, whole[:, 2 * n:2 * n + 2, :]
            else:
                k, w, part = 8, P, whole[:, :, P * n:P * n + P]
            return (part,) + tuple(x[:, buf, 0:k * w].rearrange("p (k n) -> p k n", k=k) for x in (whi, wlo))

        def piece(H, c_):
            s, h = SLOT_OF[H]
            kind, _, i, _ = SLOTS[s]
            return piece_views(kind, i, h, c_, s % RAW, (2 * H + c_) % PIECES)

        def item_piece(hh, c_):
            kind, _ = FFN[hh // 2]
            return piece_views(kind, 0, hh % 2, c_, (len(SLOTS) + hh // 2) % RAW,
                               (2 * (HALVES + hh) + c_) % PIECES, item=True)

        def filled(l, f):
            return 2 * (MIX[l][1 if f < 2 else 3 if f < 4 else f] + 1)

        def ada_banks(l, c_):
            if l:
                return c_ % 2, 2 + c_ % 2
            return 2 * ((7, 4, 5, 6)[c_] if c_ < ADA_FIRST else 4 if c_ % 2 else 7,)

        def vector_bank(m):
            return (1, 2, 5, 6)[m]

        def ff_used(kind, ch):
            return 2 * (FF[2 * FFN.index((kind, ch)) + 1] + 1)

        block = ctx.enter_context(nc.Block())

        @block.sync
        def _(sp):
            sp.dma_start(consts[:, :], shape_consts).then_inc(consts_in, 16)
            sp.dma_start(vrow[0:8, :], c_ctx.rearrange("(k p) -> k p", p=P)).then_inc(cond_in, 16)
            sp.dma_start(vrow[8:16, :], c[0].rearrange("(k p) -> k p", p=P)).then_inc(cond_in, 16)
            for s, (kind, l, i, n) in enumerate(SLOTS):
                (k, w), src = slot_parts(kind, l, i)
                if s >= RAW:
                    sp.wait_ge(lo_piece, 2 * (FIRST_HALF[s - RAW] + SLOTS[s - RAW][3]))
                dst = raw[:, s % RAW, 0:k * w].rearrange("p (k n) -> p k n", k=k)
                sp.dma_start(dst, src).then_inc(raw_landed[s % RAW], 16)
                if s == 0:
                    sp.dma_start(xtok[:, 0, :], x_prompt[0]).then_inc(x_in, 16)
                    sp.dma_start(xtok[:, 1, :], x_sample[0]).then_inc(x_in, 16)

            def item_loads(e, done):
                for j, (kind, ch) in enumerate(FFN):
                    if kind == "down":
                        src = w_e_down[0, bass.ds(e, 1), 512 * ch:512 * ch + 512, :].rearrange(
                            "a (k p) n -> p (a k) n", p=P)
                        k = 4
                    else:
                        w = w_e_gate if kind == "gate" else w_e_up
                        src = w[0, bass.ds(e, 1), :, 512 * ch:512 * ch + 512].rearrange(
                            "a (k p) n -> p (a k) n", p=P)
                        k = 8
                    slot = (len(SLOTS) + j) % RAW
                    sp.wait_ge(lo_piece, done + 2 * (HALVES + 2 * (j - RAW + 1)))
                    sp.dma_start(raw[:, slot, :].rearrange("p (k n) -> p k n", k=k), src)\
                        .then_inc(raw_landed[slot], 16)

            with sp.Fori(0, NEXP) as i:
                item_loads(i, i * FFN_PIECES)
            sp.wait_ge(tab_done, 1)
            n_over = sp.value_load(itab[0:1, 1:2], min_val=0, max_val=OVER)
            with sp.If(n_over > 0):
                with sp.Fori(0, n_over) as j:
                    e = sp.value_load(itab[0:1, bass.ds(j + 2, 1)], min_val=0, max_val=NEXP - 1)
                    item_loads(e, (j + NEXP) * FFN_PIECES)
            sp.wait_ge(fin_kept, 4)
            sp.dma_start(y_prompt[0], xtok[:, 0, :]).then_inc(y_stored, 16)
            sp.dma_start(y_sample[0], xtok[:, 1, :]).then_inc(y_stored, 16)
            sp.wait_ge(y_stored, 32)
            sp.wait_ge(stored, 64 * DEPTH)

        @block.gpsimd
        def _(pool):
            pool.memset(ones[:, :], 1.0).then_inc(setup, 1)
            pool.memset(minus_half[:, :], -0.5).then_inc(setup, 1)
            pool.memset(scpad[:, :, :, :], 0.0).then_inc(setup, 1)
            pool.memset(cfpad[:, :, :, :], 0.0).then_inc(setup, 1)

            def load_vectors(l):
                for src, at, n in ((g_norm1[l], V_N1, 8), (g_norm2[l], V_N2, 8), (g_qa[l], V_QA, 2),
                                   (cf_b[l], V_CFB, 2), (cf_ln_g[l], V_LNG, 2), (cf_ln_b[l], V_LNB, 2)):
                    pool.dma_start(vrow[at:at + n, :], src.rearrange("(k p) -> k p", p=P)).then_inc(vrow_in, 16)
                pool.dma_start(vrow[V_SC:V_SC + 2 * SCK, :], sc_w[l].rearrange("a (k p) -> (a k) p", p=P))\
                    .then_inc(vrow_in, 16)
                pool.dma_start(vrow[V_CF:V_ROWS, :], cf_w[l].rearrange("a (k p) -> (a k) p", p=P))\
                    .then_inc(vrow_in, 16)

            def load_bada(l):
                pool.wait_ge(v_turned, 2 * l + 1)
                pool.dma_start(vrow[0:48, :], b_ada[l].rearrange("(k p) -> k p", p=P)).then_inc(vrow_in, 16)

            pool.wait_ge(cond_turned, 1)
            load_vectors(0)
            load_bada(0)

            for l in range(DEPTH):
                if l:
                    pool.wait_ge(piece_used, 2 * (MIX[l - 1][-1] + 1))
                for dst, src in ((wuq[:, :, :], w_uq[l].rearrange("(k p) n -> p k n", p=P)),
                                 (wukv[:, :], w_ukv[l]),
                                 (gkv_b[:, :], g_kva[l].partition_broadcast(P)),
                                 (gq_b[:, :], g_mla_q[l].partition_broadcast(P)),
                                 (gk_b[:, :], g_mla_k[l].partition_broadcast(P)),
                                 (gnq_b[:, :], g_na_q[l].partition_broadcast(P)),
                                 (gnk_b[:, :], g_na_k[l].partition_broadcast(P))):
                    pool.dma_start(dst, src).then_inc(small_in, 16)
                pool.dma_start(ckc, cache_mla_ckv[0, l]).then_inc(cache_in, 16)
                pool.dma_start(kpc, cache_mla_kpe[0, l]).then_inc(cache_in, 16)
                for rq in range(2):
                    for rk in range(2):
                        src = bass.AP(na_rpb.tensor, l * 1860 + (rk - rq + 7) * 31 + 15 - (GRID_W - 1),
                                      [[1, GRID_W], [465, HEADS], [1, GRID_W]])
                        pool.dma_start(hank[rq * 64:rq * 64 + 64, :, rk * 64:rk * 64 + 64], src)\
                            .then_inc(hank_in, 16)
                if l == 0:
                    pool.wait_ge(v_turned, 2)
                    load_vectors(1)
                    pool.wait_ge(setup, 2)
                pool.wait_ge(stats_in, 3 * l + 1)
                pool.tensor_tensor(small[:, 0:4], small[:, 0:4], minus_half[:, :].to_broadcast([P, 4]),
                                   ALU.pow).then_inc(pool_pow, 1)
                pool.wait_ge(qa_normed, l + 1)
                pool.dma_start(new_ckv[0, l], tokA[:, 0, 256:384]).then_inc(stored, 16)
                pool.dma_start(new_kpe[0, l], tokA[:, 0, 384:416]).then_inc(stored, 16)
                pool.wait_ge(stats_in, 3 * l + 2)
                pool.tensor_tensor(small[:, 8:28], small[:, 8:28], minus_half[:, :].to_broadcast([P, 20]),
                                   ALU.pow).then_inc(pool_pow, 1)
                if l == 0:
                    load_bada(1)
                pool.wait_ge(stats_in, 3 * l + 3)
                pool.tensor_tensor(small[:, 32:48], small[:, 32:48], minus_half[:, :].to_broadcast([P, 16]),
                                   ALU.pow).then_inc(pool_pow, 1)
                pool.wait_ge(na_ready, l + 1)
                pool.dma_start(new_na_k[0, l].rearrange("s h d -> s (h d)"), tokN[:, 0, 256:512])\
                    .then_inc(stored, 16)
                pool.dma_start(new_na_v[0, l].rearrange("s h d -> s (h d)"), tokN[:, 0, 512:768])\
                    .then_inc(stored, 16)
                pool.wait_ge(o_done, 2 * l + 1)
                pool.dma_start(nakc, cache_na_k[0, l].rearrange("s h d -> s (h d)")).then_inc(nacache_in, 16)
                pool.dma_start(navc, cache_na_v[0, l].rearrange("s h d -> s (h d)")).then_inc(nacache_in, 16)
                for j in range(KT):
                    pool.wait_ge(proj_read, 8 * l + j + 1)
                    pool.tensor_tensor(gates[:, 0:2, j, :], gates[:, 0:2, j, :], gates[:, 2:4, j, :], ALU.add)\
                        .then_inc(pair_sum, 1)
                    pool.wait_ge(pair_sum, 8 * l + j + 1)
                    pool.tensor_tensor(gates[:, 0, j, :], gates[:, 0, j, :], gates[:, 1, j, :], ALU.add)\
                        .then_inc(merged_f, 1)
            pool.wait_ge(piece_used, 2 * (MIX[-1][-1] + 1))
            pool.memset(fT, 0.0).then_inc(sum_cleared, 1)
            pool.dma_start(wr, w_router[0].rearrange("(k p) e -> p k e", p=P)).then_inc(router_in, 16)

        @block.scalar
        def _(act):
            def flat2(a):
                return a.rearrange("p a b -> p (a b)")

            def flat3(a):
                return a.rearrange("p a b c -> p (a b c)")

            def hi(H, c_):
                s, _ = SLOT_OF[H]
                act.wait_ge(raw_landed[s % RAW], 16 * (s // RAW + 1))
                part, h, _ = piece(H, c_)
                if 2 * H + c_ >= PIECES:
                    act.wait_ge(piece_used, 2 * H + c_ - PIECES + 1)
                act.activation(h, part, ACT.Copy).then_inc(hi_piece, 1)

            act.wait_ge(cond_turned, 1)
            act.activation(small[:, 64:80], ps[:, 7, 0:16], ACT.Tanh, scale=0.5).then_inc(cond_th, 1)
            act.wait_ge(cond_ready, 1)
            act.activation(cond_hl[:, :, 0:2], small[:, 80:96].rearrange("p (g k) -> p k g", g=2), ACT.Copy)\
                .then_inc(cond_hi, 1)

            def keep_x():
                for b in range(4):
                    act.wait_ge(x_turned, b + 1)
                    act.activation(flat2(xT[:, 2 * b:2 * b + 2, :]), ps[:, b, :], ACT.Copy).then_inc(x_kept, 1)

            def square(p):
                act.activation(sq[:, 2 * p:2 * p + 2, :], xT[:, 2 * p:2 * p + 2, :], ACT.Square).then_inc(sq_done, 1)

            def norm_root(n):
                act.wait_ge(ms_done, n + 1)
                act.activation(rstd, rstd, ACT.Sqrt).then_inc(sd_done, 1)

            def norm_hi(n):
                for p in range(4):
                    act.wait_ge(hF_done, 4 * n + p + 1)
                    act.activation(hT_hi[:, 2 * p:2 * p + 2, :], hF[:, 2 * p:2 * p + 2, :], ACT.Copy)\
                        .then_inc(h_hi, 1)

            def keep_vectors(m):
                dst, n = (badaT[:, m // 2, :], 48) if m % 2 else (vecT[:, m // 2, :], V_ROWS)
                act.wait_ge(v_turned, m + 1)
                act.activation(dst, ps[:, vector_bank(m), 0:n], ACT.Copy).then_inc(v_kept, 1)

            def ada_task(l, n):
                c_, q = divmod(n, 2)
                if q:
                    act.wait_ge(piece_used, 2 * (ADA[l][n] + 1))
                    if c_ >= 2:
                        act.wait_ge(ada_folded, 12 * l + c_ - 1)
                    elif l:
                        act.wait_ge(ada_folded, 12)
                    act.activation(arow[:, c_ % 2, :], ps[0:4, ada_banks(l, c_)[0], :], ACT.Copy)\
                        .then_inc(ada_kept, 1)

            def evac(l, f, dst, func=ACT.Copy, n=512, scale=1.0):
                act.wait_ge(piece_used, filled(l, f))
                act.activation(dst, ps[:, f % 4, 0:n], func, scale=scale).then_inc(drained, 1)

            def squares(dst, src, kept):
                act.wait_ge(drained, kept)
                act.activation(dst, src, ACT.Square).then_inc(squared, 1)

            def keep_heads(u, d, first):
                act.wait_ge(heads_turned, 2 * u + (1 if first else 2))
                if first:
                    for g in range(2):
                        act.activation(QTf[0:d, 512 * g:512 * g + 512], ps[0:d, 4 + g, :], ACT.Copy)\
                            .then_inc(heads_kept, 1)
                    for s in range(2):
                        act.activation(KTf[0:d, 512 * s:512 * s + 512], ps[0:d, 6 + s, :], ACT.Copy)\
                            .then_inc(heads_kept, 1)
                else:
                    act.activation(KTf[0:d, 1024:1536], ps[0:d, 4, :], ACT.Copy).then_inc(heads_kept, 1)

            def exps(u, scale):
                act.wait_ge(max_done, u + 1)
                for s in range(3):
                    for h in range(HEADS):
                        b = HEADS * s + h
                        src = sbias[:, TOK * h:TOK * h + TOK] if u % 2 and s == 1 else \
                            ps[:, 5 + s, TOK * h:TOK * h + TOK]
                        act.activation(Pr[:, s, h, :], src, ACT.Exp, bias=small[:, 60 + b:61 + b], scale=scale,
                                       accum_out=small[:, 76 + b:77 + b]).then_inc(exp_done, 1)

            def keep_probs(u):
                act.wait_ge(probs_turned, u + 1)
                for s in range(3):
                    act.activation(KTf[:, 512 * s:512 * s + 512], ps[:, 5 + s, :], ACT.Copy)\
                        .then_inc(probs_kept, 1)

            def out_hi(u):
                act.wait_ge(o_turned, u + 1)
                act.activation(flat2(br_hi[:, 4 * (u % 2):4 * (u % 2) + 2, :]), ps[:, 4, :], ACT.Copy)\
                    .then_inc(o_hi, 1)

            def mixer_task(l, h):
                if h == 1:
                    for g in range(2):
                        evac(l, g, tokA[:, g, :], n=416)
                    squares(qk[:, 0:768].rearrange("p (g d) -> p g d", g=2), tokA[:, :, 0:384], 25 * l + 2)
                if h == 3:
                    for g in range(2):
                        evac(l, 2 + g, tokN[:, g, 0:512])
                    act.wait_ge(latent_turned, l + 1)
                    for k in range(2):
                        act.activation(qaT[:, k, :], ps[:, 4, 256 * k:256 * k + 256], ACT.Copy,
                                       scale=vecT[:, l, V_QA + k:V_QA + k + 1]).then_inc(latent_kept, 1)
                    act.activation(ckvT, ps[:, 5, 0:384], ACT.Copy).then_inc(latent_kept, 1)
                if h == 4:
                    evac(l, 4, tokN[:, :, 512:768])
                    act.wait_ge(qkv_done, 2 * l + 1)
                    for g in range(2):
                        act.activation(qk[:, 384 * g:384 * g + 384], ps[:, 6 + g, 0:384], ACT.Copy)\
                            .then_inc(qkv_kept, 1)
                    for s in range(2):
                        act.activation(KV[:, s, :], ps[:, 4 + s, :], ACT.Copy).then_inc(qkv_kept, 1)
                    act.wait_ge(qkv_kept, 5 * l + 2)
                    act.activation(heads_sq, qk[:, 0:768], ACT.Square).then_inc(squared, 1)
                if h == 5:
                    act.wait_ge(qkv_done, 2 * l + 2)
                    act.activation(KV[:, 2, :], ps[:, 4, :], ACT.Copy).then_inc(qkv_kept, 1)
                    squares(na_sq, tokN[:, :, 0:512], 25 * l + 4)
                if h in (5, 6):
                    evac(l, h, flat2(bc[:, 2 * (h - 5):2 * (h - 5) + 2, :]))
                if h == 8:
                    evac(l, 8, flat2(cf[:, 0:2, :]))
                    keep_heads(2 * l, QK, True)
                if h == 9:
                    evac(l, 9, flat2(cf[:, 2:4, :]), ACT.Tanh, scale=0.5)
                    keep_heads(2 * l, QK, False)
                if M_GATE <= h < M_BR:
                    n, j = divmod(2 * (h - M_GATE), 8)
                    if h == M_GATE:
                        act.wait_ge(stats_in, 3 * l + 3)
                    if h == M_GATE + 12:
                        act.wait_ge(b_lo, l + 1)
                        act.wait_ge(cf_used, l + 1)
                    evac(l, h, flat2(gates[:, n, j:j + 2, :]), ACT.Tanh, scale=0.5)
                if h == 11:
                    exps(2 * l, QK ** -0.5)
                if h == 12:
                    keep_probs(2 * l)
                    act.wait_ge(b_ready, l + 1)
                    act.activation(br_hi[:, 2:4, :], bc[:, 0:2, :], ACT.Copy).then_inc(b_hi, 1)
                if h == 14:
                    out_hi(2 * l)
                if h == 15:
                    keep_heads(2 * l + 1, HD, True)
                if h == 16:
                    keep_heads(2 * l + 1, HD, False)
                if h == 18:
                    exps(2 * l + 1, 1.0)
                if h == 19:
                    keep_probs(2 * l + 1)
                if h == 21:
                    out_hi(2 * l + 1)
                if h == 22:
                    act.wait_ge(ln_ms, l + 1)
                    act.activation(ln_sd, ln_sd, ACT.Sqrt).then_inc(ln_sdone, 1)
                if h == 24:
                    act.wait_ge(ln_z, l + 1)
                    act.activation(ln_sq, flat2(conv[:, :, :]), ACT.Tanh, scale=0.5).then_inc(ln_th, 1)
                    act.wait_ge(ln_o, l + 1)
                    act.activation(flat2(br_hi[:, 6:8, :]), ln_sq, ACT.Copy, scale=0.5).then_inc(d_hi, 1)
                if l == 0 and h in (6, 14):
                    keep_vectors(3 if h == 14 else 2)
                if h > M_O:
                    for p in ((h - M_O - 1,) if h < M_HALVES - 1 else (2, 3)):
                        act.wait_ge(wo_read, 4 * l + p + 1)
                        square(p)
                if M_BR <= h < M_O:
                    for j in merged_at(h):
                        act.wait_ge(merged_f, 8 * l + j + 1)
                        act.activation(hT_hi[:, j, :], gates[:, 0, j, :], ACT.Copy, scale=0.5)\
                            .then_inc(merged_hi, 1)

            def ff_task(hh):
                kind, ch = FFN[hh // 2]
                q = hh % 2
                if kind == "gate":
                    act.wait_ge(piece_used, 2 * (FF[hh] + 1))
                    if ch:
                        act.wait_ge(ff_hid_done, 2 * ch - 1 + q)
                    act.activation(ff_act[:, q, :], ps[:, q, :], ACT.Silu).then_inc(ff_act_done, 1)
                if kind == "up":
                    act.wait_ge(ff_hid_done, 2 * ch + q + 1)
                    if ch >= 2:
                        act.wait_ge(piece_used, ff_used("down", ch - 2))
                    a = 4 * (ch % 2) + 2 * q
                    act.activation(flat2(br_hi[:, a:a + 2, :]), ff_hid[:, q, :], ACT.Copy)\
                        .then_inc(ff_hi, 1)
                if hh == FFN_HALVES - 1:
                    for p in range(4):
                        act.wait_ge(ff_read, p + 1)
                        square(p)

            def task(H):
                phase, l, n = ROLE[H]
                if phase == "ada":
                    ada_task(l, n)
                elif phase == "mix":
                    mixer_task(l, n)
                else:
                    ff_task(n)

            for H in range(HALVES):
                for c_ in range(2):
                    hi(H, c_)
                    for done in tasks_at(H, c_):
                        task(done)
                if H == 1:
                    keep_x()
                if H in (2, 3):
                    act.wait_ge(x_kept, 4)
                    for p in (2 * H - 4, 2 * H - 3):
                        square(p)
                if H == X_ROOT:
                    norm_root(0)
                if H == V_TURN[0] + 2:
                    keep_vectors(0)
                n = norm_before(H)
                if n is not None:
                    if n == 0:
                        keep_vectors(1)
                    else:
                        norm_root(n)
                    norm_hi(n)
                    if n % 2 == 0:
                        act.wait_ge(bias_turned, n // 2 + 1)
                        act.activation(bias[:, :, :].rearrange("p h k -> p (h k)"), ps[:, 6, :], ACT.Copy)\
                            .then_inc(bias_kept, 1)
                    if n == 2:
                        act.wait_ge(stored, 64)
            task(HALVES - 1)
            norm_root(3)
            act.wait_ge(hF_done, 16)
            for n, b in enumerate((0, 2, 1, 3)):
                act.wait_ge(h2_turned, n + 1)
                act.activation(h2tok[:, b // 2, 512 * (b % 2):512 * (b % 2) + 512], ps[:, 4 + b, :], ACT.Copy)\
                    .then_inc(h2_kept, 1)

            act.wait_ge(mask_done, 1)
            act.activation(tq[:, 4:6], tq[:, 4:6], ACT.Exp).then_inc(pair_exp, 1)

            def gathered_hi(n):
                act.wait_ge(xe_t, n)
                act.activation(flat2(hT_hi[:, 0:4, :]), flat2(ps[:, 5:7, :]), ACT.Copy).then_inc(xe_hi, 1)

            gathered_hi(1)
            act.wait_ge(tab_done, 1)
            n_items = act.value_load(itab[0:1, 0:1], min_val=NEXP, max_val=ITEMS)

            def keep_y(i):
                act.wait_ge(piece_used, i * FFN_PIECES + 2 * HALVES)
                act.activation(y_tok, flat2(ps[:, 3:5, :]), ACT.Copy).then_inc(y_kept, 1)

            act.wait_ge(y_cleared, 1)
            with act.Fori(0, n_items) as i:
                def item_hi(hh):
                    slot = len(SLOTS) + hh // 2
                    act.wait_ge(raw_landed[slot % RAW], i * (16 * len(FFN) // RAW) + 16 * (slot // RAW + 1))
                    for c_ in range(2):
                        part, h, _ = item_piece(hh, c_)
                        act.wait_ge(piece_used, i * FFN_PIECES + (2 * (HALVES + hh) + c_ - PIECES + 1))
                        act.activation(h, part, ACT.Copy).then_inc(hi_piece, 1)

                def item_task(hh):
                    kind, ch = FFN[hh // 2]
                    if kind == "gate" and hh % 2:
                        act.wait_ge(piece_used, i * FFN_PIECES + 2 * (HALVES + hh + 1))
                        act.activation(ff_act[:, 0, :], ps[:, 0, :], ACT.Silu).then_inc(e_act, 1)
                    if (kind == "down" and hh % 2 == 0 and ch < CHUNKS - 1) or (kind == "up" and hh % 2 and ch == 0):
                        t = 0 if kind == "up" else ch + 1
                        act.wait_ge(e_turn, i * CHUNKS + (t + 1))
                        a = 2 * (t % 2)
                        if t >= 2:
                            act.wait_ge(piece_used, i * FFN_PIECES + 2 * (HALVES + 2 * FFN.index(("down", t - 2)) + 2))
                        act.activation(flat2(br_hi[:, a:a + 2, :]), ps[:, 2, :], ACT.Copy).then_inc(e_hi, 1)

                for hh in range(FFN_HALVES):
                    item_hi(hh)
                    if hh:
                        item_task(hh - 1)
                    if hh == 1:
                        keep_y(i)
                    if hh == I_TURN + 1:
                        act.wait_ge(selT_t, i + 1)
                        act.activation(selT, ps[:, 6, 0:256], ACT.Copy).then_inc(selT_kept, 1)
                    if hh == I_GATHER + 1:
                        gathered_hi(i + 2)
            keep_y(n_items)

            for b in range(4):
                act.wait_ge(fin_t, b + 1)
                act.activation(xtok[:, b // 2, 512 * (b % 2):512 * (b % 2) + 512], ps[:, b, :], ACT.Copy)\
                    .then_inc(fin_kept, 1)

        @block.vector
        def _(dve):
            links = [0]

            def link(ins):
                links[0] += 1
                ins.then_inc(dve_link, 1)
                dve.wait_ge(dve_link, links[0])

            tt, ts, stt = dve.tensor_tensor, dve.tensor_scalar, dve.scalar_tensor_tensor

            def lo(H, c_):
                part, h, w = piece(H, c_)
                dve.wait_ge(hi_piece, 2 * H + c_ + 1)
                tt(w, part, h.bitcast(F32), ALU.subtract).then_inc(lo_piece, 1)

            dve.wait_ge(cond_th, 1)
            link(ts(small[:, 64:80], small[:, 64:80], 0.5, 0.5, ALU.mult, ALU.add))
            tt(small[:, 80:96], small[:, 64:80], ps[:, 7, 0:16], ALU.mult).then_inc(cond_ready, 1)
            dve.wait_ge(cond_hi, 1)
            tt(cond_hl[:, :, 2:4], small[:, 80:96].rearrange("p (g k) -> p k g", g=2),
               cond_hl[:, :, 0:2].bitcast(F32), ALU.subtract).then_inc(cond_lo, 1)

            def keep_modulation(l, c_):
                dve.wait_ge(ada_folded, 12 * l + c_ + 1)
                dve.wait_ge(v_kept, 2 * l + 2)
                tt(modT[:, l, 4 * c_:4 * c_ + 4, :],
                   ps[:, ada_banks(l, c_)[1], 0:8].rearrange("p (m g) -> p m g", g=2),
                   badaT[:, l, 4 * c_:4 * c_ + 4].unsqueeze(2).to_broadcast([P, 4, 2]), ALU.add).then_inc(mod_kept, 1)

            def norm_mean(n):
                dve.wait_ge(stat_done, n + 1)
                ts(rstd, ps[:, 0, 0:256], 1.0 / D, EPS, ALU.mult, ALU.add).then_inc(ms_done, 1)

            def norm_apply(n):
                l, s = divmod(n, 2)
                dve.wait_ge(mod_kept, 12 * l + (12 if n else ADA_FIRST))
                stt(scaleT[:, s, :, :], modT[:, l, 24 * s + 8:24 * s + 16, :], 1.0,
                    vecT[:, l, V_N2 if s else V_N1:(V_N2 if s else V_N1) + 8].unsqueeze(2).to_broadcast([P, 8, 2]),
                    ALU.add, ALU.mult)
                dve.wait_ge(sd_done, n + 1)
                link(dve.reciprocal(rstd, rstd))
                for k in range(0, KT + 2, 2):
                    if k < KT:
                        link(tt(hF[:, k:k + 2, :], xT[:, k:k + 2, :], rstd.unsqueeze(1).to_broadcast([P, 2, NT]),
                                ALU.mult))
                        for kk in range(k, k + 2):
                            for g in range(2):
                                part = hF[:, kk, TOK * g:TOK * g + TOK]
                                ins = ts(part, part, scaleT[:, s, kk, g:g + 1], modT[:, l, 24 * s + kk, g:g + 1],
                                         ALU.mult, ALU.add)
                        ins.then_inc(hF_done, 1)
                    if k and n < 3:
                        dve.wait_ge(h_hi, 4 * n + k // 2)
                        tt(hT_lo[:, k - 2:k, :], hF[:, k - 2:k, :], hT_hi[:, k - 2:k, :].bitcast(F32),
                           ALU.subtract).then_inc(h_lo, 1)

            def wide_col(a, n):
                return a.unsqueeze(2).to_broadcast([P, a.shape[1], n])

            def latents(l):
                dve.wait_ge(squared, 3 * l + 1)
                s = qk[:, 0:768].rearrange("p (g d) -> p g d", g=2)
                dve.tensor_reduce(small[:, 0:2], s[:, :, 0:256], AX.X, ALU.add)
                link(dve.tensor_reduce(small[:, 2:4], s[:, :, 256:384], AX.X, ALU.add))
                ts(small[:, 0:2], small[:, 0:2], 1.0 / QL, EPS, ALU.mult, ALU.add)
                ts(small[:, 2:4], small[:, 2:4], 1.0 / KVL, EPS, ALU.mult, ALU.add).then_inc(stats_in, 1)
                dve.wait_ge(pool_pow, 3 * l + 1)
                tt(tokA[:, :, 0:256], tokA[:, :, 0:256], wide_col(small[:, 0:2], 256), ALU.mult)
                link(tt(tokA[:, :, 256:384], tokA[:, :, 256:384], wide_col(small[:, 2:4], 128), ALU.mult))
                dve.wait_ge(small_in, 112 * (l + 1))
                tt(tokA[:, :, 256:384], tokA[:, :, 256:384], gkv_b[:, :].unsqueeze(1).to_broadcast([P, 2, KVL]),
                   ALU.mult).then_inc(qa_normed, 1)

            def head_stats(l):
                dve.wait_ge(qkv_kept, 5 * l + 5)
                dve.wait_ge(cache_in, 32 * (l + 1))
                dve.wait_ge(squared, 3 * l + 2)
                link(dve.tensor_reduce(small[:, 8:16], heads_sq.rearrange("p (a d) -> p a d", d=QK), AX.X, ALU.add))
                knope = KV[:, :, :].rearrange("p s (h d) -> p s h d", h=HEADS)[:, :, :, 0:NOPE]
                link(tt(heads_sq.rearrange("p (s h d) -> p s h d", s=3, h=HEADS), knope, knope, ALU.mult))
                link(dve.tensor_reduce(small[:, 16:28], heads_sq.rearrange("p (a d) -> p a d", d=NOPE), AX.X,
                                       ALU.add))
                kpe = tokA[:, :, 384:416]
                tt(heads_sq[:, 0:64].rearrange("p (g d) -> p g d", g=2), kpe, kpe, ALU.mult)
                link(tt(heads_sq[:, 64:96], kpc, kpc, ALU.mult))
                link(dve.tensor_reduce(small[:, 112:115], heads_sq[:, 0:96].rearrange("p (s d) -> p s d", s=3),
                                       AX.X, ALU.add))
                kss = small[:, 16:28].rearrange("p (s h) -> p s h", s=3)
                link(tt(kss, kss, wide_col(small[:, 112:115], HEADS), ALU.add))
                ts(small[:, 8:28], small[:, 8:28], 1.0 / QK, EPS, ALU.mult, ALU.add).then_inc(stats_in, 1)

            def head_norm(l):
                dve.wait_ge(pool_pow, 3 * l + 2)
                q = qk[:, 0:768].rearrange("p (a d) -> p a d", d=QK)
                kn = qk[:, 768:1920].rearrange("p (a d) -> p a d", d=QK)
                tt(q, q, wide_col(small[:, 8:16], QK), ALU.mult)
                rs = small[:, 16:28].rearrange("p (s h) -> p s h", s=3)
                tt(Kn[:, :, :, 0:NOPE], KV[:, :, :].rearrange("p s (h d) -> p s h d", h=HEADS)[:, :, :, 0:NOPE],
                   rs.unsqueeze(3).to_broadcast([P, 3, HEADS, NOPE]), ALU.mult)
                tt(Kn[:, 0:2, :, NOPE:QK], tokA[:, :, 384:416].unsqueeze(2).to_broadcast([P, 2, HEADS, ROPE]),
                   rs[:, 0:2, :].unsqueeze(3).to_broadcast([P, 2, HEADS, ROPE]), ALU.mult)
                link(tt(Kn[:, 2, :, NOPE:QK], kpc.unsqueeze(1).to_broadcast([P, HEADS, ROPE]),
                        wide_col(small[:, 24:28], ROPE), ALU.mult))
                tt(q, q, gq_b[:, :].unsqueeze(1).to_broadcast([P, 8, QK]), ALU.mult)
                link(tt(kn, kn, gk_b[:, :].unsqueeze(1).to_broadcast([P, 12, QK]), ALU.mult))

            def rope(l):
                def trig(at):
                    return consts[:, at:at + 16].rearrange("p (a f) -> p a f", a=2).unsqueeze(1)\
                        .to_broadcast([P, HEADS, 2, 8])
                cos, sin = trig(K_COS), trig(K_SIN)
                parts = []
                for n, x in enumerate((Q[:, 1, :, NOPE:QK], Kn[:, 1, :, NOPE:QK])):
                    v = x.rearrange("p h (a b f) -> p h a b f", a=2, b=2)
                    x1, x2 = v[:, :, :, 0, :], v[:, :, :, 1, :]
                    t = [ropet[:, 4 * n + m, :].rearrange("p (h a f) -> p h a f", h=HEADS, a=2) for m in range(4)]
                    tt(t[0], x1, cos, ALU.mult)
                    tt(t[1], x2, sin, ALU.mult)
                    tt(t[2], x1, sin, ALU.mult)
                    ins = tt(t[3], x2, cos, ALU.mult)
                    parts.append((x1, x2, t))
                link(ins)
                for x1, x2, t in parts:
                    tt(x1, t[0], t[1], ALU.subtract)
                    ins = tt(x2, t[2], t[3], ALU.add)
                ins.then_inc(qk_ready, 1)

            def na_stats(l):
                dve.wait_ge(drained, 25 * l + 5)
                dve.wait_ge(squared, 3 * l + 3)
                link(dve.tensor_reduce(small[:, 32:48], big[:, 0:1024].rearrange("p (a d) -> p a d", d=HD), AX.X,
                                       ALU.add))
                ts(small[:, 32:48], small[:, 32:48], 1.0 / HD, EPS, ALU.mult, ALU.add).then_inc(stats_in, 1)

            def na_norm(l):
                dve.wait_ge(pool_pow, 3 * l + 3)
                x = tokN[:, :, 0:512].rearrange("p g (a d) -> p g a d", d=HD)
                rs = small[:, 32:48].rearrange("p (g a) -> p g a", g=2).unsqueeze(3).to_broadcast([P, 2, 8, HD])
                link(tt(x, x, rs, ALU.mult))
                link(ts(gnq_b[:, :], gnq_b[:, :], HD ** -0.5, None, ALU.mult))
                for a, gain in ((0, gnq_b), (4, gnk_b)):
                    y = x[:, :, a:a + 4, :]
                    ins = tt(y, y, gain[:, :].unsqueeze(1).unsqueeze(1).to_broadcast([P, 2, 4, HD]), ALU.mult)
                ins.then_inc(na_ready, 1)

            def softmax_max(u, scale):
                dve.wait_ge(scores_done, u + 1)
                if u % 2:
                    dve.wait_ge(bias_kept, u // 2 + 1)
                    if u // 2 == 0:
                        dve.wait_ge(consts_in, 16)
                    link(tt(sbias, ps[:, 6, :], bias[:, :, :].rearrange("p h k -> p (h k)"), ALU.add))
                    m = sbias.rearrange("p (h k) -> p h k", h=HEADS)
                    link(tt(m, m, consts[:, K_MASK:K_MASK + TOK].unsqueeze(1).to_broadcast([P, HEADS, TOK]),
                            ALU.add))
                for s in range(3):
                    src = sbias if u % 2 and s == 1 else ps[:, 5 + s, :]
                    ins = dve.tensor_reduce(small[:, 92 + 4 * s:96 + 4 * s],
                                            src.rearrange("p (h k) -> p h k", h=HEADS), AX.X, ALU.max)
                link(ins)
                link(tt(small[:, 96:100], small[:, 96:100], small[:, 100:104], ALU.max))
                ts(small[:, 60:68], small[:, 92:100], -scale, None, ALU.mult)
                ts(small[:, 68:72], small[:, 96:100], -scale, None, ALU.mult).then_inc(max_done, 1)

            def scale_out(u):
                dve.wait_ge(exp_done, 12 * (u + 1))
                link(tt(small[:, 80:84], small[:, 80:84], small[:, 84:88], ALU.add))
                link(dve.reciprocal(small[:, 104:112], small[:, 76:84]))
                dve.wait_ge(o_done, u + 1)
                tt(O.rearrange("p g (h d) -> p g h d", h=HEADS),
                   ps[:, 4, :].rearrange("p (g h d) -> p g h d", g=2, h=HEADS),
                   small[:, 104:112].rearrange("p (g h) -> p g h", g=2).unsqueeze(3)
                   .to_broadcast([P, 2, HEADS, HD]), ALU.mult).then_inc(o_scaled, 1)

            def out_lo(u):
                a = 4 * (u % 2)
                dve.wait_ge(o_hi, u + 1)
                tt(br_lo[:, a:a + 2, :].rearrange("p a b -> p (a b)"), ps[:, 4, :],
                   br_hi[:, a:a + 2, :].bitcast(F32).rearrange("p a b -> p (a b)"), ALU.subtract)\
                    .then_inc(o_lo, 1)

            def two(a):
                return a.rearrange("p (g t) -> p g t", g=2)

            conv_ops = [0]

            def tap(l, pad, taps, row, k, tile):
                src = pad[:, tile, :, k:k + TOK]
                dst = two(conv[:, tile, :])
                w = vecT[:, l, row + 2 * k + tile:row + 2 * k + tile + 1]
                if k:
                    dve.wait_ge(conv_v, conv_ops[0] - 1)
                    ins = stt(dst, src, w, dst, ALU.mult, ALU.add)
                else:
                    ins = ts(dst, src, w, None, ALU.mult)
                ins.then_inc(conv_v, 1)
                conv_ops[0] += 1

            def branch_b(l):
                for k in range(SCK):
                    for tile in range(2):
                        tap(l, scpad, SCK, V_SC, k, tile)
                dve.wait_ge(conv_v, conv_ops[0])
                tt(bc[:, 0:2, :], bc[:, 0:2, :], conv[:, :, :], ALU.mult).then_inc(b_ready, 1)

            def branch_d(l, first, last):
                for n in range(first, last):
                    tap(l, cfpad, CFK, V_CF, n // 2, n % 2)

            def mixer_task(l, h):
                if h == 1:
                    latents(l)
                if h == 5:
                    head_stats(l)
                if h == 6:
                    na_stats(l)
                    head_norm(l)
                if h == 7:
                    rope(l)
                    dve.wait_ge(drained, 25 * l + 7)
                    dve.wait_ge(piece_used, filled(l, 7))
                    if l == 0:
                        dve.wait_ge(setup, 4)
                    tt(scpad[:, :, :, 1:1 + TOK], ps[:, 3, :].rearrange("p (a g t) -> p a g t", a=2, g=2),
                       bc[:, 2:4, :].rearrange("p a (g t) -> p a g t", g=2), ALU.mult).then_inc(xv_read, 1)
                if h == 8:
                    dve.wait_ge(xv_read, l + 1)
                    na_norm(l)
                    branch_b(l)
                if h == 10:
                    softmax_max(2 * l, QK ** -0.5)
                if h == 11:
                    dve.wait_ge(drained, 25 * l + 9)
                    for tile in range(2):
                        ins = stt(cfpad[:, tile, :, 15:15 + TOK], two(cf[:, 2 + tile, :]), 1.0,
                                  two(cf[:, tile, :]), ALU.add, ALU.mult)
                    ins.then_inc(cf_used, 1)
                    dve.wait_ge(cf_used, l + 1)
                    dve.wait_ge(b_ready, l + 1)
                    branch_d(l, 0, 8)
                if h == 12:
                    dve.wait_ge(b_hi, l + 1)
                    tt(br_lo[:, 2:4, :], bc[:, 0:2, :], br_hi[:, 2:4, :].bitcast(F32), ALU.subtract)\
                        .then_inc(b_lo, 1)
                    branch_d(l, 8, 15)
                if h == 13:
                    scale_out(2 * l)
                    branch_d(l, 15, 22)
                if h == 14:
                    out_lo(2 * l)
                    branch_d(l, 22, 29)
                if h == 15:
                    branch_d(l, 29, 38)
                if h == 16:
                    branch_d(l, 38, 46)
                if h == 17:
                    softmax_max(2 * l + 1, 1.0)
                if h == 18:
                    branch_d(l, 46, 55)
                if h == 19:
                    branch_d(l, 55, 62)
                if h == 20:
                    scale_out(2 * l + 1)
                    dve.wait_ge(conv_v, conv_ops[0])
                    for tile in range(2):
                        ins = ts(conv[:, tile, :], conv[:, tile, :], 0.5, vecT[:, l, V_CFB + tile:V_CFB + tile + 1],
                                 ALU.mult, ALU.add)
                    ins.then_inc(conv_ready, 1)
                if h == 21:
                    out_lo(2 * l + 1)
                    dve.wait_ge(ln_sum, l + 1)
                    dve.wait_ge(conv_ready, l + 1)
                    for tile in range(2):
                        ins = stt(conv[:, tile, :], ps[:, 5, 0:256], -1.0 / BW, conv[:, tile, :], ALU.mult, ALU.add)
                    link(ins)
                    tt(ln_sq, conv[:, :, :].rearrange("p a t -> p (a t)"),
                       conv[:, :, :].rearrange("p a t -> p (a t)"), ALU.mult).then_inc(ln_sq_done, 1)
                if h == 22:
                    dve.wait_ge(ln_sqsum, l + 1)
                    ts(ln_sd, ps[:, 6, 0:256], 1.0 / BW, EPS, ALU.mult, ALU.add).then_inc(ln_ms, 1)
                if h == 23:
                    dve.wait_ge(ln_sdone, l + 1)
                    link(dve.reciprocal(ln_sd, ln_sd))
                    link(tt(conv[:, :, :], conv[:, :, :], ln_sd.unsqueeze(1).to_broadcast([P, 2, NT]), ALU.mult))
                    for tile in range(2):
                        ins = ts(conv[:, tile, :], conv[:, tile, :], vecT[:, l, V_LNG + tile:V_LNG + tile + 1],
                                 vecT[:, l, V_LNB + tile:V_LNB + tile + 1], ALU.mult, ALU.add)
                    ins.then_inc(ln_z, 1)
                if h == 24:
                    dve.wait_ge(ln_th, l + 1)
                    stt(ln_sq, ln_sq, 1.0, conv[:, :, :].rearrange("p a t -> p (a t)"), ALU.add, ALU.mult)\
                        .then_inc(ln_o, 1)
                    dve.wait_ge(d_hi, l + 1)
                    stt(br_lo[:, 6:8, :].rearrange("p a t -> p (a t)"), ln_sq, 0.5,
                        br_hi[:, 6:8, :].bitcast(F32).rearrange("p a t -> p (a t)"), ALU.mult, ALU.subtract)\
                        .then_inc(d_lo, 1)
                if M_BR <= h < M_O:
                    for j in (2 * (h - M_BR), 2 * (h - M_BR) + 1):
                        dve.wait_ge(piece_used, 2 * MIX[l][h] + j % 2 + 1)
                        dve.wait_ge(drained, 25 * (l + 1))
                        g4 = gates[:, :, j, :].rearrange("p (b n) t -> p b n t", b=2)
                        stt(g4, g4, 1.0, ps[:, 2 * (j % 2):2 * (j % 2) + 2, :].rearrange("p b (n t) -> p b n t", n=2),
                            ALU.add, ALU.mult).then_inc(proj_read, 1)
                    for j in merged_at(h):
                        dve.wait_ge(merged_hi, 8 * l + j + 1)
                        stt(hT_lo[:, j, :], gates[:, 0, j, :], 0.5, hT_hi[:, j, :].bitcast(F32), ALU.mult,
                            ALU.subtract).then_inc(merged_lo, 1)
                if M_O <= h:
                    dve.wait_ge(piece_used, 2 * (MIX[l][h] + 1))
                    for jj in range(2):
                        j = 2 * (h - M_O) + jj
                        for g in range(2):
                            r = xT[:, j, TOK * g:TOK * g + TOK]
                            a = 256 * jj + TOK * g
                            ins = stt(r, ps[:, h - M_O, a:a + TOK], modT[:, l, 16 + j, g:g + 1], r, ALU.mult, ALU.add)
                    ins.then_inc(wo_read, 1)

            def ff_task(hh):
                kind, ch = FFN[hh // 2]
                q = hh % 2
                if kind == "up":
                    n = 2 * ch + q + 1
                    dve.wait_ge(ff_act_done, n)
                    dve.wait_ge(piece_used, 2 * (FF[hh] + 1))
                    if ch:
                        dve.wait_ge(ff_hi, n - 2)
                    tt(ff_hid[:, q, :], ff_act[:, q, :], ps[:, 2 + q, :], ALU.mult).then_inc(ff_hid_done, 1)
                    dve.wait_ge(ff_hi, n)
                    a = 4 * (ch % 2) + 2 * q
                    tt(br_lo[:, a:a + 2, :].rearrange("p a b -> p (a b)"), ff_hid[:, q, :],
                       br_hi[:, a:a + 2, :].bitcast(F32).rearrange("p a b -> p (a b)"), ALU.subtract)\
                        .then_inc(ff_lo, 1)

                if hh == FFN_HALVES - 1:
                    dve.wait_ge(piece_used, ff_used("down", CHUNKS - 1))
                    for j in range(KT):
                        for g in range(2):
                            r = xT[:, j, TOK * g:TOK * g + TOK]
                            a = 256 * (j % 2) + TOK * g
                            ins = stt(r, ps[:, 4 + j // 2, a:a + TOK], modT[:, 0, 40 + j, g:g + 1], r,
                                      ALU.mult, ALU.add)
                        if j % 2:
                            ins.then_inc(ff_read, 1)

            def task(H):
                phase, l, n = ROLE[H]
                if phase == "mix":
                    mixer_task(l, n)
                elif phase == "ff":
                    ff_task(n)
                if H and ROLE[H - 1][0] == "ada" and ROLE[H - 1][2] % 2 and norm_before(H) is None:
                    l, n = ROLE[H - 1][1:]
                    if l or n // 2 >= ADA_FIRST:
                        keep_modulation(l, n // 2)

            for H in range(HALVES):
                for c_ in range(2):
                    lo(H, c_)
                    for done in tasks_at(H, c_):
                        task(done)
                if H == X_STAT + 1:
                    norm_mean(0)
                n = norm_before(H)
                if n == 0:
                    for c_ in range(ADA_FIRST):
                        keep_modulation(0, c_)
                elif n is not None:
                    norm_mean(n)
                if n == 1:
                    keep_modulation(0, 11)
                if n is not None:
                    norm_apply(n)
            task(HALVES - 1)
            norm_mean(3)
            norm_apply(3)

            def col(a):
                return a.unsqueeze(2)

            left = consts[:, K_LEFT:K_LEFT + 8].unsqueeze(1).to_broadcast([P, 2, 8])
            dve.wait_ge(lg_done, 1)
            for g in range(2):
                ins = dve.tensor_copy(lg[:, g, :], ps[:, 2 * g, 256:264])
            link(ins)

            def first_largest(logits, top, onehot):
                link(dve.tensor_reduce(top, logits, AX.X, ALU.max))
                link(tt(tmp, logits, col(top).to_broadcast([P, 2, 8]), ALU.is_ge))
                link(tt(tmp, tmp, left, ALU.mult))
                link(dve.tensor_reduce(tq[:, 8:10], tmp, AX.X, ALU.max))
                link(tt(onehot, left, col(tq[:, 8:10]).to_broadcast([P, 2, 8]), ALU.is_equal))

            first_largest(lg, tq[:, 0:2], oh1)
            link(stt(lg2, oh1, -1e30, lg, ALU.mult, ALU.add))
            first_largest(lg2, tq[:, 2:4], oh2)
            link(tt(tq[:, 4:6], tq[:, 2:4], tq[:, 0:2], ALU.subtract))
            tt(mask, oh1, oh2, ALU.add).then_inc(mask_done, 1)
            dve.wait_ge(pair_exp, 1)
            link(ts(tq[:, 6:8], tq[:, 4:6], 1.0, None, ALU.add))
            link(dve.reciprocal(tq[:, 6:8], tq[:, 6:8]))
            link(tt(tq[:, 4:6], tq[:, 4:6], tq[:, 6:8], ALU.mult))
            tt(oh1, oh1, col(tq[:, 6:8]).to_broadcast([P, 2, 8]), ALU.mult)
            link(tt(oh2, oh2, col(tq[:, 4:6]).to_broadcast([P, 2, 8]), ALU.mult))
            tt(tab[:, 2, :, 0:8], oh1, oh2, ALU.add)
            dve.tensor_copy(tab[:, 1, :, 0:8], mask)
            dve.wait_ge(pos_done, 1)
            dve.tensor_copy(tab[:, 0, :, 0:8], ps[:, 1, 0:16].rearrange("p (g e) -> p g e", g=2))
            link(ts(ov, ps[:, 1, 16:24], float(CAP), None, ALU.is_gt))

            iota = consts[:, K_IOTA:K_IOTA + P]

            def select(n):
                dve.tensor_copy(stage, tab[:, :, :, bass.ds(n, 1)].rearrange("p q t i -> p q (t i)"))\
                    .then_inc(staged, 1)
                dve.wait_ge(staged, n + 1)
                for t in range(2):
                    ts(sel[:, t, :], iota, stage[:, 0, t:t + 1], stage[:, 1, t:t + 1], ALU.is_equal, ALU.mult)
                    ins = ts(selg[:, t, :], iota, stage[:, 0, t:t + 1], stage[:, 2, t:t + 1], ALU.is_equal,
                             ALU.mult)
                ins.then_inc(sel_done, 1)

            def gathered_lo(n):
                dve.wait_ge(xe_hi, n)
                tt(hT_lo[:, 0:4, :].rearrange("p a b -> p (a b)"), ps[:, 5:7, :].rearrange("p a b -> p (a b)"),
                   hT_hi[:, 0:4, :].bitcast(F32).rearrange("p a b -> p (a b)"), ALU.subtract).then_inc(xe_lo, 1)

            def add_scattered(hh, i):
                for r, bank in I_SCATTER[hh]:
                    dve.wait_ge(sc_fill, i * 4 + (r + 1))
                    f = fT[:, 2 * r:2 * r + 2, :].rearrange("p a b -> p (a b)")
                    tt(f, ps[:, bank, :], f, ALU.add).then_inc(item_added, 1)

            select(0)
            dve.wait_ge(h2_kept, 4)
            dve.memset(ps[:, 3:5, :], 0.0).then_inc(y_cleared, 1)
            dve.memset(selT, 0.0).then_inc(selT_kept, 1)

            dve.memset(tab[:, :, :, ITEMS:ITEMS + 1], 0.0)
            link(tt(w64, consts[:, K_BEFORE:K_BEFORE + 64].rearrange("p (a e) -> p a e", a=8),
                    ov.unsqueeze(1).to_broadcast([P, 8, 8]), ALU.mult))
            link(dve.tensor_reduce(rank, w64, AX.X, ALU.add))
            for k in range(OVER):
                ins = stt(ohk[:, k, :], rank, float(k), ov, ALU.is_equal, ALU.mult)
            link(ins)
            for q in range(3):
                a = tab[:, q, :, 0:8]
                if q == 0:
                    link(ts(tmp, a, float(-CAP), None, ALU.add))
                    a = tmp
                for t in range(2):
                    link(tt(wide[:, t, :, :], ohk, a[:, t, :].unsqueeze(1).to_broadcast([P, OVER, 8]), ALU.mult))
                link(dve.tensor_reduce(tab[:, q, :, NEXP:ITEMS], wide, AX.X, ALU.add))
            link(tt(wide[:, 0, :, :], ohk, consts[:, K_EXP:K_EXP + 8].unsqueeze(1).to_broadcast([P, OVER, 8]),
                    ALU.mult))
            dve.tensor_reduce(eidx[:, 2:2 + OVER], wide[:, 0, :, :], AX.X, ALU.add)
            link(dve.tensor_reduce(eidx[:, 1:2], ov, AX.X, ALU.add))
            link(ts(eidx[:, 0:1], eidx[:, 1:2], float(NEXP), None, ALU.add))
            dve.tensor_copy(itab[0:1, 0:OVER + 2], eidx[0:1, :]).then_inc(tab_done, 1)
            gathered_lo(1)

            dve.wait_ge(tab_done, 1)
            dve.wait_ge(sum_cleared, 1)
            n_items = dve.value_load(itab[0:1, 0:1], min_val=NEXP, max_val=ITEMS)
            with dve.Fori(0, n_items) as i:
                def item_lo(hh):
                    for c_ in range(2):
                        part, h, w = item_piece(hh, c_)
                        dve.wait_ge(hi_piece, i * FFN_PIECES + (2 * (HALVES + hh) + c_ + 1))
                        tt(w, part, h.bitcast(F32), ALU.subtract).then_inc(lo_piece, 1)

                def item_task(hh):
                    kind, ch = FFN[hh // 2]
                    if kind == "up" and hh % 2:
                        dve.wait_ge(e_act, i * CHUNKS + (ch + 1))
                        dve.wait_ge(piece_used, i * FFN_PIECES + 2 * (HALVES + hh + 1))
                        tt(ff_hid[:, 0, :], ff_act[:, 0, :], ps[:, 1, :], ALU.mult).then_inc(e_hid, 1)
                    if (kind == "down" and hh % 2 == 0 and ch < CHUNKS - 1) or (kind == "up" and hh % 2 and ch == 0):
                        t = 0 if kind == "up" else ch + 1
                        dve.wait_ge(e_hi, i * CHUNKS + (t + 1))
                        a = 2 * (t % 2)
                        tt(br_lo[:, a:a + 2, :].rearrange("p a b -> p (a b)"), ps[:, 2, :],
                           br_hi[:, a:a + 2, :].bitcast(F32).rearrange("p a b -> p (a b)"), ALU.subtract)\
                            .then_inc(e_lo, 1)

                for hh in range(FFN_HALVES):
                    item_lo(hh)
                    if hh:
                        item_task(hh - 1)
                    if hh - 1 in I_SCATTER:
                        add_scattered(hh - 1, i)
                    if hh == I_SELECT:
                        dve.wait_ge(selT_t, i + 1)
                        dve.wait_ge(xe_t, i + 1)
                        select(i + 1)
                    if hh == I_GATHER + 1:
                        gathered_lo(i + 2)
            for hh in I_SCATTER:
                add_scattered(hh, n_items)
            dve.wait_ge(item_added, n_items * 4 + 4)
            for j in range(KT):
                for g in range(2):
                    r = xT[:, j, TOK * g:TOK * g + TOK]
                    ins = stt(r, fT[:, j, TOK * g:TOK * g + TOK], modT[:, 1, 40 + j, g:g + 1], r, ALU.mult, ALU.add)
            ins.then_inc(moe_done, 1)

        @block.tensor
        def _(pe):
            mm = pe.matmul

            def mm3(out, a_hi, a_lo, b_hi, b_lo, start, stop, shared=False):
                mm(out, a_hi, b_hi, start=start, stop=False, skip_group_check=shared)
                mm(out, a_hi, b_lo, start=False, stop=False, skip_group_check=shared)
                return mm(out, a_lo, b_hi, start=False, stop=stop, skip_group_check=shared)

            def turn(out, x):
                return pe.transpose(out, x, ident[0:x.shape[0], 0:x.shape[0]])

            def tok(g):
                return slice(TOK * g, TOK * g + TOK)

            pe.wait_ge(consts_in, 16)
            pe.wait_ge(cond_in, 32)
            turn(ps[:, 7, 0:16], vrow[0:16, :]).then_inc(cond_turned, 1)
            pe.wait_ge(cond_lo, 1)

            def turn_x():
                pe.wait_ge(x_in, 32)
                for b in range(4):
                    for k in (2 * b, 2 * b + 1):
                        for g in range(2):
                            a = 256 * (k % 2) + TOK * g
                            ins = turn(ps[:, b, a:a + TOK], xtok[:, g, P * k:P * k + P])
                    ins.then_inc(x_turned, 1)

            def turn_vectors(m):
                n = 48 if m % 2 else V_ROWS
                pe.wait_ge(vrow_in, 16 * (9 * (m // 2) + (9 if m % 2 else 8)))
                turn(ps[:, vector_bank(m), 0:n], vrow[0:n, :]).then_inc(v_turned, 1)

            def fold(l, c_):
                pe.wait_ge(ada_kept, 12 * l + c_ + 1)
                if l and c_ % 2 == 0:
                    pe.wait_ge(ff_hid_done, 2 * (c_ // 2 + 1) + 2)
                bank = ada_banks(l, c_)[1]
                for q in range(4):
                    ins = mm(ps[:, bank, 2 * q:2 * q + 2], arow[0:4, c_ % 2, P * q:P * q + P],
                             consts[0:4, K_FOLD:K_FOLD + 2], start=True, stop=True)
                ins.then_inc(ada_folded, 1)

            def ada(l, n, chunk):
                c_, q = divmod(n, 2)
                bank = ada_banks(l, c_)[0]
                if q == 0 and l:
                    pe.wait_ge(ff_act_done, 2 * chunk + 2)
                    if c_ % 2:
                        pe.wait_ge(ff_hid_done, 2 * chunk + 2)
                if q == 0 and l == 0 and c_ > ADA_FIRST + 1:
                    pe.wait_ge(mod_kept, c_ - 1)
                if q == 0 and (l, c_) == (0, ADA_FIRST + 1):
                    pe.wait_ge(o_lo, 2)
                for m in range(2):
                    pe.wait_ge(lo_piece, 2 * ADA[l][n] + m + 1)
                    _, wh, wl = piece(ADA[l][n], m)
                    for k in range(2):
                        kk = 4 * q + 2 * m + k
                        x = cond_hl[:, kk, :]
                        mm(ps[0:4, bank, :], x, wh[:, k, :], start=(kk == 0), stop=False)
                        ins = mm(ps[0:4, bank, :], x, wl[:, k, :], start=False, stop=(kk == KT - 1))
                    ins.then_inc(piece_used, 1)

            def stat(n, pairs=range(4)):
                for p in pairs:
                    pe.wait_ge(sq_done, 4 * n + p + 1)
                    for k in (2 * p, 2 * p + 1):
                        ins = mm(ps[:, 0, 0:NT], ones[:, :], sq[:, k, :], start=(k == 0), stop=(k == KT - 1))
                    if p == 3:
                        ins.then_inc(stat_done, 1)

            def normed(n, k):
                pe.wait_ge(h_lo, 4 * n + k // 2 + 1)

            def free_bank(l, f):
                if f - 4 == 7:
                    pe.wait_ge(xv_read, l + 1)
                elif f >= 4:
                    pe.wait_ge(drained, 25 * l + (f - 3 if f - 4 < 7 else f - 4))

            def heads(u, d, q, k, first):
                if first:
                    for g in range(2):
                        for h in range(HEADS):
                            turn(ps[0:d, 4 + g, TOK * h:TOK * h + TOK], q(g, h))
                    for s in range(2):
                        for h in range(HEADS):
                            ins = turn(ps[0:d, 6 + s, TOK * h:TOK * h + TOK], k(s, h))
                else:
                    pe.wait_ge(heads_kept, 5 * u + 1)
                    for h in range(HEADS):
                        ins = turn(ps[0:d, 4, TOK * h:TOK * h + TOK], k(2, h))
                ins.then_inc(heads_turned, 1)

            def scores(u, d):
                pe.wait_ge(heads_kept, 5 * (u + 1))
                for s in range(3):
                    for h in range(HEADS):
                        ins = mm(ps[:, 5 + s, TOK * h:TOK * h + TOK], QT[0:d, min(s, 1), h, :], KTt[0:d, s, h, :],
                                 start=True, stop=True)
                ins.then_inc(scores_done, 1)

            def turn_probs(u):
                pe.wait_ge(exp_done, 12 * (u + 1))
                for s in range(3):
                    for h in range(HEADS):
                        ins = turn(ps[:, 5 + s, TOK * h:TOK * h + TOK], Pr[:, s, h, :])
                ins.then_inc(probs_turned, 1)

            def weigh(u, v):
                pe.wait_ge(probs_kept, 3 * (u + 1))
                for g in range(2):
                    for h in range(HEADS):
                        o = ps[:, 4, 256 * g + HD * h:256 * g + HD * h + HD]
                        for s in ((0,), (1, 2))[g]:
                            ins = mm(o, KTt[:, s, h, :], v(s, h), start=(s < 2), stop=(s != 1))
                ins.then_inc(o_done, 1)

            def turn_out(u):
                pe.wait_ge(o_scaled, u + 1)
                for k in range(2):
                    for g in range(2):
                        a = NT * k + TOK * g
                        ins = turn(ps[:, 4, a:a + TOK], tokA[:, g, P * k:P * k + P])
                ins.then_inc(o_turned, 1)

            def mla_q(g, h):
                return Q[:, g, h, :]

            def mla_k(s, h):
                return Kn[:, s, h, :]

            def mla_v(s, h):
                return KV[:, s, 128 * h + NOPE:128 * h + 128]

            def na_q(g, h):
                return tokN[:, g, HD * h:HD * h + HD]

            def na_k(s, h):
                return tokN[:, s, 256 + HD * h:256 + HD * h + HD] if s < 2 else nakc[:, HD * h:HD * h + HD]

            def na_v(s, h):
                return tokN[:, s, 512 + HD * h:512 + HD * h + HD] if s < 2 else navc[:, HD * h:HD * h + HD]

            def attention_step(l, h):
                if h == 3:
                    pe.wait_ge(qa_normed, l + 1)
                    pe.wait_ge(cache_in, 32 * (l + 1))
                    for k in range(2):
                        for g in range(2):
                            a = NT * k + TOK * g
                            turn(ps[:, 4, a:a + TOK], tokA[:, g, P * k:P * k + P])
                    for s in range(3):
                        ins = turn(ps[:, 5, TOK * s:TOK * s + TOK], tokA[:, s, 256:384] if s < 2 else ckc)
                    ins.then_inc(latent_turned, 1)
                if h == 4:
                    pe.wait_ge(latent_kept, 3 * (l + 1))
                    pe.wait_ge(small_in, 112 * (l + 1))
                    pe.wait_ge(bias_kept, l + 1)
                    for g in range(2):
                        for k in range(2):
                            mm(ps[:, 6 + g, 0:384], qaT[:, k, tok(g)], wuq[:, k, :], start=(k == 0), stop=(k == 1))
                    for s in range(2):
                        ins = mm(ps[:, 4 + s, :], ckvT[:, tok(s)], wukv[:, :], start=True, stop=True)
                    ins.then_inc(qkv_done, 1)
                if h == 5:
                    pe.wait_ge(qkv_kept, 5 * l + 4)
                    mm(ps[:, 4, :], ckvT[:, 256:384], wukv[:, :], start=True, stop=True).then_inc(qkv_done, 1)
                if l == 0 and h in (6, 14):
                    turn_vectors(3 if h == 14 else 2)
                if h == 8:
                    pe.wait_ge(qk_ready, l + 1)
                    pe.wait_ge(v_kept, 3)
                    heads(2 * l, QK, mla_q, mla_k, True)
                if h == 9:
                    heads(2 * l, QK, mla_q, mla_k, False)
                if h == 10:
                    scores(2 * l, QK)
                if h == 12:
                    turn_probs(2 * l)
                if h == 13:
                    weigh(2 * l, mla_v)
                if h == 14:
                    turn_out(2 * l)
                if h == 15:
                    pe.wait_ge(na_ready, l + 1)
                    pe.wait_ge(o_lo, 2 * l + 1)
                    pe.wait_ge(v_kept, 4)
                    heads(2 * l + 1, HD, na_q, na_k, True)
                if h == 16:
                    pe.wait_ge(nacache_in, 32 * (l + 1))
                    heads(2 * l + 1, HD, na_q, na_k, False)
                if h == 17:
                    scores(2 * l + 1, HD)
                if h == 19:
                    turn_probs(2 * l + 1)
                if h == 20:
                    weigh(2 * l + 1, na_v)
                if h == 21:
                    turn_out(2 * l + 1)
                    pe.wait_ge(conv_ready, l + 1)
                    for tile in range(2):
                        ins = mm(ps[:, 5, 0:NT], ones[:, :], conv[:, tile, :], start=(tile == 0), stop=(tile == 1))
                    ins.then_inc(ln_sum, 1)
                if h == 22:
                    pe.wait_ge(ln_sq_done, l + 1)
                    for tile in range(2):
                        ins = mm(ps[:, 6, 0:NT], ones[:, :], ln_sq[:, NT * tile:NT * tile + NT],
                                 start=(tile == 0), stop=(tile == 1))
                    ins.then_inc(ln_sqsum, 1)

            def mixer_half(l, h):
                H = MIX[l][h]
                kind, _, i, _ = SLOTS[SLOT_OF[H][0]]
                q = SLOT_OF[H][1]
                if kind == "na_v" or kind in ("sc", "cf", "gates"):
                    free_bank(l, h)
                if h == M_BR:
                    pe.wait_ge(drained, 25 * (l + 1))
                    pe.wait_ge(b_lo, l + 1)
                    pe.wait_ge(d_lo, l + 1)
                    pe.wait_ge(o_lo, 2 * l + 2)
                if h == M_O:
                    pe.wait_ge(proj_read, 8 * l + 7)
                for c_ in range(2):
                    pe.wait_ge(lo_piece, 2 * H + c_ + 1)
                    _, wh, wl = piece(H, c_)
                    if kind in ("tok", "na_qk"):
                        for g in range(2):
                            bank, n = (2 + g, 512) if kind == "na_qk" else (g, 416)
                            if h < 2:
                                normed(2 * l, 4 * q + 2 * c_)
                            for k in range(2):
                                kk = 4 * q + 2 * c_ + k
                                ins = mm3(ps[:, bank, 0:n], hT_hi[:, kk, tok(g)], hT_lo[:, kk, tok(g)],
                                          wh[:, k, :], wl[:, k, :], kk == 0, kk == KT - 1)
                    elif kind == "na_v":
                        for g in range(2):
                            a = 256 * g + P * c_
                            for k in range(KT):
                                ins = mm3(ps[:, 0, a:a + P], hT_hi[:, k, tok(g)], hT_lo[:, k, tok(g)],
                                          wh[:, k, :], wl[:, k, :], k == 0, k == KT - 1)
                    elif kind == "branch":
                        j = 2 * (h - M_BR) + c_
                        if j >= 2:
                            pe.wait_ge(proj_read, 8 * l + j - 1)
                        for n in range(4):
                            for k in range(2):
                                ins = mm3(ps[:, 2 * c_ + n // 2, NT * (n % 2):NT * (n % 2) + NT],
                                          wh[:, 2 * n + k, :], wl[:, 2 * n + k, :],
                                          br_hi[:, 2 * n + k, :], br_lo[:, 2 * n + k, :], k == 0, k == 1)
                    else:
                        bank = h - M_O if kind == "out" else h % 4
                        for k in range(KT):
                            if h == M_O and c_ == 0:
                                pe.wait_ge(merged_lo, 8 * l + k + 1)
                            ins = mm3(ps[:, bank, NT * c_:NT * c_ + NT], wh[:, k, :], wl[:, k, :],
                                      hT_hi[:, k, :], hT_lo[:, k, :], k == 0, k == KT - 1)
                    ins.then_inc(piece_used, 1)

            def ff(hh):
                kind, ch = FFN[hh // 2]
                q = hh % 2
                if kind == "down":
                    pe.wait_ge(ff_lo, 2 * ch + q + 1)
                elif ch:
                    pe.wait_ge(ff_hid_done if kind == "up" else ff_act_done, 2 * ch - 1 + q)
                    if kind == "up" and ch >= 2:
                        pe.wait_ge(mod_kept, 12 + 2 * ch - 2)
                for c_ in range(2):
                    pe.wait_ge(lo_piece, 2 * FF[hh] + c_ + 1)
                    _, wh, wl = piece(FF[hh], c_)
                    if kind == "down":
                        x = 4 * (ch % 2) + 2 * q + c_
                        first, last = (ch, q, c_) == (0, 0, 0), (ch, q, c_) == (CHUNKS - 1, 1, 1)
                        for j in range(KT):
                            ins = mm3(ps[:, 4 + j // 2, NT * (j % 2):NT * (j % 2) + NT],
                                      wh[:, 0, P * j:P * j + P], wl[:, 0, P * j:P * j + P],
                                      br_hi[:, x, :], br_lo[:, x, :], first and j % 2 == 0, last, shared=True)
                    else:
                        bank = 2 * (kind == "up") + q
                        for k in range(KT):
                            if hh == c_ == 0 and k % 2 == 0:
                                normed(1, k)
                            ins = mm3(ps[:, bank, NT * c_:NT * c_ + NT], wh[:, k, :], wl[:, k, :],
                                      hT_hi[:, k, :], hT_lo[:, k, :], k == 0, k == KT - 1)
                    ins.then_inc(piece_used, 1)

            to_fold, chunk = None, 0
            for H in range(HALVES):
                phase, l, h = ROLE[H]
                n = norm_before(H)
                if n is not None:
                    if n:
                        stat(n, (3,) if n == 1 else range(4))
                    if to_fold is not None:
                        fold(*to_fold)
                        to_fold = None
                    if n % 2 == 0:
                        pe.wait_ge(hank_in, 64 * (l + 1))
                        pe.wait_ge(mod_kept, 24 if l else ADA_FIRST)
                        mm(ps[:, 6, :], consts[:, K_FLIP:K_FLIP + P], KV[:, 2, :], start=True, stop=True)\
                            .then_inc(bias_turned, 1)
                if phase == "ada":
                    ada(l, h, chunk)
                elif phase == "mix":
                    mixer_half(l, h)
                    attention_step(l, h)
                else:
                    ff(h)
                    chunk = max(chunk, FFN[h // 2][1])
                if to_fold is not None:
                    fold(*to_fold)
                to_fold = (l, h // 2) if phase == "ada" and h % 2 else None
                if H == 1:
                    turn_x()
                if H == X_STAT:
                    pe.wait_ge(setup, 4)
                    pe.wait_ge(x_kept, 4)
                    stat(0)
                if H in V_TURN:
                    pe.wait_ge(x_kept, 4)
                    turn_vectors(V_TURN.index(H))
                if H == MIX[0][-1] + 1:
                    stat(1, range(3))
            stat(3)

            pe.wait_ge(router_in, 16)
            for p in range(4):
                pe.wait_ge(hF_done, 12 + p + 1)
                for k in (2 * p, 2 * p + 1):
                    for g in range(2):
                        ins = mm(ps[:, 2 * g, 256:264], hF[:, k, tok(g)], wr[:, k, :], start=(k == 0),
                                 stop=(k == KT - 1))
                if p == 3:
                    ins.then_inc(lg_done, 1)
                for g in range(2):
                    for k in (2 * p, 2 * p + 1):
                        ins = turn(ps[:, 4 + 2 * g + k // 4, P * (k % 4):P * (k % 4) + P], hF[:, k, tok(g)])
                    if p % 2:
                        ins.then_inc(h2_turned, 1)
            pe.wait_ge(mask_done, 1)
            upper = consts[:, K_UP:K_UP + P]
            mm(ps[:, 1, 0:8], upper, mask[:, 0, :], start=True, stop=True)
            mm(ps[:, 1, 8:16], ones[:, :], mask[:, 0, :], start=True, stop=False)
            mm(ps[:, 1, 8:16], upper, mask[:, 1, :], start=False, stop=True)
            mm(ps[:, 1, 16:24], ones[:, :], mask[:, 0, :], start=True, stop=False)
            mm(ps[:, 1, 16:24], ones[:, :], mask[:, 1, :], start=False, stop=True).then_inc(pos_done, 1)

            pe.wait_ge(h2_kept, 4)
            def gather(n):
                pe.wait_ge(sel_done, n)
                for k in range(KT):
                    for t in range(2):
                        ins = mm(ps[:, 5 + k // 4, P * (k % 4):P * (k % 4) + P], h2tok[:, t, P * k:P * k + P],
                                 sel[:, t, :], start=(t == 0), stop=(t == 1))
                ins.then_inc(xe_t, 1)

            gather(1)
            pe.wait_ge(tab_done, 1)
            n_items = pe.value_load(itab[0:1, 0:1], min_val=NEXP, max_val=ITEMS)
            xe_h = hT_hi[:, 0:4, :].rearrange("p a (b s) -> p (a b) s", b=2)
            xe_l = hT_lo[:, 0:4, :].rearrange("p a (b s) -> p (a b) s", b=2)
            hd_h = br_hi[:, 0:4, :].rearrange("p a (b s) -> p (a b) s", b=2)
            hd_l = br_lo[:, 0:4, :].rearrange("p a (b s) -> p (a b) s", b=2)

            def scatter(hh, i):
                for r, bank in I_SCATTER[hh]:
                    if r == 0:
                        pe.wait_ge(y_kept, i + 1)
                        pe.wait_ge(selT_kept, i + 1)
                    if r == 3:
                        pe.wait_ge(item_added, i * 4 + 1)
                    for jj in range(2):
                        j = 2 * r + jj
                        ins = mm(ps[:, bank, NT * jj:NT * jj + NT], y_tok[:, P * j:P * j + P], selT, start=True,
                                 stop=True)
                    ins.then_inc(sc_fill, 1)

            with pe.Fori(0, n_items) as i:
                pe.wait_ge(xe_lo, i + 1)
                for hh in range(FFN_HALVES):
                    kind, ch = FFN[hh // 2]
                    q = hh % 2
                    if kind == "down":
                        pe.wait_ge(e_lo, i * CHUNKS + (ch + 1))
                        if ch == q == 0:
                            pe.wait_ge(y_kept, i + 1)
                    for c_ in range(2):
                        pe.wait_ge(lo_piece, i * FFN_PIECES + (2 * (HALVES + hh) + c_ + 1))
                        _, wh, wl = item_piece(hh, c_)
                        if kind == "down":
                            k = 2 * q + c_
                            x = 4 * (ch % 2) + k
                            for n in range(2):
                                a = slice(512 * n, 512 * n + 512)
                                ins = mm3(ps[:, 3 + n, :], hd_h[:, x, :], hd_l[:, x, :], wh[:, 0, a], wl[:, 0, a],
                                          (ch, k) == (0, 0), (ch, k) == (CHUNKS - 1, 3))
                        else:
                            for kk in range(2):
                                k = 4 * q + 2 * c_ + kk
                                ins = mm3(ps[:, 1 if kind == "up" else 0, :], xe_h[:, k, :], xe_l[:, k, :],
                                          wh[:, kk, :], wl[:, kk, :], k == 0, k == KT - 1)
                        ins.then_inc(piece_used, 1)
                    if (kind == "down" and not q and ch < CHUNKS - 1) or (kind == "up" and q and ch == 0):
                        t = 0 if kind == "up" else ch + 1
                        pe.wait_ge(e_hid, i * CHUNKS + (t + 1))
                        for k in range(4):
                            ins = turn(ps[:, 2, P * k:P * k + P], ff_hid[:, 0, P * k:P * k + P])
                        ins.then_inc(e_turn, 1)
                    if hh in I_SCATTER:
                        pe.wait_ge(xe_lo, i + 1)
                        scatter(hh, i)
                    if hh == I_TURN:
                        pe.wait_ge(item_added, i * 4 + 4)
                        for t in range(2):
                            ins = turn(ps[:, 6, TOK * t:TOK * t + TOK], selg[:, t, :])
                        ins.then_inc(selT_t, 1)
                    if hh == I_GATHER:
                        pe.wait_ge(selT_kept, i + 2)
                        gather(i + 2)
            pe.wait_ge(xe_lo, n_items + 1)
            for hh in I_SCATTER:
                scatter(hh, n_items)

            pe.wait_ge(moe_done, 1)
            for b in range(4):
                for k in range(4 * (b % 2), 4 * (b % 2) + 4):
                    ins = turn(ps[:, b, P * (k % 4):P * (k % 4) + P], xT[:, k, tok(b // 2)])
                ins.then_inc(fin_t, 1)


_INS = ['x_prompt', 'x_sample', 'cache_mla_ckv', 'cache_mla_kpe', 'cache_na_k', 'cache_na_v', 'c', 'c_ctx',
        'w_ada', 'b_ada', 'g_norm1', 'w_in', 'g_qa', 'w_uq', 'g_kva', 'w_ukv', 'g_mla_q', 'g_mla_k', 'sc_w',
        'g_na_q', 'g_na_k', 'na_rpb', 'cf_w', 'cf_b', 'cf_ln_g', 'cf_ln_b', 'w_br', 'w_o', 'g_norm2',
        'w_ff_gate', 'w_ff_up', 'w_ff_down', 'w_router', 'w_e_gate', 'w_e_up', 'w_e_down']
_OUTS = [(1, 128, 1024), (1, 128, 1024), (1, 2, 128, 128), (1, 2, 128, 32), (1, 2, 128, 4, 64), (1, 2, 128, 4, 64)]


def shape_constants():
    import numpy as np
    k = np.zeros((P, K_COLS), np.float32)
    n = np.arange(P)
    k[:, K_ID:K_ID + P] = np.eye(P)
    k[:, K_UP:K_UP + P] = n[:, None] < n[None, :]
    k[:, K_IOTA:K_IOTA + P] = n[None, :]
    cq = n % GRID_W
    start = np.clip(cq - 8, 0, GRID_W - 16)
    ok = (cq[None, :] >= start[:, None]) & (cq[None, :] < start[:, None] + 16)
    k[:, K_MASK:K_MASK + P] = np.where(ok, 0.0, -1e30)
    k[n, K_FLIP + (n // 64) * 64 + 63 - cq] = 1.0
    inv = np.float32(10000.0) ** (-np.arange(8, dtype=np.float32) / np.float32(8))
    for a, pos in enumerate((n // GRID_W, n % GRID_W)):
        ang = pos.astype(np.float32)[:, None] * inv[None, :]
        k[:, K_COS + 8 * a:K_COS + 8 * a + 8] = np.cos(ang)
        k[:, K_SIN + 8 * a:K_SIN + 8 * a + 8] = np.sin(ang)
    k[0:4, K_FOLD:K_FOLD + 2] = np.array([[1, 0], [0, 1], [1, 0], [0, 1]])
    e = np.arange(8)
    k[:, K_BEFORE:K_BEFORE + 64] = (e[None, :] < e[:, None]).reshape(1, 64)
    k[:, K_EXP:K_EXP + 8] = e
    k[:, K_LEFT:K_LEFT + 8] = 8 - e
    return k


def kernel(**inputs):
    import numpy as _np
    import concourse.bacc as _bacc
    from concourse import mybir as _mybir
    from concourse.bass_utils import run_bass_kernel_spmd as _run

    nc = _bacc.Bacc("TRN2", target_bir_lowering=False, num_devices=1)
    arrays, args = {}, []
    for name in _INS + ["shape_consts"]:
        a = shape_constants() if name == "shape_consts" else _np.ascontiguousarray(inputs[name])
        arrays[f"in_{name}_dram"] = a
        args.append(nc.dram_tensor(f"in_{name}_dram", a.shape, _mybir.dt.from_np(a.dtype), kind="ExternalInput").ap())
    for i, shape in enumerate(_OUTS):
        dt = _mybir.dt.from_np(_np.dtype("float32"))
        args.append(nc.dram_tensor(f"out_{i}_dram", shape, dt, kind="ExternalOutput").ap())
    build(nc, *args)
    r = _run(nc, [arrays], core_ids=[0])
    return tuple(r.results[0][f"out_{i}_dram"] for i in range(len(_OUTS)))
```
